# Optimizing a Trainium2 kernel written in Bass

```python
import math
import jax, jax.numpy as jnp
from jax import lax
import numpy as np

D_MODEL = 1024
BATCH = 1
SEQ = 1024
DEPTH = 1

MEM_LEN = 256
LN_EPS = 1e-5
DN_ALPHA = (2.0 * DEPTH) ** 0.25
DN_BETA = (8.0 * DEPTH) ** -0.25

DIL_GROUPS = ((128, 1), (512, 4), (2048, 16))
N_DIL_GROUPS = 3
DIL_HEADS = 4
DIL_HEAD_DIM = 128
DIL_WIDTH = DIL_HEADS * DIL_HEAD_DIM
DIL_GROUP_COLS = N_DIL_GROUPS * DIL_HEADS * DIL_HEAD_DIM
DIL_QKV_COLS = 3 * DIL_GROUP_COLS
DIL_BLOCK = 128

REL_BUCKETS = 32
REL_MAX_DIST = 2048

HG_HEADS = 4
HG_DK = 128
HG_DV = 128
HG_WIDTH = HG_HEADS * HG_DV
HG_COLS = 4 * HG_WIDTH
HG_I_OFF = DIL_QKV_COLS + HG_WIDTH
HG_CHUNK = 64

MEM_HEADS = 4
MEM_HEAD_DIM = 128
MEM_WIDTH = MEM_HEADS * MEM_HEAD_DIM

N_BRANCHES = 3
GATE_COLS = N_BRANCHES * D_MODEL
IN_COLS = DIL_QKV_COLS + HG_COLS + MEM_WIDTH + GATE_COLS
IN_SPLITS = (DIL_QKV_COLS, DIL_QKV_COLS + HG_COLS, DIL_QKV_COLS + HG_COLS + MEM_WIDTH)

PEER_HEADS = 8
PEER_N_KEYS = 128
PEER_N_EXPERTS = PEER_N_KEYS * PEER_N_KEYS
PEER_DHALF = 128
PEER_DKEY = 2 * PEER_DHALF
PEER_TOPK = 16
PEER_TOK_BLOCK = 128

kernel_name = 'hybrid_dilated_hgrn2_mem_peer_deepnorm'

def _layer_norm(t, g, b):
    t32 = t.astype(jnp.float32)
    mu = jnp.mean(t32, axis=-1, keepdims=True)
    var = jnp.mean(jnp.square(t32 - mu), axis=-1, keepdims=True)
    return ((t32 - mu) * lax.rsqrt(var + LN_EPS) * g.astype(jnp.float32) + b.astype(jnp.float32)).astype(t.dtype)

def _t5_bucket(dist):
    max_exact = REL_BUCKETS // 2
    n = np.maximum(dist, 0)
    large = max_exact + (np.log(np.maximum(n, 1) / max_exact) / math.log(REL_MAX_DIST / max_exact)
                         * (REL_BUCKETS - max_exact)).astype(np.int32)
    large = np.minimum(large, REL_BUCKETS - 1)
    return np.where(n < max_exact, n, large).astype(np.int32)

def _dilated_group(q, k, v, bias_table, window, dilation):
    b, s, h, hd = q.shape
    span = dilation * DIL_BLOCK
    sp = -(-s // span) * span
    sub = sp // dilation
    nb = sub // DIL_BLOCK

    def to_blocks(t):
        t = jnp.pad(t, ((0, 0), (0, sp - s), (0, 0), (0, 0)))
        t = t.reshape(b, sub, dilation, h, hd).transpose(0, 2, 1, 3, 4)
        return t.reshape(b, dilation, nb, DIL_BLOCK, h, hd)

    def with_prev(t):
        prev = jnp.pad(t[:, :, :-1], ((0, 0), (0, 0), (1, 0), (0, 0), (0, 0), (0, 0)))
        return jnp.concatenate([prev, t], axis=3)

    qb = to_blocks(q)
    kb = with_prev(to_blocks(k))
    vb = with_prev(to_blocks(v))
    qi = np.arange(DIL_BLOCK)[:, None]
    kj = np.arange(2 * DIL_BLOCK)[None, :]
    delta = qi + DIL_BLOCK - kj
    in_window = (delta >= 0) & (delta <= window // dilation)
    rel = jnp.transpose(bias_table[_t5_bucket(delta * dilation)], (2, 0, 1)).astype(jnp.float32)
    not_first = np.arange(nb)[:, None, None] > 0
    valid = in_window[None] & (not_first | (kj >= DIL_BLOCK)[None])
    logits = jnp.einsum('brnqhd,brnkhd->brnhqk', qb, kb).astype(jnp.float32) * (hd ** -0.5) + rel[None, None, None]
    logits = jnp.where(valid[None, None, :, None], logits, -jnp.inf)
    lse = jax.nn.logsumexp(logits, axis=-1)
    p = jnp.exp(logits - lse[..., None])
    o = jnp.einsum('brnhqk,brnkhd->brnqhd', p.astype(v.dtype), vb)
    o = o.reshape(b, dilation, sub, h, hd).transpose(0, 2, 1, 3, 4).reshape(b, sp, h, hd)[:, :s]
    lse = lse.transpose(0, 1, 2, 4, 3).reshape(b, dilation, sub, h).transpose(0, 2, 1, 3).reshape(b, sp, h)[:, :s]
    return o, lse

def _dilated_attention(dil, rel_bias):
    b, s, _ = dil.shape
    dil = dil.reshape(b, s, 3, N_DIL_GROUPS, DIL_HEADS, DIL_HEAD_DIM)
    outs, lses = [], []
    for g_idx, (window, dilation) in enumerate(DIL_GROUPS):
        o_g, lse_g = _dilated_group(dil[:, :, 0, g_idx], dil[:, :, 1, g_idx], dil[:, :, 2, g_idx],
                                    rel_bias[:, g_idx * DIL_HEADS:(g_idx + 1) * DIL_HEADS], window, dilation)
        outs.append(o_g)
        lses.append(lse_g)
    w_groups = jax.nn.softmax(jnp.stack(lses, axis=0), axis=0)
    o = jnp.einsum('gbsh,gbshd->bshd', w_groups, jnp.stack(outs, axis=0).astype(jnp.float32))
    return o.reshape(b, s, DIL_WIDTH).astype(dil.dtype)

def _hgrn2(f_raw, i_in, q_in, g_in, lb, norm_w):
    b, s, _ = f_raw.shape
    n = s // HG_CHUNK

    def heads(t):
        return t.astype(jnp.float32).reshape(b, n, HG_CHUNK, HG_HEADS, -1).transpose(0, 3, 1, 2, 4)

    lbh = lb.astype(jnp.float32).reshape(HG_HEADS, 1, 1, HG_DK)
    f = lbh + (1.0 - lbh) * jax.nn.sigmoid(heads(f_raw))
    log_f = jnp.log(f)
    key = 1.0 - f
    qh = heads(q_in)
    ih = heads(i_in)
    a = jnp.cumsum(log_f, axis=3)
    a_mid = a[:, :, :, HG_CHUNK // 2 - 1:HG_CHUNK // 2]
    a_last = a[:, :, :, -1:]
    causal = np.tril(np.ones((HG_CHUNK, HG_CHUNK), dtype=bool))
    sc = jnp.einsum('bhncd,bhnsd->bhncs', qh * jnp.exp(a - a_mid), key * jnp.exp(a_mid - a))
    o_intra = jnp.einsum('bhncs,bhnsv->bhncv', jnp.where(causal, sc, 0.0), ih)
    upd = jnp.einsum('bhncd,bhncv->bhndv', key * jnp.exp(a_last - a), ih)
    decay = jnp.exp(a_last[:, :, :, 0])

    def step(state, inp):
        dec, u = inp
        return dec[..., None] * state + u, state

    init = jnp.zeros((b, HG_HEADS, HG_DK, HG_DV), jnp.float32)
    _, before = lax.scan(step, init, (jnp.moveaxis(decay, 2, 0), jnp.moveaxis(upd, 2, 0)))
    before = jnp.moveaxis(before, 0, 2)
    o_inter = jnp.einsum('bhncd,bhndv->bhncv', qh * jnp.exp(a), before)
    o = o_intra + o_inter
    o = o * lax.rsqrt(jnp.mean(o * o, axis=-1, keepdims=True) + LN_EPS)
    o = o.transpose(0, 2, 3, 1, 4).reshape(b, s, HG_WIDTH)
    o = o * norm_w.astype(jnp.float32) * jax.nn.silu(g_in.astype(jnp.float32))
    return o.astype(f_raw.dtype)

def _memory_attention(q_in, mem, w_mem_kv):
    b, s, _ = q_in.shape
    m = mem.shape[1]
    k, v = jnp.split(jnp.einsum('bmd,de->bme', mem, w_mem_kv), 2, axis=-1)
    q = q_in.reshape(b, s, MEM_HEADS, MEM_HEAD_DIM)
    k = k.reshape(b, m, MEM_HEADS, MEM_HEAD_DIM)
    v = v.reshape(b, m, MEM_HEADS, MEM_HEAD_DIM)
    logits = jnp.einsum('bshd,bmhd->bhsm', q, k).astype(jnp.float32) * (MEM_HEAD_DIM ** -0.5)
    p = jax.nn.softmax(logits, axis=-1)
    return jnp.einsum('bhsm,bmhd->bshd', p.astype(v.dtype), v).reshape(b, s, MEM_WIDTH)

def _peer(h, w_q, sub_keys, u_tab, v_tab):
    b, s, d = h.shape
    q = jnp.einsum('bsd,dk->bsk', h, w_q).reshape(b, s, PEER_HEADS, 2, PEER_DHALF)
    sc = jnp.einsum('bshpk,hpnk->bshpn', q, sub_keys).astype(jnp.float32)
    s1, i1 = lax.top_k(sc[..., 0, :], PEER_TOPK)
    s2, i2 = lax.top_k(sc[..., 1, :], PEER_TOPK)
    cand = (s1[..., :, None] + s2[..., None, :]).reshape(b, s, PEER_HEADS, PEER_TOPK * PEER_TOPK)
    cidx = (i1[..., :, None] * PEER_N_KEYS + i2[..., None, :]).reshape(b, s, PEER_HEADS, PEER_TOPK * PEER_TOPK)
    top, pos = lax.top_k(cand, PEER_TOPK)
    idx = jnp.take_along_axis(cidx, pos, axis=-1)
    gate = jax.nn.softmax(top, axis=-1)
    n_blk = (b * s) // PEER_TOK_BLOCK
    xb = h.reshape(n_blk, PEER_TOK_BLOCK, d)
    ib = idx.reshape(n_blk, PEER_TOK_BLOCK, PEER_HEADS * PEER_TOPK)
    gb = gate.reshape(n_blk, PEER_TOK_BLOCK, PEER_HEADS * PEER_TOPK).astype(h.dtype)

    def block(args):
        xt, it, gt = args
        act = jax.nn.gelu(jnp.einsum('td,ted->te', xt, u_tab[it]), approximate=False)
        return jnp.einsum('te,ted->td', gt * act, v_tab[it])

    return lax.map(block, (xb, ib, gb)).reshape(b, s, d)

def setup_inputs(seed: int = 0) -> dict:
    key = jax.random.key(seed)
    ks = jax.random.split(key, 18)
    f32 = jnp.float32

    def nrm(k, shape, scale):
        return jax.random.normal(k, shape, f32) * scale

    col_scale = np.ones((IN_COLS,), np.float32)
    col_scale[2 * DIL_GROUP_COLS:3 * DIL_GROUP_COLS] = DN_BETA
    col_scale[HG_I_OFF:HG_I_OFF + HG_WIDTH] = DN_BETA
    mem_scale = np.concatenate([np.ones((MEM_WIDTH,)), np.full((MEM_WIDTH,), DN_BETA)]).astype(np.float32)
    d_inv = D_MODEL ** -0.5
    return {
        'x': nrm(ks[0], (BATCH, SEQ, D_MODEL), 1.0),
        'mem': nrm(ks[1], (BATCH, MEM_LEN, D_MODEL), 1.0),
        'w_in': nrm(ks[2], (DEPTH, D_MODEL, IN_COLS), d_inv) * jnp.asarray(col_scale),
        'b_gate': nrm(ks[3], (DEPTH, GATE_COLS), 0.1),
        'w_mem_kv': nrm(ks[4], (DEPTH, D_MODEL, 2 * MEM_WIDTH), d_inv) * jnp.asarray(mem_scale),
        'rel_bias': nrm(ks[5], (REL_BUCKETS, N_DIL_GROUPS * DIL_HEADS), 0.3),
        'hgrn_lb': nrm(ks[6], (DEPTH + 1, HG_HEADS * HG_DK), 0.1),
        'hgrn_norm_w': 1.0 + nrm(ks[7], (DEPTH, HG_WIDTH), 0.05),
        'w_branch': nrm(ks[8], (DEPTH, N_BRANCHES, DIL_WIDTH, D_MODEL), DIL_WIDTH ** -0.5 * DN_BETA),
        'w_out': nrm(ks[9], (DEPTH, D_MODEL, D_MODEL), d_inv * DN_BETA),
        'ln1_g': 1.0 + nrm(ks[10], (DEPTH, D_MODEL), 0.05),
        'ln1_b': nrm(ks[11], (DEPTH, D_MODEL), 0.02),
        'w_peer_q': nrm(ks[12], (DEPTH, D_MODEL, PEER_HEADS * PEER_DKEY), d_inv),
        'peer_sub_keys': nrm(ks[13], (DEPTH, PEER_HEADS, 2, PEER_N_KEYS, PEER_DHALF), PEER_DHALF ** -0.5),
        'peer_u': nrm(ks[14], (DEPTH, PEER_N_EXPERTS, D_MODEL), d_inv),
        'peer_v': nrm(ks[15], (DEPTH, PEER_N_EXPERTS, D_MODEL), DN_BETA),
        'ln2_g': 1.0 + nrm(ks[16], (DEPTH, D_MODEL), 0.05),
        'ln2_b': nrm(ks[17], (DEPTH, D_MODEL), 0.02),
    }

def reference(x, mem, w_in, b_gate, w_mem_kv, rel_bias, hgrn_lb, hgrn_norm_w, w_branch, w_out,
              ln1_g, ln1_b, w_peer_q, peer_sub_keys, peer_u, peer_v, ln2_g, ln2_b):
    lb_layers = jnp.cumsum(jax.nn.softmax(hgrn_lb.astype(jnp.float32), axis=0), axis=0)
    h = x
    for layer in range(DEPTH):
        b, s, _ = h.shape
        proj = jnp.einsum('bsd,de->bse', h, w_in[layer])
        dil, hg, mem_q, gate_logits = jnp.split(proj, IN_SPLITS, axis=-1)
        a_out = _dilated_attention(dil, rel_bias)
        f_raw, i_in, q_in, g_in = jnp.split(hg, 4, axis=-1)
        b_out = _hgrn2(f_raw, i_in, q_in, g_in, lb_layers[layer], hgrn_norm_w[layer])
        c_out = _memory_attention(mem_q, mem, w_mem_kv[layer])
        branches = jnp.stack([a_out, b_out, c_out], axis=2)
        gates = jax.nn.sigmoid((gate_logits + b_gate[layer]).reshape(b, s, N_BRANCHES, D_MODEL))
        widened = jnp.einsum('bsgw,gwd->bsgd', branches, w_branch[layer])
        merged = jnp.sum(gates * widened, axis=2)
        mix = jnp.einsum('bsd,de->bse', merged, w_out[layer])
        h = _layer_norm(DN_ALPHA * h + mix, ln1_g[layer], ln1_b[layer])
        ffn = _peer(h, w_peer_q[layer], peer_sub_keys[layer], peer_u[layer], peer_v[layer])
        h = _layer_norm(DN_ALPHA * h + ffn, ln2_g[layer], ln2_b[layer])
    return h


_drawn_inputs = setup_inputs


def setup_inputs(seed=0):
    import zlib

    import numpy as np

    out = dict(_drawn_inputs(seed))
    spreads = {}
    factors = {'b_gate': 3.343, 'rel_bias': 3.58, 'hgrn_norm_w': 3.003, 'ln2_b': 2.881}
    for name, (base, spread) in spreads.items():
        noise = np.random.default_rng([zlib.crc32(name.encode()), seed]).standard_normal(out[name].shape)
        drawn = base * np.exp(spread * noise) if base else spread * noise
        out[name] = __import__('jax').numpy.asarray(drawn.astype(out[name].dtype))
    for name, factor in factors.items():
        out[name] = (out[name] * factor).astype(out[name].dtype)
    return out
```

```python
import math
from contextlib import ExitStack

import numpy as np

import concourse.bass as bass
from concourse import mybir

F32 = mybir.dt.float32
F32R = mybir.dt.float32r
U32 = mybir.dt.uint32
ALU = mybir.AluOpType
ACT = mybir.ActivationFunctionType
AX = mybir.AxisListType.X

P = 128
S = 1024
D = 1024
KD = D // P
HALF = 512
NHALF = S // HALF
NB = HALF // P
NH = 4
G = 3
DIL = (1, 4, 16)
MEM = 256
CH = 64
NCH = HALF // CH
N_EXP = 16384
PH = 8
TOPK = 16
SLOTS = PH * TOPK
ALPHA = 2.0 ** 0.25
EPS = 1e-5
SCALE = 128.0 ** -0.5
NEG = -1e30
LOW = -3e38
BUCKETS = 32
BUCKET_MAX_DIST = 2048

BATCH = 4
RING = 4
E_ROWS = 4
E_GROUPS = SLOTS // E_ROWS
E_MID, E_OUT, E_PQ = 8, 8, 8
NBATCH = SLOTS // BATCH
G_OUT = E_MID * (D // P) // E_ROWS
G_PQ = G_OUT + E_OUT * (D // P // 2) // E_ROWS

C_Q, C_K, C_V = 0, G * NH * P, 2 * G * NH * P
C_HG = 3 * G * NH * P
C_MQ = C_HG + 4 * NH * P
C_GATE = C_MQ + NH * P

HEAD_TILES = [("f", C_HG), ("i", C_HG + 512), ("hq", C_HG + 1024), ("g", C_HG + 1536), ("mq", C_MQ)]
for _g in range(G):
    HEAD_TILES += [(f"k{_g}", C_K + 512 * _g), (f"v{_g}", C_V + 512 * _g), (f"q{_g}", C_Q + 512 * _g)]
NT_HEAD = len(HEAD_TILES)
NT_MID = 6
T_MID = NH * NT_HEAD
T_OUT = T_MID + KD * NT_MID
T_PQ = T_OUT + KD
NT = T_PQ + 2 * PH


def bucket_constants():
    exact = BUCKETS // 2
    onehot = np.zeros((BUCKETS, G, 384), np.float32)
    mask = np.zeros((NH, G, 384), np.float32)
    for g, dil in enumerate(DIL):
        for y in range(384):
            delta = (255 if g < 2 else 63) - y
            if not 0 <= delta <= 128:
                mask[:, g, y] = NEG
            n = max(delta, 0) * dil
            large = exact + int(math.log(max(n, 1) / exact) / math.log(BUCKET_MAX_DIST / exact) * (BUCKETS - exact))
            onehot[n if n < exact else min(large, BUCKETS - 1), g, y] = 1.0
    return onehot, mask


def shape_constants():
    onehot, mask = bucket_constants()
    s, c = np.arange(P)[:, None], np.arange(P)[None, :]
    causal = ((s <= c) & (s // CH == c // CH)).astype(np.uint32)
    resets = (np.arange(HALF) % CH != 0).astype(np.float32)
    return {
        "c_ident": np.eye(P, dtype=np.float32),
        "c_onehot": onehot,
        "c_mask": mask,
        "c_causal": np.tile(causal, (1, NB)),
        "c_resets": np.tile(resets, (P, 1)),
        "c_mean": np.full((P, P), 1.0 / P, np.float32),
        "c_iota": np.tile(np.arange(TOPK, dtype=np.float32), (P, PH * TOPK)),
    }


class Steps:

    def __init__(self, sem, names, seed=1):
        self.sem = sem
        self.seed = seed
        self.names = names
        self.n = len(names)
        self.at = {name: i + 1 for i, name in enumerate(names)}
        assert len(self.at) == self.n, "two steps of one name"
        self.emitted = 0

    def after(self, name, it):
        return (it + self.seed) * self.n + self.at[name]

    def mark(self, name):
        assert self.names[self.emitted % self.n] == name, (self.names[self.emitted % self.n], name)
        self.emitted += 1
        return self.sem, 1


class Banks:

    def __init__(self, jobs, banks):
        self.bank = {j: banks[i % len(banks)] for i, j in enumerate(jobs)}
        self.before = {}
        for i, j in enumerate(jobs):
            mine = [k for k in jobs if self.bank[k] == self.bank[j]]
            n = mine.index(j)
            self.before[j] = (mine[n - 1], 0) if n else (mine[-1], 1)


PE_HEAD = """P:f P:i P:hq P:g P:mq Ti P:k0 sc P:v0 Tkl P:q0 Tv0 u0 u1 P:k1 qk0a qk0b qma qmb P:v1 ho
P:q1 Tv1 pmp pmc pvm P:k2 p0p p0c lb0 ms P:v2 pv0 qk1a qk1b P:q2 Tv2 p1p p1c lb1 pv1 qk2a qk2b
p2p p2c lb2 pv2""".split()
JOBS = [n for n in PE_HEAD if ":" not in n]

DVE_HEAD = """fa key gm scan d1 inat qe ke d2 kl scm qa vt0 s0 s1 s2 s3 s4 s5 s6 s7 s8
l0x l0y l0b mx0 mxma mxmb nmm vt1 rl0 pn0 lse0 rlm pnm ho1 cmc c0c rrs hout vt2
l1a l1b mx1 rl1 pn1 lse1 c1c l2a l2b mx2 rl2 pn2 lse2 c2c
m1 m2 md e1 e2 er ew ea1 ea2 eo""".split()
ACT_HEAD = """f i hq sg mq ln e1 e1n k0 e2 e3 kln q0 vn0 k1 x0_0 x0_1 x0_2 x0_3 ln0 xm_0 xm_1 xm_2 xm_3
sq q1 vn1 vmh cmp ovm k2 c0p lbc0 rs ov0 x1_0 x1_1 x1_2 x1_3 ln1 q2 vn2 c1p lbc1 ov1
x2_0 x2_1 x2_2 x2_3 ln2 c2p lbc2 ov2 me""".split()
TILE_EVAC = {"f": ("A", "f"), "i": ("A", "i"), "hq": ("A", "hq"), "g": ("V", "gm"), "mq": ("A", "mq")}
for _g in range(G):
    TILE_EVAC |= {f"k{_g}": ("A", f"k{_g}"), f"v{_g}": ("V", f"vt{_g}"), f"q{_g}": ("A", f"q{_g}")}
JOB_EVAC = {
    "Ti": ("V", "inat"), "sc": ("V", "scm"), "Tkl": ("A", "kln"), "u0": ("V", "s7"), "u1": ("V", "s8"),
    "Tv0": ("A", "vn0"), "Tv1": ("A", "vn1"), "Tv2": ("A", "vn2"),
    "qk0a": ("V", "l0y"), "qk0b": ("V", "l0b"), "qma": ("A", "xm_1"), "qmb": ("A", "xm_3"),
    "qk1a": ("V", "l1a"), "qk1b": ("V", "l1b"), "qk2a": ("V", "l2a"), "qk2b": ("V", "l2b"),
    "ho": ("V", "ho1"), "ms": ("A", "rs"), "pmp": ("A", "cmp"), "pmc": ("V", "cmc"), "pvm": ("A", "ovm"),
    "p0p": ("A", "c0p"), "p0c": ("V", "c0c"), "p1p": ("A", "c1p"), "p1c": ("V", "c1c"),
    "p2p": ("A", "c2p"), "p2c": ("V", "c2c"), "lb0": ("A", "lbc0"), "lb1": ("A", "lbc1"), "lb2": ("A", "lbc2"),
    "pv0": ("A", "ov0"), "pv1": ("A", "ov1"), "pv2": ("A", "ov2"),
}


def layer(nc, A):
    x_d, out_d = A["x"], A["out"]
    w_in = A["w_in"].rearrange("l (k p) c -> p (l k) c", p=P)
    w_br = A["w_branch"].rearrange("l b (k p) c -> p (l b) k c", p=P)
    w_out = A["w_out"].rearrange("l (k p) c -> p (l k) c", p=P)
    w_pq = A["w_peer_q"].rearrange("l (k p) c -> p (l k) c", p=P)
    w_kv = A["w_mem_kv"].rearrange("l (k p) c -> p (l k) c", p=P)
    u_tab = A["peer_u"].rearrange("l e d -> (l e) d")
    v_tab = A["peer_v"].rearrange("l e d -> (l e) d")

    def dram(name, shape, dt=F32):
        return nc.dram_tensor(name, shape, dt, kind="Internal").ap()

    bias_rows = dram("bias_rows", (G, NH, 384))
    bias_skew = dram("bias_skew", (G * NH, P, 384))
    bias_tabs = dram("bias_tabs", (2, G * NH, P, 2 * P))
    kspill = dram("kspill", (G, NH, P, HALF))
    vspill = dram("vspill", (G, NH, P, HALF))
    subkeys_t = dram("subkeys_t", (P, 2 * PH, P))
    h1_d = dram("h1_d", (NHALF * NB, P, D))
    idx_d = dram("idx_d", (NHALF * NB, P, SLOTS), U32)
    gate_d = dram("gate_d", (NHALF * NB, P, SLOTS))

    ctx = ExitStack()
    with ctx:
        def sem(name):
            return ctx.enter_context(nc.semaphore(name))

        base = (nc.sbuf_base + 31) // 32 * 32
        top = [base, base]
        where = {}

        def at(name, shape, dt=F32, offset=None):
            size = (int(np.prod(shape[1:])) * 4 + 31) // 32 * 32
            if offset is None:
                offset = top[0]
            top[0] = offset + size
            top[1] = max(top[1], top[0])
            assert name not in where
            where[name] = offset
            return nc.alloc_sbuf_tensor_at(name, list(shape), dt, offset=offset)

        def over(name, other, shape):
            return nc.alloc_sbuf_tensor_at(name, list(shape), F32, offset=where[other])

        ident = at("ident", [P, P])
        mean_m = at("mean_m", [P, P])
        causal = at("causal", [P, HALF], U32)
        resets = at("resets", [P, HALF])
        cols = at("cols", [P, 36])
        lbc = at("lbc", [P, 32])
        zero1 = at("zero1", [P, 1])
        aident = at("aident", [P, P])
        zer = at("zer", [P, P])
        state = at("state", [P, NH, P])
        km = at("km", [P, NH, MEM])
        vm = at("vm", [P, 2, NH * P])
        w_raw = [at(f"w_raw{i}", [P, KD, P]) for i in range(2)]
        w_hi = [at(f"w_hi{i}", [P, KD, P], F32R) for i in range(2)]
        w_lo = [at(f"w_lo{i}", [P, KD, P], F32R) for i in range(2)]
        x_hi = at("x_hi", [P, KD, HALF], F32R)
        x_lo = at("x_lo", [P, KD, HALF], F32R)
        r_br = top[0]
        branch = at("branch", [P, 3 * NH, HALF])
        r_head = top[0]
        q_t = at("q_t", [P, G, HALF])
        k_t = at("k_t", [P, G, HALF])
        qm_t = at("qm_t", [P, HALF])
        v_tmp = at("v_tmp", [P, HALF])
        v_n = at("v_n", [P, G, HALF])
        kp = [at(f"kp{g}", [P, P if g == 0 else HALF]) for g in range(G)]
        vp = [at(f"vp{g}", [P, P if g == 0 else HALF]) for g in range(G)]
        bias = at("bias", [P, 4, 2 * P])
        prob = [at(f"prob{i}", [P, NB, 2 * P]) for i in range(2)]
        ptp = [at(f"ptp{i}", [P, HALF]) for i in range(2)]
        ptc = [at(f"ptc{i}", [P, HALF]) for i in range(2)]
        hf_, hkey, hi_, hlf, ha, he1, he1n, he2, he3, hq, hg = [
            at(n, [P, HALF]) for n in "hf hkey hi hlf ha he1 he1n he2 he3 hq hg".split()]
        chain = at("chain", [P, NCH, P])
        inat = at("inat", [P, NB, P])
        kln = over("kln", "he1n", [P, NB, P])
        scm = at("scm", [P, HALF])
        hsq = over("hsq", "he1", [P, HALF])
        ht = over("ht", "he1n", [P, HALF])
        hrs = over("hrs", "he2", [P, HALF])
        og = at("og", [P, G, HALF])
        lseb = over("lseb", "hf", [P, G, HALF])
        mmax = over("mmax", "hlf", [P, HALF])
        msum = over("msum", "ha", [P, HALF])
        vmh = at("vmh", [P, 2, P])
        stat = at("stat", [P, 4, 4, NB])
        e_ring = at("e_ring", [P, E_ROWS, D])
        h1e = at("h1e", [P, D])
        pidxe = at("pidxe", [P, SLOTS], U32)
        pgatee = at("pgatee", [P, SLOTS])
        icole = at("icole", [P, 2, E_ROWS], U32)
        dotse = at("dotse", [P, 2, E_ROWS])
        coefe = at("coefe", [P, SLOTS])
        o_hi = at("o_hi", [P, 3 * NH, HALF], F32R, offset=r_head)
        o_lo = at("o_lo", [P, 3 * NH, HALF], F32R)
        m_hi = at("m_hi", [P, KD, HALF], F32R)
        m_lo = at("m_lo", [P, KD, HALF], F32R)
        sgate = at("sgate", [P, 3, HALF], offset=r_br)
        macc = at("macc", [P, 2, HALF])
        r_ln = top[0]
        res = at("res", [P, NB, D], offset=r_head)
        qp = at("qp", [P, 2 * PH, HALF])
        r_top = top[0]
        ln_g = at("ln_g", [P, D], offset=r_ln)
        ln_b = at("ln_b", [P, D])
        mixt = at("mixt", [P, 2, HALF])
        bst = at("bst", [P, 2, 6])
        bmv = at("bmv", [P, 4])
        vals = at("vals", [P, 2 * PH, TOPK], offset=r_top)
        inds = at("inds", [P, 2 * PH, TOPK], U32)
        indf = at("indf", [P, 2 * PH, TOPK])
        left = at("left", [P, 4, P])
        cand = at("cand", [P, PH, TOPK, TOPK])
        cleft = at("cleft", [P, PH, TOPK * TOPK])
        best = at("best", [P, PH, TOPK])
        pos = at("pos", [P, PH, TOPK], U32)
        posu = at("posu", [P, 2, SLOTS], U32)
        posf = at("posf", [P, 2, SLOTS])
        pick = at("pick", [P, SLOTS, TOPK])
        got = at("got", [P, 2, SLOTS])
        idxu = at("idxu", [P, SLOTS], U32)
        gex = at("gex", [P, PH, TOPK])
        gsm = at("gsm", [P, 2, PH])
        gout = at("gout", [P, SLOTS])
        diage = at("diage", [P, E_ROWS, P])
        skt = at("skt", [P, 2 * PH, P], offset=r_br)
        iota = at("iota", [P, SLOTS, TOPK])
        qs = at("qs", [P, 2 * PH, P])

        onehot = at("onehot", [BUCKETS, G, 384], offset=r_head)
        maskr = at("maskr", [NH, G, 384])
        brow = at("brow", [NH, G, 384])
        rows36 = at("rows36", [36, P])
        tab = at("tab", [P, G * NH, 2 * P])
        relb = at("relb", [BUCKETS, G * NH])
        sk_n = at("sk_n", [P, 2 * PH, P])
        sk_t = at("sk_t", [P, 2 * PH, P])
        mem_n = at("mem_n", [P, 2, D])
        mem_t = at("mem_t", [P, KD, MEM])
        wkv = at("wkv", [P, KD, HALF])
        wvv = at("wvv", [P, KD, HALF])
        x_n = at("x_n", [P, NB, D], offset=r_head)
        u_ring = at("u_ring", [P, RING * BATCH, D], offset=r_br - 2 * KD * HALF * 4)
        v_ring = at("v_ring", [P, RING * BATCH, D])
        h1 = [at(f"h1_{i}", [P, D]) for i in range(2)]
        pidx = [at(f"pidx{i}", [P, SLOTS], U32) for i in range(2)]
        pgate = [at(f"pgate{i}", [P, SLOTS]) for i in range(2)]
        icol = at("icol", [P, RING, BATCH], U32)
        dots = at("dots", [P, RING, BATCH])
        gel = at("gel", [P, RING, BATCH])
        coef = at("coef", [P, RING, BATCH])
        diag = at("diag", [P, RING, BATCH, P])
        res2 = [at(f"res2_{i}", [P, D]) for i in range(2)]
        g2 = at("g2", [P, D])
        b2 = at("b2", [P, D])
        bst2 = at("bst2", [P, 2, 6])
        bmv2 = at("bmv2", [P, 4])
        assert top[0] <= where["coefe"]

        ps = [ctx.enter_context(nc.psum_tensor(f"ps{i}", [P, HALF], F32)) for i in range(8)]
        PJ = [0, 1]
        banks = Banks(JOBS, [2, 3, 4, 5, 6, 7])

        const_in = sem("const_in")
        setup_in = sem("setup_in")
        setup_dma = sem("setup_dma")
        setup_pe, setup_act, setup_dve = sem("setup_pe"), sem("setup_act"), sem("setup_dve")
        w_landed = [sem(f"w_landed{i}") for i in range(2)]
        w_split = [sem(f"w_split{i}") for i in range(2)]
        w_used = [sem(f"w_used{i}") for i in range(2)]
        xn_in = sem("xn_in")
        stage = sem("stage")
        waited = sem("waited")
        PE = Steps(sem("pe_head"), PE_HEAD)
        V = Steps(sem("dve_head"), DVE_HEAD)
        AC = Steps(sem("act_head"), ACT_HEAD)
        BY = {"A": AC, "V": V}
        edge_in = [sem(f"edge_in{g}") for g in range(G)]
        spilled = [sem(f"spilled{g}") for g in range(G)]
        MP = Steps(sem("mid_pe"), "G0 B0 G1 B1 G2 B2".split())
        MA = Steps(sem("mid_act"), "s0 s1 s2".split())
        MV = Steps(sem("mid_dve"), "g0 g1 a1 g2 a2 hi lo".split())
        OP = Steps(sem("out_pe"), "O0 O1 T0 T1".split())
        OA = Steps(sem("out_act"), "c0 c1".split())
        OV = Steps(sem("out_dve"), "r0 r1".split())
        res_in = sem("res_in")
        LV = Steps(sem("ln_dve"), [f"{n}{tb}" for tb in range(NB) for n in ("st", "ag", "ep", "rc", "nm", "sg", "sb")])
        LA = Steps(sem("ln_act"), [f"sq{tb}" for tb in range(NB)])
        h1_out = sem("h1_out")
        XP = Steps(sem("xt_pe"), [f"t{k}" for k in range(KD)])
        XA = Steps(sem("xt_act"), [f"hi{k}" for k in range(KD)])
        XV = Steps(sem("xt_dve"), [f"lo{k}" for k in range(KD)])
        QP = Steps(sem("pq_pe"), "Q0 Q1".split())
        QA = Steps(sem("pq_act"), "c0 c1".split())
        TP = Steps(sem("topk_pe"), [f"s{q}" for q in range(4)])
        TA = Steps(sem("topk_act"), "qs ex".split())
        TK = Steps(sem("topk_dve"), [f"{n}{q}" for q in range(4) for n in ("max", "at", "rest", "max2", "at2")]
                   + "indf cand cmax cat crest cmax2 cat2 pos1 pos2 posf eq0 in0 got0 eq1 in1 got1 idx gsub gsum grec gate".split())
        o_split = sem("o_split")
        tk_in, tk_out = sem("tk_in"), sem("tk_out")
        e_blk = sem("e_blk")
        e_in = [sem(f"e_in{s}") for s in range(E_ROWS)]
        e_idx, e_moved = sem("e_idx"), sem("e_moved")
        e_dots, e_diag, e_acc = sem("e_dots"), sem("e_diag"), sem("e_acc")
        e_gelu, e_coef = sem("e_gelu"), sem("e_coef")
        p_dots, p_gelu, p_coef, p_diag, p_acc = (sem(n) for n in ("p_dots", "p_gelu", "p_coef", "p_diag", "p_acc"))
        p_idx = sem("p_idx")
        p_const = sem("p_const")
        par_in = sem("par_in")
        blk_in = [sem(f"blk_in{i}") for i in range(2)]
        u_in = [sem(f"u_in{i}") for i in range(RING * BATCH)]
        v_in = [sem(f"v_in{i}") for i in range(RING * BATCH)]
        p_close = sem("p_close")
        FA = Steps(sem("fin_act"), "c0 c1 sq".split(), seed=2)
        FV = Steps(sem("fin_dve"), "st ag ep rc nm sg sb".split())
        p_out = [sem(f"p_out{i}") for i in range(2)]

        block = ctx.enter_context(nc.Block())

        def psum_by_residue(t, dil):
            return t.rearrange("p (j r) -> p r j", r=dil)

        def grouped(t, dil):
            return t.rearrange("p (r j) -> p r j", r=dil)

        def apart(eng):
            eng.sem_inc(waited, 1)


        def cross(eng, n):
            eng.drain().then_inc(stage, 1)
            eng.wait_ge(stage, 3 * n)

        def edge_value(g, hf, h):
            per = 32 if g == 0 else 16
            return per * (h + 1) if hf == 0 else per * NH + (per + 32) * (h + 1)

        def boundary(hf, k):
            return 2 + 6 * hf + k

        @block.sync
        def _(sp):
            sp.dma_start(ident[:, :], A["c_ident"]).then_inc(const_in, 16)
            sp.dma_start(onehot[:, :, :], A["c_onehot"]).then_inc(const_in, 16)
            sp.dma_start(maskr[:, :, :], A["c_mask"]).then_inc(const_in, 16)
            sp.dma_start(relb[:, :], A["rel_bias"]).then_inc(const_in, 16)
            sp.dma_start(rows36[0:24, :], A["b_gate"].rearrange("l (a p) -> (l a) p", p=P)).then_inc(const_in, 16)
            sp.dma_start(rows36[24:32, :], A["hgrn_lb"].rearrange("l (a p) -> (l a) p", p=P)).then_inc(const_in, 16)
            sp.dma_start(rows36[32:36, :], A["hgrn_norm_w"].rearrange("l (a p) -> (l a) p", p=P)).then_inc(const_in, 16)
            sp.dma_start(mean_m[:, :], A["c_mean"]).then_inc(const_in, 16)
            sp.dma_start(causal[:, :], A["c_causal"]).then_inc(const_in, 16)
            sp.dma_start(resets[:, :], A["c_resets"]).then_inc(const_in, 16)
            sp.dma_start(mem_n[:, :, :], A["mem"].rearrange("b (m p) d -> p (b m) d", p=P)).then_inc(setup_in, 16)
            sp.dma_start(wkv[:, :, :], w_kv[:, :, 0:HALF]).then_inc(setup_in, 16)
            sp.dma_start(wvv[:, :, :], w_kv[:, :, HALF:2 * HALF]).then_inc(setup_in, 16)
            sp.dma_start(sk_n[:, :, :], A["peer_sub_keys"].rearrange("l h t n k -> n (l h t) k")).then_inc(setup_in, 16)
            sp.wait_ge(setup_dve, 2)
            sp.dma_start(bias_rows.rearrange("g h y -> h g y"), brow[:, :, :]).then_inc(setup_dma, 16)
            sp.wait_ge(setup_dma, 16)
            rep = bass.AP(tensor=bias_rows.tensor, offset=0, ap=[[384, G * NH], [0, P], [1, 384]])
            sp.dma_start(bias_skew, rep).then_inc(setup_dma, 16)
            sp.wait_ge(setup_dma, 32)
            n = 2
            with nc.allow_non_contiguous_dma(reason="rows of a diagonal-constant block"):
                for g in range(2):
                    for h in range(NH):
                        src = bass.AP(tensor=bias_skew.tensor, offset=(g * NH + h) * P * 384 + P - 1, ap=[[383, P], [1, 2 * P]])
                        sp.dma_start(tab[:, g * NH + h, :], src).then_inc(setup_dma, 16)
                        n += 1
                for h in range(NH):
                    for u in range(4):
                        src = bass.AP(tensor=bias_skew.tensor, offset=(2 * NH + h) * P * 384 + 31, ap=[[383, 32], [32, 2], [1, 32]])
                        dst = tab[32 * u:32 * u + 32, 2 * NH + h, :].rearrange("p (t k) -> p t k", t=2)[:, :, 32 * u:32 * u + 32]
                        sp.dma_start(dst, src).then_inc(setup_dma, 16)
                        n += 1
            sp.wait_ge(setup_dma, 16 * n)
            sp.dma_start(bias_tabs[1].rearrange("a p k -> p a k"), tab[:, :, :]).then_inc(setup_dma, 16)
            sp.wait_ge(setup_dma, 16 * n + 16)
            sp.sem_inc(xn_in, 1)
            sp.wait_ge(setup_dve, 9)
            sp.dma_start(bias_tabs[0].rearrange("a p k -> p a k"), tab[:, :, :]).then_inc(setup_dma, 16)
            sp.wait_ge(setup_act, 24)
            sp.dma_start(subkeys_t, sk_t[:, :, :]).then_inc(setup_dma, 16)
            sp.wait_ge(setup_dma, 16 * n + 48)

            def weight(n, src, k=KD):
                b, half_n = n
                sp.wait_ge(w_split[b], 2 * half_n + 2)
                apart(sp)
                sp.dma_start(w_raw[b][:, 0:k, :], src).then_inc(w_landed[b], 16)

            def load_e_block():
                sp.dma_start(h1e[:, :], h1_d[0]).then_inc(e_blk, 16)
                sp.dma_start(pidxe[:, :], idx_d[0]).then_inc(e_blk, 16)
                sp.dma_start(pgatee[:, :], gate_d[0]).then_inc(e_blk, 16)

            for hf in range(NHALF):
                t0 = hf * NT // 2
                sp.wait_ge(stage, 3 * (boundary(hf, 0) - 1))
                sp.dma_start(x_n[:, :, :], x_d[0, hf * HALF:(hf + 1) * HALF, :].rearrange("(b p) d -> p b d", p=P)).then_inc(xn_in, 16)
                if hf == 1:
                    load_e_block()
                with sp.Fori(0, NH) as h:
                    it = NH * hf + h
                    for t, (name, c0) in enumerate(HEAD_TILES):
                        if name[0] == "k":
                            g = int(name[1])
                            sp.wait_ge(PE.sem, PE.after(f"pv{g}", it - 1))
                            apart(sp)
                            sp.wait_ge(V.sem, V.after(("l0b", "l1b", "l2b")[g], it - 1))
                            apart(sp)
                            if g == 0:
                                sp.dma_start(bias[:, 0, :], bias_tabs[1, bass.ds(h, 1)].rearrange("a p k -> (a p) k")).then_inc(edge_in[g], 16)
                            sp.dma_start(bias[:, g + 1, :], bias_tabs[hf, bass.ds(g * NH + h, 1)].rearrange("a p k -> (a p) k")).then_inc(edge_in[g], 16)
                            if hf == 1:
                                c = HALF - P if g == 0 else 0
                                sp.dma_start(kp[g][:, :], kspill[g, bass.ds(h, 1), :, c:HALF].rearrange("a p k -> (a p) k")).then_inc(edge_in[g], 16)
                                sp.dma_start(vp[g][:, :], vspill[g, bass.ds(h, 1), :, c:HALF].rearrange("a p k -> (a p) k")).then_inc(edge_in[g], 16)
                        weight((t % 2, t0 + NT_HEAD // 2 * h + t // 2), w_in[:, :, bass.ds(c0 + P * h, P)])
                with sp.Fori(0, KD) as j:
                    for t in range(NT_MID):
                        b = t // 2
                        if t % 2 == 0:
                            src, k = w_in[:, :, bass.ds(C_GATE + b * D + P * j, P)], KD
                        else:
                            src, k = w_br[:, b, :, bass.ds(P * j, P)], NH
                        weight((t % 2, t0 + T_MID // 2 + NT_MID // 2 * j + t // 2), src, k)
                sp.wait_ge(stage, 3 * boundary(hf, 2))
                sp.dma_start(res[:, :, :], x_d[0, hf * HALF:(hf + 1) * HALF, :].rearrange("(b p) d -> p b d", p=P)).then_inc(res_in, 16)
                sp.dma_start(ln_g[:, :], A["ln1_g"].to_broadcast([P, D])).then_inc(res_in, 16)
                sp.dma_start(ln_b[:, :], A["ln1_b"].to_broadcast([P, D])).then_inc(res_in, 16)
                with sp.Fori(0, KD // 2) as e:
                    for t in range(2):
                        weight((t, t0 + T_OUT // 2 + e), w_out[:, :, bass.ds(2 * P * e + P * t, P)])
                with sp.Fori(0, PH) as e:
                    for t in range(2):
                        weight((t, t0 + T_PQ // 2 + e), w_pq[:, :, bass.ds(2 * P * e + P * t, P)])
                sp.wait_ge(stage, 3 * boundary(hf, 3))
                sp.dma_start(h1_d[NB * hf:NB * hf + NB].rearrange("b p d -> p b d"), res[:, :, :]).then_inc(h1_out, 16)
                sp.dma_start(skt[:, :, :], subkeys_t).then_inc(tk_in, 16)
                sp.dma_start(iota[:, :, :].rearrange("p a b -> p (a b)"), A["c_iota"]).then_inc(tk_in, 16)
                with sp.Fori(0, NB) as tb:
                    sp.wait_ge(TK.sem, TK.after("gate", NB * hf + tb))
                    apart(sp)
                    sp.dma_start(idx_d[bass.ds(NB * hf + tb, 1)].rearrange("a p k -> (a p) k"), idxu[:, :]).then_inc(tk_out, 16)
                    sp.dma_start(gate_d[bass.ds(NB * hf + tb, 1)].rearrange("a p k -> (a p) k"), gout[:, :]).then_inc(tk_out, 16)
                sp.wait_ge(h1_out, 16 * (hf + 1))
                sp.wait_ge(tk_out, 32 * NB * (hf + 1) + 32)

    
            sp.wait_ge(stage, 3 * boundary(1, 5))
            sp.dma_start(g2[:, :], A["ln2_g"].to_broadcast([P, D])).then_inc(par_in, 16)
            sp.dma_start(b2[:, :], A["ln2_b"].to_broadcast([P, D])).then_inc(par_in, 16)

            def load_block(tb, o):
                sp.dma_start(h1[o][:, :], h1_d[bass.ds(tb, 1)].rearrange("a p d -> (a p) d")).then_inc(blk_in[o], 16)
                sp.dma_start(pidx[o][:, :], idx_d[bass.ds(tb, 1)].rearrange("a p d -> (a p) d")).then_inc(blk_in[o], 16)
                sp.dma_start(pgate[o][:, :], gate_d[bass.ds(tb, 1)].rearrange("a p d -> (a p) d")).then_inc(blk_in[o], 16)

            def store_block(tb, o):
                sp.wait_ge(FV.sem, FV.after("sb", tb))
                apart(sp)
                sp.dma_start(out_d[0, bass.ds(P * tb, P), :], res2[o][:, :]).then_inc(p_out[o], 16)

            NBLK = NHALF * NB
            load_block(1, 1)
            load_block(2, 0)
            store_block(0, 0)
            store_block(1, 1)
            load_block(3, 1)
            with sp.Fori(1, NBLK // 2 - 1) as i:
                for o in range(2):
                    store_block(2 * i + o, o)
                    load_block(2 * i + o + 2, o)
            for o in range(2):
                store_block(NBLK - 2 + o, o)
            for o in range(2):
                sp.wait_ge(p_out[o], 16 * (NBLK // 2) + 16)

        @block.gpsimd
        def _(pool):
            for b in range(2):
                pool.sem_inc(w_split[b], 2)
            pool.memset(zero1[:, :], 0.0).then_inc(p_const, 1)
            pool.wait_ge(p_const, 3)
            def split_lo_only(b, m, k=KD):
                pool.wait_ge(w_split[b], 2 * m + 3)
                pool.tensor_tensor(out=w_lo[b][:, 0:k, :], in0=w_raw[b][:, 0:k, :], in1=w_hi[b][:, 0:k, :].bitcast(F32),
                                   op=ALU.subtract).then_inc(w_split[b], 1)

            def split_hi_lo(b, m):
                pool.wait_ge(w_landed[b], 16 * m + 16)
                pool.wait_ge(w_used[b], m + 1)
                pool.tensor_tensor(out=w_hi[b][:, :, :], in0=w_raw[b][:, :, :],
                                   in1=zero1[:, :].unsqueeze(2).to_broadcast([P, KD, P]), op=ALU.add).then_inc(w_split[b], 1)
                split_lo_only(b, m)

            def gather_rows(first, last, group, slot, table, freed):
                for k in range(first, last):
                    s, r, g = k % E_ROWS, k // E_ROWS % 2, group + k // E_ROWS
                    pool.wait_ge(freed[0], E_ROWS * (g - freed[1]) + s + 1)
                    if s == 0:
                        pool.wait_ge(e_blk, 48)
                        pool.tensor_copy(icole[:, r, :], pidxe[:, bass.ds(slot + k, E_ROWS)]).then_inc(e_idx, 1)
                        pool.wait_ge(e_idx, g + 1)
                    apart(pool)
                    pool.indirect_dma_start(out=e_ring[:, s, :], out_offset=None, in_=table,
                                            in_offset=bass.IndirectOffsetOnAxis(ap=icole[:, r, s:s + 1], axis=0)).then_inc(e_in[s], 16)

            def u_rows(first, last, group, slot):
                gather_rows(first, last, group, slot, u_tab, (e_dots, 0))

            for hf in range(NHALF):
                t0 = hf * NT // 2
                with pool.Fori(0, NH) as h:
                    for t in range(NT_HEAD):
                        split_hi_lo(t % 2, t0 + NT_HEAD // 2 * h + t // 2)
                with pool.Fori(0, KD) as j:
                    for t in range(NT_MID):
                        split_lo_only(t % 2, t0 + T_MID // 2 + NT_MID // 2 * j + t // 2, KD if t % 2 == 0 else NH)
                        if hf == 1:
                            u_rows(E_MID * t // NT_MID, E_MID * (t + 1) // NT_MID, E_MID // E_ROWS * j, E_MID * j)
                with pool.Fori(0, KD // 2) as e:
                    for t in range(2):
                        split_lo_only(t, t0 + T_OUT // 2 + e)
                        if hf == 1:
                            u_rows(E_OUT * t // 2, E_OUT * (t + 1) // 2, G_OUT + E_OUT // E_ROWS * e, E_ROWS * G_OUT + E_OUT * e)
                with pool.Fori(0, PH // 2) as e:
                    for t in range(4):
                        split_lo_only(t % 2, t0 + T_PQ // 2 + 2 * e + t // 2)
                        if hf == 1:
                            u_rows(E_PQ * t // 4, E_PQ * (t + 1) // 4, G_PQ + E_PQ // E_ROWS * e, E_ROWS * G_PQ + E_PQ * e)
            pool.wait_ge(e_dots, E_ROWS + SLOTS)
            apart(pool)
            with pool.Fori(0, NB) as tb:
                gather_rows(0, SLOTS // NB, E_GROUPS + E_GROUPS // NB * tb, SLOTS // NB * tb, v_tab,
                            (e_acc, E_GROUPS))

            def rows(table, ring, landed, r):
                for s in range(BATCH):
                    pool.indirect_dma_start(
                        out=ring[:, BATCH * r + s, :], out_offset=None, in_=table,
                        in_offset=bass.IndirectOffsetOnAxis(ap=icol[:, r, s:s + 1], axis=0)).then_inc(landed[BATCH * r + s], 16)

            def block_rows(i, o):
                pool.wait_ge(blk_in[o], 48 * (i + o))
                apart(pool)
                with pool.Fori(0, NBATCH // RING) as q:
                    for r in range(RING):
                        b = NBATCH * (2 * i + o - 1) + RING * q + r
                        pool.wait_ge(p_acc, b + 1)
                        pool.tensor_copy(icol[:, r, :], pidx[o][:, bass.ds(BATCH * (RING * q + r), BATCH)]).then_inc(p_idx, 1)
                        pool.wait_ge(p_idx, b + 1)
                        pool.wait_ge(p_dots, b + 1)
                        apart(pool)
                        rows(u_tab, u_ring, u_in, r)
                        rows(v_tab, v_ring, v_in, r)

            block_rows(0, 1)
            with pool.Fori(1, NHALF * NB // 2) as i:
                for o in range(2):
                    block_rows(i, o)

        @block.tensor
        def _(pe):
            pe.sem_inc(PE.sem, PE.n)
            for st in (MP, OP, XP, QP, TP):
                pe.sem_inc(st.sem, st.n)
            pe.sem_inc(p_acc, RING)
            pe.sem_inc(w_used[0], 1)
            pe.sem_inc(e_acc, E_ROWS)
            pe.wait_ge(const_in, 160)
            pe.transpose(ps[0][:, 0:36], rows36[:, :], ident[0:36, 0:36]).then_inc(setup_pe, 1)
            for g in range(G):
                pe.matmul(ps[1 + g][0:NH, 0:384], relb[:, NH * g:NH * g + NH], onehot[:, g, :],
                          start=True, stop=True).then_inc(setup_pe, 1)
            pe.wait_ge(setup_in, 64)
            for q in range(4):
                if q >= 2:
                    pe.wait_ge(setup_act, 20 + q - 1)
                for j in range(4):
                    last = pe.transpose(ps[4 + q % 2][:, P * j:P * j + P], sk_n[:, 4 * q + j, :], ident[:, :])
                last.then_inc(setup_pe, 1)
            for q in range(4):
                if q >= 2:
                    pe.wait_ge(setup_act, 24 + q - 1)
                for j in range(4):
                    k, m = 2 * q + j // 2, j % 2
                    last = pe.transpose(ps[6 + q % 2][:, P * j:P * j + P], mem_n[:, m, P * k:P * k + P], ident[:, :])
                last.then_inc(setup_pe, 1)
            pe.wait_ge(setup_act, 28)
            pe.wait_ge(setup_dve, 10)
            for h in range(NH):
                for k in range(KD):
                    last = pe.matmul(ps[h // 2][:, MEM * (h % 2):MEM * (h % 2) + MEM], wkv[:, k, P * h:P * h + P], mem_t[:, k, :],
                                     start=(k == 0), stop=(k == KD - 1))
            last.then_inc(setup_pe, 1)
            for m in range(2):
                for k in range(KD):
                    last = pe.matmul(ps[2 + m][:, :], mem_t[:, k, P * m:P * m + P], wvv[:, k, :],
                                     start=(k == 0), stop=(k == KD - 1))
            last.then_inc(setup_pe, 1)
            cross(pe, 1)

            def tile(n, hi, lo, k_n, out):
                b, m = n
                pe.wait_ge(w_split[b], 2 * m + 3)
                for k in range(k_n):
                    first = pe.matmul(out, w_hi[b][:, k, :], hi[:, k, :], start=(k == 0), stop=False)
                    if k == 0:
                        first.then_inc(w_used[1 - b], 1)
                    pe.matmul(out, w_hi[b][:, k, :], lo[:, k, :], start=False, stop=False)
                pe.wait_ge(w_split[b], 2 * m + 4)
                for k in range(k_n):
                    last = pe.matmul(out, w_lo[b][:, k, :], hi[:, k, :], start=False, stop=(k == k_n - 1))
                return last

            def transposes(out, blocks):
                for n, src in enumerate(blocks):
                    last = pe.transpose(out[:, P * n:P * n + P], src, ident[:, :])
                return last

            def transposed_half(src, it):
                for k in range(KD):
                    if k >= 4:
                        pe.wait_ge(XV.sem, XV.after(f"lo{k - 4}", it))
                    transposes(ps[2 + k % 4], [src[:, tb, P * k:P * k + P] for tb in range(NB)]).then_inc(*XP.mark(f"t{k}"))

            for hf in range(NHALF):
                t0 = hf * NT // 2
                pe.wait_ge(xn_in, 17 + 16 * hf)
                transposed_half(x_n, 2 * hf)
                cross(pe, boundary(hf, 0))

                with pe.Fori(0, NH) as h:
                    it = NH * hf + h

                    def a(name):
                        pe.wait_ge(AC.sem, AC.after(name, it))

                    def v(name):
                        pe.wait_ge(V.sem, V.after(name, it))

                    def bank(job):
                        before, back = banks.before[job]
                        by, step = JOB_EVAC[before]
                        pe.wait_ge(BY[by].sem, BY[by].after(step, it - back))
                        return ps[banks.bank[job]]

                    def project(t):
                        name, _ = HEAD_TILES[t]
                        by, step = TILE_EVAC[HEAD_TILES[t - 2][0]]
                        pe.wait_ge(BY[by].sem, BY[by].after(step, it - (t < 2)))
                        last = tile((t % 2, t0 + NT_HEAD // 2 * h + t // 2), x_hi, x_lo, KD, ps[PJ[t % 2]][:, :])
                        last.then_inc(*PE.mark("P:" + name))

                    def logits(g, part):
                        out = bank(f"qk{g}{'ab'[part]}")
                        if part == 0:
                            a(f"q{g}")
                            if hf == 1:
                                pe.wait_ge(edge_in[g], edge_value(g, hf, h))
                        for b in (2 * part, 2 * part + 1):
                            qb = q_t[:, g, P * b:P * b + P]
                            o = 2 * P * (b % 2)
                            if g == 0 and b > 0:
                                last = pe.matmul(out[:, o:o + 2 * P], qb, k_t[:, g, P * (b - 1):P * (b + 1)], start=True, stop=True)
                            else:
                                pk = kp[g][:, 0:P] if g == 0 else kp[g][:, P * b:P * b + P]
                                pe.matmul(out[:, o:o + P], qb, pk, start=True, stop=True)
                                last = pe.matmul(out[:, o + P:o + 2 * P], qb, k_t[:, g, P * b:P * b + P], start=True, stop=True)
                        last.then_inc(*PE.mark(f"qk{g}{'ab'[part]}"))

                    def prob_t(i, tag, part):
                        out = bank(f"p{tag}{'pc'[part]}")
                        transposes(out, [prob[i][:, b, P * part:P * part + P] for b in range(NB)]).then_inc(*PE.mark(f"p{tag}{'pc'[part]}"))

                    def values(g, i):
                        out = bank(f"pv{g}")
                        a(f"c{g}p")
                        v(f"c{g}c")
                        for b in range(NB):
                            if g == 0:
                                pv = v_n[:, g, P * (b - 1):P * b] if b else vp[g][:, :]
                            else:
                                pv = vp[g][:, P * b:P * b + P]
                            pe.matmul(out[:, P * b:P * b + P], pv, ptp[i][:, P * b:P * b + P], start=True, stop=False)
                            last = pe.matmul(out[:, P * b:P * b + P], v_n[:, g, P * b:P * b + P], ptc[i][:, P * b:P * b + P], start=False, stop=True)
                        last.then_inc(*PE.mark(f"pv{g}"))

                    def lse_rows(g):
                        out = bank(f"lb{g}")
                        v(f"lse{g}")
                        for b in range(NB):
                            last = pe.matmul(out[:, P * b:P * b + P], stat[:, g, 3, b:b + 1].to_broadcast([P, P]), ident[:, :],
                                             start=True, stop=True)
                        last.then_inc(*PE.mark(f"lb{g}"))

                    def v_blocks(g):
                        out = bank(f"Tv{g}")
                        v(f"vt{g}")
                        transposes(out, [v_tmp[:, P * b:P * b + P] for b in range(NB)]).then_inc(*PE.mark(f"Tv{g}"))

                    for t in range(5):
                        project(t)
                    out = bank("Ti")
                    a("i")
                    transposes(out, [hi_[:, P * b:P * b + P] for b in range(NB)]).then_inc(*PE.mark("Ti"))
                    project(5)
                    out = bank("sc")
                    v("ke")
                    for b in range(NB):
                        last = pe.matmul(out[:, P * b:P * b + P], he1n[:, P * b:P * b + P], he1[:, P * b:P * b + P], start=True, stop=True)
                    last.then_inc(*PE.mark("sc"))
                    project(6)
                    out = bank("Tkl")
                    v("kl")
                    transposes(out, [he2[:, P * b:P * b + P] for b in range(NB)]).then_inc(*PE.mark("Tkl"))
                    project(7)
                    v_blocks(0)
                    a("kln")
                    v("inat")
                    for j in range(2):
                        out = bank(f"u{j}")
                        for n in range(4):
                            c = 2 * n + j
                            r0 = CH * j
                            last = pe.matmul(out[:, P * n:P * n + P], kln[r0:r0 + CH, c // 2, :], inat[r0:r0 + CH, c // 2, :], start=True, stop=True)
                        last.then_inc(*PE.mark(f"u{j}"))
                    project(8)
                    logits(0, 0)
                    logits(0, 1)
                    for j in range(2):
                        out = bank(f"qm{'ab'[j]}")
                        a("mq")
                        for n in range(2):
                            b = 2 * j + n
                            last = pe.matmul(out[:, MEM * n:MEM * n + MEM], qm_t[:, P * b:P * b + P],
                                             km[:, bass.ds(h, 1), :].rearrange("p a m -> p (a m)"), start=True, stop=True)
                        last.then_inc(*PE.mark(f"qm{'ab'[j]}"))
                    project(9)
                    out = bank("ho")
                    v("s7")
                    for b in range(NB):
                        pe.matmul(out[:, P * b:P * b + P], inat[:, b, :], scm[:, P * b:P * b + P], start=True, stop=False)
                        for c in (2 * b, 2 * b + 1):
                            last = pe.matmul(out[:, CH * c:CH * c + CH], chain[:, c, :], hq[:, CH * c:CH * c + CH], start=False, stop=(c % 2 == 1))
                    last.then_inc(*PE.mark("ho"))
                    project(10)
                    v_blocks(1)
                    v("pnm")
                    prob_t(1, "m", 0)
                    prob_t(1, "m", 1)
                    out = bank("pvm")
                    a("cmp")
                    v("cmc")
                    pe.matmul(out[:, :], vmh[:, 0, :], ptp[0][:, :], start=True, stop=False)
                    pe.matmul(out[:, :], vmh[:, 1, :], ptc[0][:, :], start=False, stop=True).then_inc(*PE.mark("pvm"))
                    project(11)
                    v("pn0")
                    prob_t(0, "0", 0)
                    prob_t(0, "0", 1)
                    lse_rows(0)
                    out = bank("ms")
                    a("sq")
                    pe.matmul(out[:, :], mean_m[:, :], hsq[:, :], start=True, stop=True).then_inc(*PE.mark("ms"))
                    project(12)
                    values(0, 1)
                    logits(1, 0)
                    logits(1, 1)
                    project(13)
                    v_blocks(2)
                    v("pn1")
                    prob_t(0, "1", 0)
                    prob_t(0, "1", 1)
                    lse_rows(1)
                    values(1, 0)
                    logits(2, 0)
                    logits(2, 1)
                    v("pn2")
                    prob_t(1, "2", 0)
                    prob_t(1, "2", 1)
                    lse_rows(2)
                    values(2, 1)
                cross(pe, boundary(hf, 1))
                pe.wait_ge(o_split, 2 * hf + 2)

                with pe.Fori(0, KD) as j:
                    it = KD * hf + j
                    for t in range(NT_MID):
                        b, name = t // 2, f"{'GB'[t % 2]}{t // 2}"
                        n = (t % 2, t0 + T_MID // 2 + NT_MID // 2 * j + t // 2)
                        if t % 2 == 0:
                            pe.wait_ge(MA.sem, MA.after(f"s{(b - 1) % 3}", it - (b == 0)))
                            last = tile(n, x_hi, x_lo, KD, ps[0][:, :])
                        else:
                            pe.wait_ge(MV.sem, MV.after(f"g{(b - 1) % 3}", it - (b == 0)))
                            last = tile(n, o_hi[:, NH * b:NH * b + NH, :], o_lo[:, NH * b:NH * b + NH, :], NH, ps[1][:, :])
                        last.then_inc(*MP.mark(name))
                cross(pe, boundary(hf, 2))

                with pe.Fori(0, KD // 2) as e:
                    it = KD // 2 * hf + e
                    for t in range(2):
                        pe.wait_ge(OA.sem, OA.after(f"c{t}", it - 1))
                        tile((t, t0 + T_OUT // 2 + e), m_hi, m_lo, KD, ps[t][:, :]).then_inc(*OP.mark(f"O{t}"))
                    for t in range(2):
                        pe.wait_ge(OA.sem, OA.after(f"c{t}", it))
                        pe.wait_ge(OV.sem, OV.after(f"r{t}", it - 1))
                        transposes(ps[2 + t], [mixt[:, t, P * b:P * b + P] for b in range(NB)]).then_inc(*OP.mark(f"T{t}"))
                pe.wait_ge(LV.sem, LV.after(f"sb{NB - 1}", hf))
                transposed_half(res, 2 * hf + 1)
                cross(pe, boundary(hf, 3))

                with pe.Fori(0, PH // 2) as e2:
                    for e, t in ((2 * e2 + u, t) for u in range(2) for t in range(2)):
                        it = PH * hf + e
                        pe.wait_ge(QA.sem, QA.after(f"c{t}", it - 1))
                        tile((t, t0 + T_PQ // 2 + e), x_hi, x_lo, KD, ps[t][:, :]).then_inc(*QP.mark(f"Q{t}"))
                cross(pe, boundary(hf, 4))

                pe.wait_ge(tk_in, 32 * hf + 32)
                if hf == 1:
                    pe.wait_ge(e_blk, 48)
                    for c in range(2):
                        pe.matmul(ps[c][:, :], aident[:, :], h1e[:, HALF * c:HALF * c + HALF], start=True, stop=False)
                with pe.Fori(0, NB) as tb:
                    it = NB * hf + tb
                    pe.wait_ge(TA.sem, TA.after("qs", it))
                    for q in range(4):
                        pe.wait_ge(TK.sem, TK.after(f"rest{q}", it - 1))
                        for n in range(4):
                            last = pe.matmul(ps[2 + q][:, P * n:P * n + P], qs[:, 4 * q + n, :], skt[:, 4 * q + n, :], start=True, stop=True)
                        last.then_inc(*TP.mark(f"s{q}"))
                    if hf == 1:
                        for k in range(SLOTS // NB):
                            s, g = k % E_ROWS, E_GROUPS // NB * tb + k // E_ROWS
                            pe.wait_ge(e_diag, E_ROWS * g + s + 1)
                            pe.wait_ge(e_in[s], 16 * (E_GROUPS + g) + 16)
                            for c in range(2):
                                last = pe.matmul(ps[c][:, :], diage[:, s, :], e_ring[:, s, HALF * c:HALF * c + HALF], start=False, stop=False)
                            last.then_inc(e_acc, 1)
                if hf == 1:
                    for c in range(2):
                        last = pe.matmul(ps[c][:, :], zer[:, :], h1e[:, HALF * c:HALF * c + HALF], start=False, stop=True)
                    last.then_inc(p_close, 1)
                cross(pe, boundary(hf, 5))

            def block_sum(i, o):
                tb = 2 * i + o
                acc = [ps[2 * o], ps[2 * o + 1]]
                pe.wait_ge(blk_in[o], 48 * (i + o))
                pe.wait_ge(FA.sem, FA.after("c1", tb - 2))
                for c in range(2):
                    pe.matmul(acc[c][:, :], aident[:, :], h1[o][:, HALF * c:HALF * c + HALF], start=True, stop=False)
                with pe.Fori(0, NBATCH // RING) as q:
                    for r in range(RING):
                        pe.wait_ge(p_diag, NBATCH * (tb - 1) + RING * q + r + 1)
                        for s in range(BATCH):
                            pe.wait_ge(v_in[BATCH * r + s], 16 * (NBATCH // RING * (tb - 1) + q) + 16)
                            for c in range(2):
                                last = pe.matmul(acc[c][:, :], diag[:, r, s, :], v_ring[:, BATCH * r + s, HALF * c:HALF * c + HALF],
                                                 start=False, stop=False)
                        last.then_inc(p_acc, 1)
                for c in range(2):
                    last = pe.matmul(acc[c][:, :], zer[:, :], h1[o][:, HALF * c:HALF * c + HALF], start=False, stop=True)
                last.then_inc(p_close, 1)

            block_sum(0, 1)
            with pe.Fori(1, NHALF * NB // 2) as i:
                for o in range(2):
                    block_sum(i, o)

        @block.scalar
        def _(act):
            act.sem_inc(AC.sem, AC.n)
            for st in (MA, OA, LA, XA, QA, TA):
                act.sem_inc(st.sem, st.n)
            act.sem_inc(FA.sem, FA.seed * FA.n)
            act.sem_inc(p_gelu, RING)
            for g in range(G):
                act.sem_inc(spilled[g], 32)
            for o in range(2):
                act.sem_inc(p_out[o], 16)
            act.wait_ge(setup_pe, 1)
            act.activation(cols[:, :], ps[0][:, 0:36], ACT.Copy).then_inc(setup_act, 1)
            act.wait_ge(setup_dve, 4)
            act.activation(lbc[:, 8:16], lbc[:, 0:8], ACT.Exp).then_inc(setup_act, 1)
            act.wait_ge(setup_act, 2)
            act.sem_inc(setup_act, 18)
            for q in range(4):
                act.wait_ge(setup_pe, 5 + q)
                act.activation(sk_t[:, 4 * q:4 * q + 4, :].rearrange("p a n -> p (a n)"), ps[4 + q % 2][:, :], ACT.Copy).then_inc(setup_act, 1)
            for q in range(4):
                act.wait_ge(setup_pe, 9 + q)
                act.activation(mem_t[:, 2 * q:2 * q + 2, :].rearrange("p a m -> p (a m)"), ps[6 + q % 2][:, :], ACT.Copy).then_inc(setup_act, 1)
            act.wait_ge(setup_pe, 13)
            for j in range(2):
                act.activation(km[:, 2 * j:2 * j + 2, :].rearrange("p a m -> p (a m)"), ps[j][:, :], ACT.Copy).then_inc(setup_act, 1)
            act.wait_ge(setup_pe, 14)
            for m in range(2):
                act.activation(vm[:, m, :], ps[2 + m][:, :], ACT.Copy).then_inc(setup_act, 1)
            cross(act, 1)

            def split_hi(it):
                for k in range(KD):
                    act.wait_ge(XP.sem, XP.after(f"t{k}", it))
                    act.activation(x_hi[:, k, :], ps[2 + k % 4][:, :], ACT.Copy).then_inc(*XA.mark(f"hi{k}"))

            def weight_hi(b, m, k=KD):
                act.wait_ge(w_landed[b], 16 * m + 16)
                act.wait_ge(w_used[b], m + 1)
                act.activation(w_hi[b][:, 0:k, :], w_raw[b][:, 0:k, :], ACT.Copy).then_inc(w_split[b], 1)

            def e_diags(first, last, tb):
                for k in range(first, last):
                    s = k % E_ROWS
                    act.wait_ge(e_acc, SLOTS // NB * tb + k + 1)
                    act.activation(diage[:, s, :], ident[:, :], ACT.Copy,
                                   scale=coefe[:, bass.ds(SLOTS // NB * tb + k, 1)]).then_inc(e_diag, 1)

            def e_gelus():
                act.wait_ge(e_moved, 2 + E_GROUPS)
                act.activation(coefe[:, :], coefe[:, :], ACT.Gelu).then_inc(e_gelu, 1)

            for hf in range(NHALF):
                t0 = hf * NT // 2
                split_hi(2 * hf)
                cross(act, boundary(hf, 0))
                with act.Fori(0, NH) as h:
                    it = NH * hf + h

                    def p(name, back=0):
                        act.wait_ge(PE.sem, PE.after(name, it - back))

                    def v(name, back=0):
                        act.wait_ge(V.sem, V.after(name, it - back))

                    def me(name):
                        act.wait_ge(AC.sem, AC.after(name, it))

                    def copy(step, out, in_, func=ACT.Copy, **kw):
                        return act.activation(out, in_, func, **kw).then_inc(*AC.mark(step))

                    def pj(t):
                        return ps[PJ[t % 2]][:, :]

                    def job(name):
                        return ps[banks.bank[name]]

                    def by_residue(step, buf, g, t, name):
                        p(name)
                        copy(step, grouped(buf[:, g, :], DIL[g]), psum_by_residue(pj(t), DIL[g]))

                    def exps(g, i, source, tag):
                        for b in range(NB):
                            act.activation(prob[i][:, b, :], source(b), ACT.Exp, bias=stat[:, g, 0, b:b + 1],
                                           scale=(SCALE if tag == "m" else 1.0), accum_out=stat[:, g, 1, b:b + 1]).then_inc(*AC.mark(f"x{tag}_{b}"))

                    def values_out(g):
                        p(f"pv{g}")
                        if g == 0:
                            v("eo", 1)
                        copy(f"ov{g}", psum_by_residue(og[:, g, :], DIL[g]), grouped(job(f"pv{g}")[:, :], DIL[g]))

                    def lse_out(g):
                        p(f"lb{g}")
                        copy(f"lbc{g}", psum_by_residue(lseb[:, g, :], DIL[g]), grouped(job(f"lb{g}")[:, :], DIL[g]))

                    def spill(g):
                        if hf == 0:
                            me(f"vn{g}")
                            act.dma_start(kspill[g, bass.ds(h, 1)].rearrange("a p k -> (a p) k"), k_t[:, g, :]).then_inc(spilled[g], 16)
                            act.dma_start(vspill[g, bass.ds(h, 1)].rearrange("a p k -> (a p) k"), v_n[:, g, :]).then_inc(spilled[g], 16)

                    def before_k(g):
                        if hf == 0:
                            act.wait_ge(spilled[g], 32 * h + 32)
                        p(f"qk{g}b", 1)

                    p("P:f")
                    v("ew", 1)
                    copy("f", hf_[:, :], pj(0), ACT.Sigmoid)
                    p("P:i")
                    p("Ti", 1)
                    copy("i", hi_[:, :], pj(1))
                    p("P:hq")
                    p("ho", 1)
                    copy("hq", hq[:, :], pj(2))
                    p("P:g")
                    v("ho1", 1)
                    copy("sg", hg[:, :], pj(3), ACT.Sigmoid)
                    p("P:mq")
                    p("qmb", 1)
                    copy("mq", qm_t[:, :], pj(4))
                    v("fa")
                    copy("ln", hlf[:, :], hf_[:, :], ACT.Ln)
                    v("d1")
                    p("sc", 1)
                    copy("e1", he1[:, :], hlf[:, :], ACT.Exp)
                    copy("e1n", he1n[:, :], hlf[:, :], ACT.Exp, scale=-1.0)
                    before_k(0)
                    by_residue("k0", k_t, 0, 5, "P:k0")
                    v("d2")
                    p("Tkl", 1)
                    copy("e2", he2[:, :], hf_[:, :], ACT.Exp)
                    v("s8", 1)
                    copy("e3", he3[:, :], ha[:, :], ACT.Exp)
                    p("Tkl")
                    p("u1", 1)
                    copy("kln", kln[:, :, :].rearrange("p b d -> p (b d)"), job("Tkl")[:, :])
                    by_residue("q0", q_t, 0, 7, "P:q0")
                    p("Tv0")
                    p("pv0", 1)
                    copy("vn0", v_n[:, 0, :], job("Tv0")[:, :])
                    spill(0)
                    before_k(1)
                    by_residue("k1", k_t, 1, 8, "P:k1")
                    v("mx0")
                    exps(0, 0, lambda b: prob[0][:, b, :], "0")
                    me("x0_3")
                    p("lb0", 1)
                    copy("ln0", stat[:, 0, 3, :], stat[:, 0, 1, :], ACT.Ln)
                    v("nmm")
                    p("qmb")
                    p("p2c", 1)
                    exps(3, 1, lambda b: job("qm" + "ab"[b // 2])[:, MEM * (b % 2):MEM * (b % 2) + MEM], "m")
                    p("ho")
                    p("ms", 1)
                    copy("sq", hsq[:, :], job("ho")[:, :], ACT.Square)
                    by_residue("q1", q_t, 1, 10, "P:q1")
                    p("Tv1")
                    p("pv1", 1)
                    copy("vn1", v_n[:, 1, :], job("Tv1")[:, :])
                    spill(1)
                    p("pvm", 1)
                    copy("vmh", vmh[:, :, :], vm[:, :, bass.ds(P * h, P)])
                    p("pmp")
                    p("pv1", 1)
                    copy("cmp", ptp[0][:, :], job("pmp")[:, :])
                    p("pvm")
                    copy("ovm", branch[:, bass.ds(2 * NH + h, 1), :].rearrange("p a t -> p (a t)"), job("pvm")[:, :])
                    before_k(2)
                    by_residue("k2", k_t, 2, 11, "P:k2")
                    p("p0p")
                    p("pv2", 1)
                    copy("c0p", ptp[1][:, :], job("p0p")[:, :])
                    lse_out(0)
                    p("ms")
                    v("hout", 1)
                    copy("rs", hrs[:, :], job("ms")[:, :], ACT.Sqrt, bias=EPS)
                    values_out(0)
                    v("mx1")
                    exps(1, 0, lambda b: prob[0][:, b, :], "1")
                    me("x1_3")
                    copy("ln1", stat[:, 1, 3, :], stat[:, 1, 1, :], ACT.Ln)
                    by_residue("q2", q_t, 2, 13, "P:q2")
                    p("Tv2")
                    copy("vn2", v_n[:, 2, :], job("Tv2")[:, :])
                    spill(2)
                    p("p1p")
                    copy("c1p", ptp[0][:, :], job("p1p")[:, :])
                    lse_out(1)
                    values_out(1)
                    v("mx2")
                    exps(2, 1, lambda b: prob[1][:, b, :], "2")
                    me("x2_3")
                    copy("ln2", stat[:, 2, 3, :], stat[:, 2, 1, :], ACT.Ln)
                    p("p2p")
                    copy("c2p", ptp[1][:, :], job("p2p")[:, :])
                    lse_out(2)
                    values_out(2)
                    v("md")
                    copy("me", lseb[:, :, :], lseb[:, :, :], ACT.Exp)
                if hf == 0:
                    for g in range(G):
                        act.wait_ge(spilled[g], 32 * NH + 32)
                cross(act, boundary(hf, 1))

                with act.Fori(0, KD) as j:
                    it = KD * hf + j
                    for b in range(3):
                        n = t0 + T_MID // 2 + NT_MID // 2 * j + b
                        weight_hi(0, n)
                        weight_hi(1, n, NH)
                        act.wait_ge(MP.sem, MP.after(f"G{b}", it))
                        act.wait_ge(MV.sem, MV.after(f"g{b}", it - 1))
                        act.activation(sgate[:, b, :], ps[0][:, :], ACT.Sigmoid,
                                       bias=cols[:, bass.ds(KD * b + j, 1)]).then_inc(*MA.mark(f"s{b}"))
                cross(act, boundary(hf, 2))

                with act.Fori(0, KD // 2) as e:
                    it = KD // 2 * hf + e
                    for t in range(2):
                        weight_hi(t, t0 + T_OUT // 2 + e)
                    for t in range(2):
                        act.wait_ge(OP.sem, OP.after(f"O{t}", it))
                        act.wait_ge(OP.sem, OP.after(f"T{t}", it - 1))
                        act.activation(mixt[:, t, :], ps[t][:, :], ACT.Copy).then_inc(*OA.mark(f"c{t}"))
                for tb in range(NB):
                    act.wait_ge(LV.sem, LV.after(f"ep{tb}", hf))
                    act.activation(bmv[:, 3:4], bmv[:, 2:3], ACT.Sqrt).then_inc(*LA.mark(f"sq{tb}"))
                split_hi(2 * hf + 1)
                cross(act, boundary(hf, 3))

                with act.Fori(0, PH) as e:
                    it = PH * hf + e
                    for t in range(2):
                        weight_hi(t, t0 + T_PQ // 2 + e)
                    for t in range(2):
                        act.wait_ge(QP.sem, QP.after(f"Q{t}", it))
                        act.activation(qp[:, bass.ds(2 * e + t, 1), :].rearrange("p a t -> p (a t)"), ps[t][:, :], ACT.Copy).then_inc(*QA.mark(f"c{t}"))
                if hf == 1:
                    e_gelus()
                cross(act, boundary(hf, 4))

                with act.Fori(0, NB) as tb:
                    it = NB * hf + tb
                    act.wait_ge(TP.sem, TP.after("s3", it - 1))
                    act.activation(qs[:, :, :], qp[:, :, bass.ds(P * tb, P)], ACT.Copy).then_inc(*TA.mark("qs"))
                    if hf == 1:
                        e_diags(0, 3 * SLOTS // NB // 4, tb)
                    act.wait_ge(TK.sem, TK.after("gsub", it))
                    act.activation(gex[:, :, :], gex[:, :, :], ACT.Exp).then_inc(*TA.mark("ex"))
                    if hf == 1:
                        e_diags(3 * SLOTS // NB // 4, SLOTS // NB, tb)
                cross(act, boundary(hf, 5))

            def diagonals(i, o, q, r):
                b = NBATCH * (2 * i + o - 1) + RING * q + r
                act.wait_ge(p_coef, b + 1)
                act.wait_ge(p_acc, b + 1)
                for s in range(BATCH):
                    last = act.activation(diag[:, r, s, :], ident[:, :], ACT.Copy, scale=coef[:, r, s:s + 1])
                last.then_inc(p_diag, 1)

            def finish(i, o):
                tb = 2 * i + o
                act.wait_ge(p_close, tb + 1)
                act.wait_ge(p_out[o], 16 * i + 16)
                for c in range(2):
                    act.activation(res2[o][:, HALF * c:HALF * c + HALF], ps[2 * o + c][:, :], ACT.Copy).then_inc(*FA.mark(f"c{c}"))
                act.wait_ge(FV.sem, FV.after("ep", tb))
                act.activation(bmv2[:, 3:4], bmv2[:, 2:3], ACT.Sqrt).then_inc(*FA.mark("sq"))

            def block_acts(i, o):
                with act.Fori(0, NBATCH // RING) as q:
                    for r in range(RING):
                        act.wait_ge(p_dots, RING + NBATCH * (2 * i + o - 1) + RING * q + r + 1)
                        act.activation(gel[:, r, :], dots[:, r, :], ACT.Gelu).then_inc(p_gelu, 1)
                        diagonals(i, o, q, r)
                finish(i, o)

            finish(0, 0)
            block_acts(0, 1)
            with act.Fori(1, NHALF * NB // 2) as i:
                for o in range(2):
                    block_acts(i, o)

        @block.vector
        def _(dve):
            dve.sem_inc(V.sem, V.n)
            for st in (MV, OV, LV, XV, TK, FV):
                dve.sem_inc(st.sem, st.n)
            dve.sem_inc(p_dots, RING)
            dve.sem_inc(tk_out, 32)
            dve.sem_inc(e_dots, E_ROWS)
            dve.sem_inc(e_moved, 2)
            dve.wait_ge(const_in, 160)
            dve.wait_ge(setup_pe, 4)
            for g in range(G):
                last = dve.tensor_tensor(out=brow[:, g, :], in0=ps[1 + g][0:NH, 0:384], in1=maskr[:, g, :], op=ALU.add)
            last.then_inc(setup_dve, 1)
            dve.memset(tab[:, 2 * NH:3 * NH, :], NEG).then_inc(setup_dve, 1)
            dve.wait_ge(setup_act, 1)
            dve.tensor_tensor(out=lbc[:, 16:20], in0=cols[:, 24:28], in1=cols[:, 28:32], op=ALU.max).then_inc(setup_dve, 1)
            dve.wait_ge(setup_dve, 3)
            for r in range(2):
                last = dve.tensor_tensor(out=lbc[:, 4 * r:4 * r + 4], in0=cols[:, 24 + 4 * r:28 + 4 * r], in1=lbc[:, 16:20], op=ALU.subtract)
            last.then_inc(setup_dve, 1)
            dve.wait_ge(setup_act, 2)
            dve.tensor_tensor(out=lbc[:, 20:24], in0=lbc[:, 8:12], in1=lbc[:, 12:16], op=ALU.add).then_inc(setup_dve, 1)
            dve.wait_ge(setup_dve, 5)
            dve.reciprocal(lbc[:, 20:24], lbc[:, 20:24]).then_inc(setup_dve, 1)
            dve.wait_ge(setup_dve, 6)
            dve.tensor_tensor(out=lbc[:, 24:28], in0=lbc[:, 8:12], in1=lbc[:, 20:24], op=ALU.mult).then_inc(setup_dve, 1)
            dve.tensor_tensor(out=lbc[:, 28:32], in0=lbc[:, 12:16], in1=lbc[:, 20:24], op=ALU.mult).then_inc(setup_dve, 1)
            dve.memset(state[:, :, :], 0.0)
            dve.tensor_scalar(out=aident[:, :], in0=ident[:, :], scalar1=ALPHA, scalar2=None, op0=ALU.mult).then_inc(p_const, 1)
            dve.memset(zer[:, :], 0.0).then_inc(p_const, 1)
            dve.wait_ge(xn_in, 1)
            dve.memset(tab[:, :, 0:P], NEG).then_inc(setup_dve, 1)
            dve.wait_ge(setup_dve, 9)
            dve.sem_inc(setup_dve, 1)
            cross(dve, 1)

            def split_lo(it):
                for k in range(KD):
                    dve.wait_ge(XA.sem, XA.after(f"hi{k}", it))
                    dve.tensor_tensor(out=x_lo[:, k, :], in0=ps[2 + k % 4][:, :], in1=x_hi[:, k, :].bitcast(F32),
                                      op=ALU.subtract).then_inc(*XV.mark(f"lo{k}"))

            def norm(mark, step, it, rows, stats, mv, gain, shift, sqrt_done, tag=""):
                for c in range(2):
                    last = dve.bn_stats(out=stats[:, c, :], in_=rows[:, HALF * c:HALF * c + HALF])
                last.then_inc(*mark("st" + tag))
                dve.wait_ge(step.sem, step.after("st" + tag, it))
                apart(dve)
                dve.bn_aggr(out=mv[:, 0:2], in_=stats[:, :, :]).then_inc(*mark("ag" + tag))
                dve.wait_ge(step.sem, step.after("ag" + tag, it))
                dve.tensor_scalar(out=mv[:, 2:3], in0=mv[:, 1:2], scalar1=EPS, scalar2=None, op0=ALU.add).then_inc(*mark("ep" + tag))
                sqrt_done()
                dve.reciprocal(mv[:, 3:4], mv[:, 3:4]).then_inc(*mark("rc" + tag))
                dve.wait_ge(step.sem, step.after("rc" + tag, it))
                dve.tensor_scalar(out=rows, in0=rows, scalar1=mv[:, 0:1], scalar2=mv[:, 3:4], op0=ALU.subtract, op1=ALU.mult).then_inc(*mark("nm" + tag))
                dve.wait_ge(step.sem, step.after("nm" + tag, it))
                dve.tensor_tensor(out=rows, in0=rows, in1=gain, op=ALU.mult).then_inc(*mark("sg" + tag))
                dve.wait_ge(step.sem, step.after("sg" + tag, it))
                dve.tensor_tensor(out=rows, in0=rows, in1=shift, op=ALU.add).then_inc(*mark("sb" + tag))

            def e_rows(first, last, group, slot):
                for k in range(first, last):
                    s, r, g = k % E_ROWS, k // E_ROWS % 2, group + k // E_ROWS
                    if s == 0:
                        dve.wait_ge(e_blk, 48)
                        dve.wait_ge(e_moved, g + 1)
                    dve.wait_ge(e_in[s], 16 * g + 16)
                    dve.tensor_tensor_reduce(out=e_ring[:, s, :], in0=e_ring[:, s, :], in1=h1e[:, :], scale=1.0, scalar=0.0,
                                             op0=ALU.mult, op1=ALU.add, accum_out=dotse[:, r, s:s + 1]).then_inc(e_dots, 1)
                    if s == E_ROWS - 1:
                        dve.wait_ge(e_dots, E_ROWS * g + 2 * E_ROWS)
                        dve.tensor_copy(coefe[:, bass.ds(slot + k - s, E_ROWS)], dotse[:, r, :]).then_inc(e_moved, 1)

            def e_gates():
                dve.wait_ge(e_gelu, 1)
                dve.tensor_tensor(out=coefe[:, :], in0=coefe[:, :], in1=pgatee[:, :], op=ALU.mult).then_inc(e_coef, 1)

            for hf in range(NHALF):
                split_lo(2 * hf)
                cross(dve, boundary(hf, 0))
                if hf == 0:
                    dve.memset(scm[:, :], 0.0)
                    for g in range(G):
                        dve.memset(kp[g][:, :], 0.0)
                        dve.memset(vp[g][:, :], 0.0)
                else:
                    dve.memset(scm[:, :], 0.0)
                with dve.Fori(0, NH) as h:
                    it = NH * hf + h

                    def a(name, back=0):
                        dve.wait_ge(AC.sem, AC.after(name, it - back))

                    def p(name, back=0):
                        dve.wait_ge(PE.sem, PE.after(name, it - back))

                    def me(name):
                        dve.wait_ge(V.sem, V.after(name, it))

                    def job(name):
                        return ps[banks.bank[name]]

                    def tt(step, out, in0, in1, op):
                        dve.tensor_tensor(out=out, in0=in0, in1=in1, op=op).then_inc(*V.mark(step))

                    def chunks(t):
                        return t[:, :].rearrange("p (c n) -> p c n", n=CH)

                    def at_chunk(t, n):
                        return chunks(t)[:, :, n:n + 1].to_broadcast([P, NCH, CH])

                    def pairs(name):
                        return job(name)[:, :].rearrange("p (b k) -> p b k", b=2)

                    def logit(step, g, blocks, src, table):
                        dve.scalar_tensor_tensor(out=prob[1 if g == 2 else 0][:, blocks, :],
                                                 in0=src, scalar=SCALE, in1=table, op0=ALU.mult, op1=ALU.add).then_inc(*V.mark(step))

                    def softmax_scale(g, tag, i):
                        a(f"x{tag}_3")
                        dve.reciprocal(stat[:, g, 2, :], stat[:, g, 1, :]).then_inc(*V.mark("rl" + tag))
                        me("rl" + tag)
                        tt("pn" + tag, prob[i][:, :, :], prob[i][:, :, :],
                           stat[:, g, 2, :].unsqueeze(2).to_broadcast([P, NB, 2 * P]), ALU.mult)

                    def lse(g):
                        a(f"ln{g}")
                        tt(f"lse{g}", stat[:, g, 3, :], stat[:, g, 3, :], stat[:, g, 0, :], ALU.subtract)

                    def maxes(g, i, last):
                        me(last)
                        dve.tensor_reduce(out=stat[:, g, 0, :], in_=prob[i][:, :, :], axis=AX, op=ALU.max, negate=True).then_inc(*V.mark(f"mx{g}"))

                    def v_tokens(g, t):
                        p(f"P:v{g}")
                        p(f"Tv{g - 1}") if g else p(f"Tv{G - 1}", 1)
                        dve.tensor_copy(grouped(v_tmp[:, :], DIL[g]), psum_by_residue(ps[PJ[t % 2]][:, :], DIL[g])).then_inc(*V.mark(f"vt{g}"))

                    def head_col(c0):
                        return bass.ds(c0 + h, 1)

                    a("f")
                    dve.tensor_scalar(out=hf_[:, :], in0=hf_[:, :], scalar1=lbc[:, head_col(28)], scalar2=lbc[:, head_col(24)],
                                      op0=ALU.mult, op1=ALU.add).then_inc(*V.mark("fa"))
                    me("fa")
                    dve.tensor_scalar(out=hkey[:, :], in0=hf_[:, :], scalar1=-1.0, scalar2=1.0, op0=ALU.mult, op1=ALU.add).then_inc(*V.mark("key"))
                    a("sg")
                    tt("gm", hg[:, :], ps[PJ[1]][:, :], hg[:, :], ALU.mult)
                    a("ln")
                    a("e3", 1)
                    dve.tensor_tensor_scan(out=ha[:, :], data0=resets[:, :], data1=hlf[:, :], initial=0.0, op0=ALU.mult, op1=ALU.add).then_inc(*V.mark("scan"))
                    me("scan")
                    tt("d1", chunks(hlf), chunks(ha), at_chunk(ha, CH // 2 - 1), ALU.subtract)
                    p("Ti")
                    p("ho", 1)
                    dve.tensor_copy(inat[:, :, :].rearrange("p b d -> p (b d)"), job("Ti")[:, :]).then_inc(*V.mark("inat"))
                    a("e1n")
                    tt("qe", he1[:, :], hq[:, :], he1[:, :], ALU.mult)
                    tt("ke", he1n[:, :], hkey[:, :], he1n[:, :], ALU.mult)
                    tt("d2", chunks(hf_), at_chunk(ha, CH - 1), chunks(ha), ALU.subtract)
                    a("e2")
                    tt("kl", he2[:, :], hkey[:, :], he2[:, :], ALU.mult)
                    p("sc")
                    apart(dve)
                    dve.copy_predicated(scm[:, :], causal[:, :], job("sc")[:, :]).then_inc(*V.mark("scm"))
                    a("e3")
                    me("qe")
                    tt("qa", hq[:, :], hq[:, :], he3[:, :], ALU.mult)
                    v_tokens(0, 6)
                    dve.tensor_copy(chain[:, 0, :], state[:, head_col(0), :].rearrange("p a d -> p (a d)")).then_inc(*V.mark("s0"))
                    for c in range(NCH):
                        me(f"s{c}")
                        if c < 2:
                            p(f"u{c}")
                        out = chain[:, c + 1, :] if c < NCH - 1 else state[:, head_col(0), :].rearrange("p a d -> p (a d)")
                        dve.scalar_tensor_tensor(out=out, in0=chain[:, c, :], scalar=he3[:, CH * c + CH - 1:CH * c + CH],
                                                 in1=job(f"u{c % 2}")[:, P * (c // 2):P * (c // 2) + P], op0=ALU.mult, op1=ALU.add).then_inc(*V.mark(f"s{c + 1}"))
                    dve.wait_ge(edge_in[0], edge_value(0, hf, h))
                    p("qk0a")
                    p("p1c", 1)
                    logit("l0x", 0, 0, job("qk0a")[:, 0:2 * P], bias[:, 1, :])
                    logit("l0y", 0, 1, job("qk0a")[:, 2 * P:4 * P], bias[:, 0, :])
                    p("qk0b")
                    logit("l0b", 0, slice(2, 4), pairs("qk0b"), bias[:, 0:1, :].to_broadcast([P, 2, 2 * P]))
                    maxes(0, 0, "l0b")
                    for j in range(2):
                        p(f"qm{'ab'[j]}")
                        dve.tensor_reduce(out=stat[:, 3, 3, 2 * j:2 * j + 2], in_=pairs(f"qm{'ab'[j]}"), axis=AX, op=ALU.max).then_inc(*V.mark(f"mxm{'ab'[j]}"))
                    me("mxmb")
                    dve.tensor_scalar(out=stat[:, 3, 0, :], in0=stat[:, 3, 3, :], scalar1=-SCALE, scalar2=None, op0=ALU.mult).then_inc(*V.mark("nmm"))
                    v_tokens(1, 9)
                    softmax_scale(0, "0", 0)
                    lse(0)
                    softmax_scale(3, "m", 1)
                    a("sq")
                    dve.scalar_tensor_tensor(out=ht[:, :], in0=job("ho")[:, :], scalar=cols[:, head_col(32)], in1=hg[:, :],
                                             op0=ALU.mult, op1=ALU.mult).then_inc(*V.mark("ho1"))
                    p("pmc")
                    p("pv1", 1)
                    dve.tensor_copy(ptc[0][:, :], job("pmc")[:, :]).then_inc(*V.mark("cmc"))
                    p("p0c")
                    p("pv2", 1)
                    dve.tensor_copy(ptc[1][:, :], job("p0c")[:, :]).then_inc(*V.mark("c0c"))
                    a("rs")
                    dve.reciprocal(hrs[:, :], hrs[:, :]).then_inc(*V.mark("rrs"))
                    me("rrs")
                    tt("hout", branch[:, head_col(NH), :].rearrange("p a t -> p (a t)"), ht[:, :], hrs[:, :], ALU.mult)
                    v_tokens(2, 12)
                    for g in (1, 2):
                        i = g - 1
                        dve.wait_ge(edge_in[g], edge_value(g, hf, h))
                        p("p0c" if g == 1 else "pmc")
                        for j in range(2):
                            p(f"qk{g}{'ab'[j]}")
                            logit(f"l{g}{'ab'[j]}", g, slice(2 * j, 2 * j + 2), pairs(f"qk{g}{'ab'[j]}"), bias[:, g + 1:g + 2, :].to_broadcast([P, 2, 2 * P]))
                        maxes(g, i, f"l{g}b")
                        softmax_scale(g, str(g), i)
                        lse(g)
                        p(f"p{g}c")
                        dve.tensor_copy(ptc[i][:, :], job(f"p{g}c")[:, :]).then_inc(*V.mark(f"c{g}c"))
                    a("lbc2")
                    tt("m1", mmax[:, :], lseb[:, 0, :], lseb[:, 1, :], ALU.max)
                    me("m1")
                    tt("m2", mmax[:, :], mmax[:, :], lseb[:, 2, :], ALU.max)
                    me("m2")
                    tt("md", lseb[:, :, :], lseb[:, :, :], mmax[:, :].unsqueeze(1).to_broadcast([P, G, HALF]), ALU.subtract)
                    a("me")
                    tt("e1", msum[:, :], lseb[:, 0, :], lseb[:, 1, :], ALU.add)
                    me("e1")
                    tt("e2", msum[:, :], msum[:, :], lseb[:, 2, :], ALU.add)
                    me("e2")
                    dve.reciprocal(msum[:, :], msum[:, :]).then_inc(*V.mark("er"))
                    tt("ew", og[:, :, :], og[:, :, :], lseb[:, :, :], ALU.mult)
                    me("ew")
                    tt("ea1", og[:, 0, :], og[:, 0, :], og[:, 1, :], ALU.add)
                    me("ea1")
                    tt("ea2", og[:, 0, :], og[:, 0, :], og[:, 2, :], ALU.add)
                    me("ea2")
                    tt("eo", branch[:, head_col(0), :].rearrange("p a t -> p (a t)"), og[:, 0, :], msum[:, :], ALU.mult)
                cross(dve, boundary(hf, 1))

                dve.tensor_copy(o_hi[:, :, :], branch[:, :, :]).then_inc(o_split, 1)
                dve.wait_ge(o_split, 2 * hf + 1)
                dve.tensor_tensor(out=o_lo[:, :, :], in0=branch[:, :, :], in1=o_hi[:, :, :].bitcast(F32), op=ALU.subtract).then_inc(o_split, 1)
                with dve.Fori(0, KD) as j:
                    it = KD * hf + j

                    def m(name):
                        dve.wait_ge(MV.sem, MV.after(name, it))

                    for b in range(3):
                        if hf == 1:
                            e_rows(2 * b, 2 * b + 2, E_MID // E_ROWS * j, E_MID * j)
                        dve.wait_ge(MA.sem, MA.after(f"s{b}", it))
                        dve.wait_ge(MP.sem, MP.after(f"B{b}", it))
                        if b == 0:
                            dve.wait_ge(MV.sem, MV.after("lo", it - 1))
                        dve.tensor_tensor(out=macc[:, min(b, 1), :], in0=ps[1][:, :], in1=sgate[:, b, :], op=ALU.mult).then_inc(*MV.mark(f"g{b}"))
                        if b:
                            m(f"g{b}")
                            dve.tensor_tensor(out=macc[:, 0, :], in0=macc[:, 0, :], in1=macc[:, 1, :], op=ALU.add).then_inc(*MV.mark(f"a{b}"))
                            m(f"a{b}")
                    if hf == 1:
                        e_rows(6, 8, E_MID // E_ROWS * j, E_MID * j)
                    mh = m_hi[:, bass.ds(j, 1), :].rearrange("p a t -> p (a t)")
                    ml = m_lo[:, bass.ds(j, 1), :].rearrange("p a t -> p (a t)")
                    dve.tensor_copy(mh, macc[:, 0, :]).then_inc(*MV.mark("hi"))
                    m("hi")
                    dve.tensor_tensor(out=ml, in0=macc[:, 0, :], in1=mh.bitcast(F32), op=ALU.subtract).then_inc(*MV.mark("lo"))
                cross(dve, boundary(hf, 2))

                dve.wait_ge(res_in, 48 * (hf + 1))
                with dve.Fori(0, KD // 2) as e:
                    it = KD // 2 * hf + e
                    for t in range(2):
                        if hf == 1:
                            e_rows(4 * t, 4 * t + 4, G_OUT + E_OUT // E_ROWS * e, E_ROWS * G_OUT + E_OUT * e)
                        dve.wait_ge(OP.sem, OP.after(f"T{t}", it))
                        r = res[:, :, bass.ds(2 * P * e + P * t, P)]
                        dve.scalar_tensor_tensor(out=r, in0=r, scalar=ALPHA, in1=ps[2 + t][:, :].rearrange("p (b c) -> p b c", b=NB),
                                                 op0=ALU.mult, op1=ALU.add).then_inc(*OV.mark(f"r{t}"))
                dve.wait_ge(OV.sem, OV.after("r1", KD // 2 * (hf + 1) - 1))
                for tb in range(NB):
                    norm(LV.mark, LV, hf, res[:, tb, :], bst, bmv, ln_g[:, :], ln_b[:, :],
                         lambda: dve.wait_ge(LA.sem, LA.after(f"sq{tb}", hf)), tag=str(tb))
                split_lo(2 * hf + 1)
                cross(dve, boundary(hf, 3))
                if hf == 1:
                    with dve.Fori(0, PH // 2) as e:
                        e_rows(0, E_PQ, G_PQ + E_PQ // E_ROWS * e, E_ROWS * G_PQ + E_PQ * e)
                    e_gates()
                cross(dve, boundary(hf, 4))

                dve.wait_ge(tk_in, 32 * hf + 32)
                with dve.Fori(0, NB) as tb:
                    it = NB * hf + tb

                    def m(name):
                        dve.wait_ge(TK.sem, TK.after(name, it))
                        apart(dve)

                    for q in range(4):
                        dve.wait_ge(TP.sem, TP.after(f"s{q}", it))
                        apart(dve)
                        sc = [ps[2 + q][:, P * n:P * n + P] for n in range(4)]
                        for n in range(4):
                            last = dve.max(out=vals[:, 4 * q + n, 0:8], in_=sc[n])
                        last.then_inc(*TK.mark(f"max{q}"))
                        m(f"max{q}")
                        for n in range(4):
                            last = dve.max_index(out=inds[:, 4 * q + n, 0:8], in_max=vals[:, 4 * q + n, 0:8], in_values=sc[n])
                        last.then_inc(*TK.mark(f"at{q}"))
                        for n in range(4):
                            last = dve.match_replace(out=left[:, n, :], in_to_replace=vals[:, 4 * q + n, 0:8], in_values=sc[n], imm_value=LOW)
                        last.then_inc(*TK.mark(f"rest{q}"))
                        m(f"rest{q}")
                        for n in range(4):
                            last = dve.max(out=vals[:, 4 * q + n, 8:16], in_=left[:, n, :])
                        last.then_inc(*TK.mark(f"max2{q}"))
                        m(f"max2{q}")
                        for n in range(4):
                            last = dve.max_index(out=inds[:, 4 * q + n, 8:16], in_max=vals[:, 4 * q + n, 8:16], in_values=left[:, n, :])
                        last.then_inc(*TK.mark(f"at2{q}"))
                    m("at23")
                    dve.tensor_copy(indf[:, :, :], inds[:, :, :]).then_inc(*TK.mark("indf"))
                    both = vals[:, :, :].rearrange("p (h t) k -> p h t k", t=2)
                    dve.tensor_tensor(out=cand[:, :, :, :], in0=both[:, :, 0, :].unsqueeze(3).to_broadcast([P, PH, TOPK, TOPK]),
                                      in1=both[:, :, 1, :].unsqueeze(2).to_broadcast([P, PH, TOPK, TOPK]), op=ALU.add).then_inc(*TK.mark("cand"))
                    m("cand")
                    c_h = [cand[:, n, :, :].rearrange("p a b -> p (a b)") for n in range(PH)]
                    for n in range(PH):
                        last = dve.max(out=best[:, n, 0:8], in_=c_h[n])
                    last.then_inc(*TK.mark("cmax"))
                    m("cmax")
                    for n in range(PH):
                        last = dve.max_index(out=pos[:, n, 0:8], in_max=best[:, n, 0:8], in_values=c_h[n])
                    last.then_inc(*TK.mark("cat"))
                    for n in range(PH):
                        last = dve.match_replace(out=cleft[:, n, :], in_to_replace=best[:, n, 0:8], in_values=c_h[n], imm_value=LOW)
                    last.then_inc(*TK.mark("crest"))
                    m("crest")
                    for n in range(PH):
                        last = dve.max(out=best[:, n, 8:16], in_=cleft[:, n, :])
                    last.then_inc(*TK.mark("cmax2"))
                    m("cmax2")
                    for n in range(PH):
                        last = dve.max_index(out=pos[:, n, 8:16], in_max=best[:, n, 8:16], in_values=cleft[:, n, :])
                    last.then_inc(*TK.mark("cat2"))
                    m("cat2")
                    flat = pos[:, :, :].rearrange("p h k -> p (h k)")
                    dve.tensor_scalar(out=posu[:, 0, :], in0=flat, scalar1=4, scalar2=None, op0=ALU.logical_shift_right).then_inc(*TK.mark("pos1"))
                    dve.tensor_scalar(out=posu[:, 1, :], in0=flat, scalar1=TOPK - 1, scalar2=None, op0=ALU.bitwise_and).then_inc(*TK.mark("pos2"))
                    m("pos2")
                    dve.tensor_copy(posf[:, :, :], posu[:, :, :]).then_inc(*TK.mark("posf"))
                    m("posf")
                    ind = indf[:, :, :].rearrange("p (h t) k -> p h t k", t=2)
                    for t in range(2):
                        dve.tensor_tensor(out=pick[:, :, :], in0=iota[:, :, :], in1=posf[:, t, :].unsqueeze(2).to_broadcast([P, SLOTS, TOPK]),
                                          op=ALU.is_equal).then_inc(*TK.mark(f"eq{t}"))
                        m(f"eq{t}")
                        pk = pick[:, :, :].rearrange("p (h k) c -> p h k c", h=PH)
                        dve.tensor_tensor(out=pk, in0=pk, in1=ind[:, :, t, :].unsqueeze(2).to_broadcast([P, PH, TOPK, TOPK]),
                                          op=ALU.mult).then_inc(*TK.mark(f"in{t}"))
                        m(f"in{t}")
                        dve.tensor_reduce(out=got[:, t, :], in_=pick[:, :, :], axis=AX, op=ALU.add).then_inc(*TK.mark(f"got{t}"))
                        m(f"got{t}")
                    dve.wait_ge(tk_out, 32 * it + 32)
                    dve.scalar_tensor_tensor(out=idxu[:, :], in0=got[:, 0, :], scalar=float(P), in1=got[:, 1, :], op0=ALU.mult, op1=ALU.add).then_inc(*TK.mark("idx"))
                    dve.tensor_tensor(out=gex[:, :, :], in0=best[:, :, :], in1=best[:, :, 0:1].to_broadcast([P, PH, TOPK]), op=ALU.subtract).then_inc(*TK.mark("gsub"))
                    dve.wait_ge(TA.sem, TA.after("ex", it))
                    dve.tensor_reduce(out=gsm[:, 0, :], in_=gex[:, :, :], axis=AX, op=ALU.add).then_inc(*TK.mark("gsum"))
                    m("gsum")
                    dve.reciprocal(gsm[:, 1, :], gsm[:, 0, :]).then_inc(*TK.mark("grec"))
                    m("grec")
                    dve.tensor_tensor(out=gout[:, :].rearrange("p (h k) -> p h k", h=PH), in0=gex[:, :, :],
                                      in1=gsm[:, 1, :].unsqueeze(2).to_broadcast([P, PH, TOPK]), op=ALU.mult).then_inc(*TK.mark("gate"))
                dve.wait_ge(tk_out, 32 * NB * (hf + 1) + 32)
                cross(dve, boundary(hf, 5))

            def dot(i, o, q, r):
                tb = 2 * i + o
                dve.wait_ge(p_gelu, NBATCH * (tb - 1) + RING * q + r + 1)
                for s in range(BATCH):
                    dve.wait_ge(u_in[BATCH * r + s], 16 * (NBATCH // RING * (tb - 1) + q) + 16)
                    last = dve.tensor_tensor_reduce(out=u_ring[:, BATCH * r + s, :], in0=u_ring[:, BATCH * r + s, :], in1=h1[o][:, :], scale=1.0,
                                                    scalar=0.0, op0=ALU.mult, op1=ALU.add, accum_out=dots[:, r, s:s + 1])
                last.then_inc(p_dots, 1)

            def coefficient(i, o, q, r):
                dve.wait_ge(p_gelu, RING + NBATCH * (2 * i + o - 1) + RING * q + r + 1)
                dve.tensor_tensor(out=coef[:, r, :], in0=gel[:, r, :], in1=pgate[o][:, bass.ds(BATCH * (RING * q + r), BATCH)],
                                  op=ALU.mult).then_inc(p_coef, 1)

            def finish(i, o):
                tb = 2 * i + o
                dve.wait_ge(FA.sem, FA.after("c1", tb))
                norm(FV.mark, FV, tb, res2[o][:, :], bst2, bmv2, g2[:, :], b2[:, :],
                     lambda: dve.wait_ge(FA.sem, FA.after("sq", tb)))

            def block_dots(i, o):
                dve.wait_ge(blk_in[o], 48 * (i + o))
                apart(dve)
                with dve.Fori(0, NBATCH // RING) as q:
                    dot(i, o, q, 0)
                    for r in range(1, RING):
                        dot(i, o, q, r)
                        coefficient(i, o, q, r - 1)
                    coefficient(i, o, q, RING - 1)
                finish(i, o)

            dve.wait_ge(par_in, 32)
            finish(0, 0)
            block_dots(0, 1)
            with dve.Fori(1, NHALF * NB // 2) as i:
                for o in range(2):
                    block_dots(i, o)


_INS = ["x", "mem", "w_in", "b_gate", "w_mem_kv", "rel_bias", "hgrn_lb", "hgrn_norm_w", "w_branch", "w_out",
        "ln1_g", "ln1_b", "w_peer_q", "peer_sub_keys", "peer_u", "peer_v", "ln2_g", "ln2_b"]


def kernel(**inputs):
    import concourse.bacc as bacc
    from concourse.bass_utils import run_bass_kernel_spmd

    nc = bacc.Bacc("TRN2", target_bir_lowering=False, num_devices=1)
    arrays = {f"in_{n}": np.ascontiguousarray(inputs[n]) for n in _INS}
    arrays |= {f"in_{n}": a for n, a in shape_constants().items()}
    aps = {n[3:]: nc.dram_tensor(n, a.shape, mybir.dt.from_np(a.dtype), kind="ExternalInput").ap() for n, a in arrays.items()}
    aps["out"] = nc.dram_tensor("out_0", (1, S, D), F32, kind="ExternalOutput").ap()
    layer(nc, aps)
    r = run_bass_kernel_spmd(nc, [arrays], core_ids=[0])
    return r.results[0]["out_0"]
```

```python
import math
from contextlib import ExitStack

import numpy as np

import concourse.bass as bass
from concourse import mybir

F32 = mybir.dt.float32
F32R = mybir.dt.float32r
U32 = mybir.dt.uint32
ALU = mybir.AluOpType
ACT = mybir.ActivationFunctionType
AX = mybir.AxisListType.X

P = 128
S = 1024
D = 1024
KD = D // P
HALF = 512
NHALF = S // HALF
NB = HALF // P
NH = 4
G = 3
DIL = (1, 4, 16)
MEM = 256
CH = 64
NCH = HALF // CH
PH = 8
TOPK = 16
SLOTS = PH * TOPK
ALPHA = 2.0 ** 0.25
EPS = 1e-5
SCALE = 128.0 ** -0.5
NEG = -1e30
LOW = -3e38
BUCKETS = 32
BUCKET_MAX_DIST = 2048

BATCH = 4
RING = 4
E_ROWS = 4
E_GROUPS = SLOTS // E_ROWS
E_MID, E_OUT, E_PQ = 8, 8, 8
NBATCH = SLOTS // BATCH
G_OUT = E_MID * (D // P) // E_ROWS
G_PQ = G_OUT + E_OUT * (D // P // 2) // E_ROWS

C_Q, C_K, C_V = 0, G * NH * P, 2 * G * NH * P
C_HG = 3 * G * NH * P
C_MQ = C_HG + 4 * NH * P
C_GATE = C_MQ + NH * P

HEAD_TILES = [("f", C_HG), ("i", C_HG + 512), ("hq", C_HG + 1024), ("g", C_HG + 1536), ("mq", C_MQ)]
for _g in range(G):
    HEAD_TILES += [(f"k{_g}", C_K + 512 * _g), (f"v{_g}", C_V + 512 * _g), (f"q{_g}", C_Q + 512 * _g)]
NT_HEAD = len(HEAD_TILES)
NT_MID = 6
T_MID = NH * NT_HEAD
T_OUT = T_MID + KD * NT_MID
T_PQ = T_OUT + KD
NT = T_PQ + 2 * PH


def bucket_constants():
    exact = BUCKETS // 2
    onehot = np.zeros((BUCKETS, G, 384), np.float32)
    mask = np.zeros((NH, G, 384), np.float32)
    for g, dil in enumerate(DIL):
        for y in range(384):
            delta = (255 if g < 2 else 63) - y
            if not 0 <= delta <= 128:
                mask[:, g, y] = NEG
            n = max(delta, 0) * dil
            large = exact + int(math.log(max(n, 1) / exact) / math.log(BUCKET_MAX_DIST / exact) * (BUCKETS - exact))
            onehot[n if n < exact else min(large, BUCKETS - 1), g, y] = 1.0
    return onehot, mask


def shape_constants():
    onehot, mask = bucket_constants()
    s, c = np.arange(P)[:, None], np.arange(P)[None, :]
    causal = ((s <= c) & (s // CH == c // CH)).astype(np.uint32)
    resets = (np.arange(HALF) % CH != 0).astype(np.float32)
    return {
        "c_ident": np.eye(P, dtype=np.float32),
        "c_onehot": onehot,
        "c_mask": mask,
        "c_causal": np.tile(causal, (1, NB)),
        "c_resets": np.tile(resets, (P, 1)),
        "c_mean": np.full((P, P), 1.0 / P, np.float32),
        "c_iota": np.tile(np.arange(TOPK, dtype=np.float32), (P, 1)),
    }


class Steps:

    def __init__(self, sem, names, seed=1):
        self.sem = sem
        self.seed = seed
        self.names = names
        self.n = len(names)
        self.at = {name: i + 1 for i, name in enumerate(names)}
        assert len(self.at) == self.n, "two steps of one name"
        self.emitted = 0

    def after(self, name, it):
        return (it + self.seed) * self.n + self.at[name]

    def mark(self, name):
        assert self.names[self.emitted % self.n] == name, (self.names[self.emitted % self.n], name)
        self.emitted += 1
        return self.sem, 1


class Tiles:
    pass


class Banks:

    def __init__(self, jobs, banks):
        self.bank = {j: banks[i % len(banks)] for i, j in enumerate(jobs)}
        self.before = {}
        for i, j in enumerate(jobs):
            mine = [k for k in jobs if self.bank[k] == self.bank[j]]
            n = mine.index(j)
            self.before[j] = (mine[n - 1], 0) if n else (mine[-1], 1)


PE_HEAD = """P:f P:i P:hq P:g P:mq Ti P:k0 P:v0 sc P:q0 Tkl Tv0 u0 u1 P:k1 qk0a qk0b qma qmb P:v1 ho
P:q1 Tv1 p0p p0c lb0 P:k2 pmp pmc pvm qk1a qk1b P:v2 pv0 ms P:q2 Tv2 qk2a qk2b
p1p p1c lb1 pv1 p2p p2c lb2 pv2""".split()
JOBS = [n for n in PE_HEAD if ":" not in n]

DVE_HEAD = """fa key gm scan d1 inat qe ke d2 kl scm qa vt0 s0 s1 s2 s3 s4 s5 s6 s7 s8
l0x l0y l0b mx0 mxma mxmb nmm vt1 rl0 pn0 lse0 ho1 rlm pnm c0c cmc l1a l1b mx1 vt2 rl1 pn1 lse1
rrs hout l2a l2b mx2 c1c rl2 pn2 lse2 c2c
m1 m2 md e1 e2 er ew ea1 ea2 eo""".split()
ACT_HEAD = """f i hq sg mq ln e1 e1n k0 e2 e3 kln q0 vn0 k1 x0_0 x0_1 x0_2 x0_3 ln0 xm_0 xm_1 xm_2 xm_3
sq q1 vn1 vmh c0p lbc0 k2 cmp ovm x1_0 x1_1 x1_2 x1_3 ln1 ov0 rs q2 vn2 c1p lbc1
x2_0 x2_1 x2_2 x2_3 ln2 ov1 c2p lbc2 ov2 me""".split()
TILE_EVAC = {"f": ("A", "f"), "i": ("A", "i"), "hq": ("A", "hq"), "g": ("V", "gm"), "mq": ("A", "mq")}
for _g in range(G):
    TILE_EVAC |= {f"k{_g}": ("A", f"k{_g}"), f"v{_g}": ("V", f"vt{_g}"), f"q{_g}": ("A", f"q{_g}")}
JOB_EVAC = {
    "Ti": ("V", "inat"), "sc": ("V", "scm"), "Tkl": ("A", "kln"), "u0": ("V", "s7"), "u1": ("V", "s8"),
    "Tv0": ("A", "vn0"), "Tv1": ("A", "vn1"), "Tv2": ("A", "vn2"),
    "qk0a": ("V", "l0y"), "qk0b": ("V", "l0b"), "qma": ("A", "xm_1"), "qmb": ("A", "xm_3"),
    "qk1a": ("V", "l1a"), "qk1b": ("V", "l1b"), "qk2a": ("V", "l2a"), "qk2b": ("V", "l2b"),
    "ho": ("V", "ho1"), "ms": ("A", "rs"), "pmp": ("A", "cmp"), "pmc": ("V", "cmc"), "pvm": ("A", "ovm"),
    "p0p": ("A", "c0p"), "p0c": ("V", "c0c"), "p1p": ("A", "c1p"), "p1c": ("V", "c1c"),
    "p2p": ("A", "c2p"), "p2c": ("V", "c2c"), "lb0": ("A", "lbc0"), "lb1": ("A", "lbc1"), "lb2": ("A", "lbc2"),
    "pv0": ("A", "ov0"), "pv1": ("A", "ov1"), "pv2": ("A", "ov2"),
}


def layer(nc, A):
    x_d, out_d = A["x"], A["out"]
    w_in = A["w_in"].rearrange("l (k p) c -> p (l k) c", p=P)
    w_br = A["w_branch"].rearrange("l b (k p) c -> p (l b) k c", p=P)
    w_out = A["w_out"].rearrange("l (k p) c -> p (l k) c", p=P)
    w_pq = A["w_peer_q"].rearrange("l (k p) c -> p (l k) c", p=P)
    w_kv = A["w_mem_kv"].rearrange("l (k p) c -> p (l k) c", p=P)
    u_tab = A["peer_u"].rearrange("l e d -> (l e) d")
    v_tab = A["peer_v"].rearrange("l e d -> (l e) d")

    def dram(name, shape, dt=F32):
        return nc.dram_tensor(name, shape, dt, kind="Internal").ap()

    bias_rows = dram("bias_rows", (G, NH, 384))
    bias_skew = dram("bias_skew", (G * NH, P, 384))
    bias_tabs = dram("bias_tabs", (2, G * NH, P, 2 * P))
    kspill = dram("kspill", (G, NH, P, HALF))
    vspill = dram("vspill", (G, NH, P, HALF))
    subkeys_t = dram("subkeys_t", (P, 2 * PH, P))
    qp_d = dram("qp_d", (NHALF, 2 * PH, P, HALF))
    h1_d = dram("h1_d", (NHALF * NB, P, D))
    idx_d = dram("idx_d", (NHALF * NB, P, SLOTS), U32)
    gate_d = dram("gate_d", (NHALF * NB, P, SLOTS))

    ctx = ExitStack()
    with ctx:
        def sem(name):
            return ctx.enter_context(nc.semaphore(name))

        base = (nc.sbuf_base + 31) // 32 * 32
        top = [base, base]
        where = {}

        def at(name, shape, dt=F32, offset=None):
            size = (int(np.prod(shape[1:])) * 4 + 31) // 32 * 32
            if offset is None:
                offset = top[0]
            top[0] = offset + size
            top[1] = max(top[1], top[0])
            assert name not in where
            where[name] = offset
            return nc.alloc_sbuf_tensor_at(name, list(shape), dt, offset=offset)

        def over(name, other, shape):
            return nc.alloc_sbuf_tensor_at(name, list(shape), F32, offset=where[other])

        ident = at("ident", [P, P])
        mean_m = at("mean_m", [P, P])
        causal = at("causal", [P, HALF], U32)
        resets = at("resets", [P, HALF])
        cols = at("cols", [P, 36])
        lbc = at("lbc", [P, 32])
        zero1 = at("zero1", [P, 1])
        aident = at("aident", [P, P])
        zer = at("zer", [P, P])
        state = at("state", [P, NH, P])
        km = at("km", [P, NH, MEM])
        vm = at("vm", [P, 2, NH * P])
        w_raw = [at(f"w_raw{i}", [P, KD, P]) for i in range(2)]
        w_hi = [at(f"w_hi{i}", [P, KD, P], F32R) for i in range(2)]
        w_lo = [at(f"w_lo{i}", [P, KD, P], F32R) for i in range(2)]
        x_hi = at("x_hi", [P, KD, HALF], F32R)
        x_lo = at("x_lo", [P, KD, HALF], F32R)
        r_br = top[0]
        branch = at("branch", [P, 3 * NH, HALF])
        r_head = top[0]
        q_t = at("q_t", [P, G, HALF])
        k_t = at("k_t", [P, G, HALF])
        qm_t = at("qm_t", [P, HALF])
        v_tmp = at("v_tmp", [P, HALF])
        v_n = at("v_n", [P, G, HALF])
        kp = [at(f"kp{g}", [P, P if g == 0 else HALF]) for g in range(G)]
        vp = [at(f"vp{g}", [P, P if g == 0 else HALF]) for g in range(G)]
        bias = at("bias", [P, 4, 2 * P])
        prob = [at(f"prob{i}", [P, NB, 2 * P]) for i in range(2)]
        ptp = [at(f"ptp{i}", [P, HALF]) for i in range(2)]
        ptc = [at(f"ptc{i}", [P, HALF]) for i in range(2)]
        hf_, hkey, hi_, hlf, ha, he1, he1n, he2, he3, hq, hg = [
            at(n, [P, HALF]) for n in "hf hkey hi hlf ha he1 he1n he2 he3 hq hg".split()]
        chain = at("chain", [P, NCH, P])
        inat = at("inat", [P, NB, P])
        kln = over("kln", "he1n", [P, NB, P])
        scm = at("scm", [P, HALF])
        hsq = over("hsq", "he1", [P, HALF])
        ht = over("ht", "he1n", [P, HALF])
        hrs = over("hrs", "he2", [P, HALF])
        og = at("og", [P, G, HALF])
        lseb = over("lseb", "hf", [P, G, HALF])
        mmax = over("mmax", "hlf", [P, HALF])
        msum = over("msum", "ha", [P, HALF])
        vmh = at("vmh", [P, 2, P])
        stat = at("stat", [P, 4, 4, NB])
        r_side = top[0]
        e_ring = at("e_ring", [P, E_ROWS, D])
        h1e = at("h1e", [P, D])
        pidxe = at("pidxe", [P, SLOTS], U32)
        pgatee = at("pgatee", [P, SLOTS])
        icole = at("icole", [P, 2, E_ROWS], U32)
        dotse = at("dotse", [P, 2, E_ROWS])
        coefe = at("coefe", [P, SLOTS])
        o_hi = at("o_hi", [P, 3 * NH, HALF], F32R, offset=r_head)
        o_lo = at("o_lo", [P, 3 * NH, HALF], F32R)
        m_hi = at("m_hi", [P, KD, HALF], F32R)
        m_lo = at("m_lo", [P, KD, HALF], F32R)
        sgate = at("sgate", [P, 3, HALF])
        assert top[0] <= r_side
        macc = at("macc", [P, 2, HALF], offset=r_br)
        r_ln = top[0]
        res = at("res", [P, NB, D], offset=r_head)
        qst = [at(f"qst{t}", [P, HALF]) for t in range(2)]
        r_top = top[0]
        ln_g = at("ln_g", [P, D], offset=r_ln)
        ln_b = at("ln_b", [P, D])
        mixt = at("mixt", [P, 2, HALF])
        bst = at("bst", [P, NB, 2, 6])
        bmv = at("bmv", [P, NB, 4])
        def topk_tiles(tag, offset):
            t = Tiles()
            t.skt = at("skt" + tag, [P, 2 * PH, P], offset=offset)
            t.qs = [at(f"qs{i}{tag}", [P, 4, P]) for i in range(2)]
            t.iota = at("iota" + tag, [P, TOPK])
            t.vals = at("vals" + tag, [P, 4, TOPK])
            t.inds = at("inds" + tag, [P, 4, TOPK], U32)
            t.indf = at("indf" + tag, [P, 4, TOPK])
            t.left = at("left" + tag, [P, 4, P])
            t.cand = at("cand" + tag, [P, 2, TOPK, TOPK])
            t.cleft = at("cleft" + tag, [P, 2, TOPK * TOPK])
            t.pick = over("pick" + tag, "cand" + tag, [P, 4 * TOPK, TOPK])
            t.best = at("best" + tag, [P, PH, TOPK])
            t.pos = at("pos" + tag, [P, PH, TOPK], U32)
            t.posu = at("posu" + tag, [P, 2, 2, TOPK], U32)
            t.posf = at("posf" + tag, [P, 2, 2, TOPK])
            t.got = at("got" + tag, [P, 2, 2, TOPK])
            t.idxu = at("idxu" + tag, [P, SLOTS], U32)
            t.gex = at("gex" + tag, [P, PH, TOPK])
            t.gsm = at("gsm" + tag, [P, 2, PH])
            t.gout = at("gout" + tag, [P, SLOTS])
            return t

        tk_tiles = [topk_tiles("_side", r_side), topk_tiles("_own", r_top)]
        diage = at("diage", [P, E_ROWS, P])

        onehot = at("onehot", [BUCKETS, G, 384], offset=r_head)
        maskr = at("maskr", [NH, G, 384])
        brow = at("brow", [NH, G, 384])
        rows36 = at("rows36", [36, P])
        tab = at("tab", [P, G * NH, 2 * P])
        relb = at("relb", [BUCKETS, G * NH])
        sk_n = at("sk_n", [P, 2 * PH, P])
        sk_t = at("sk_t", [P, 2 * PH, P])
        mem_n = at("mem_n", [P, 2, D])
        mem_t = at("mem_t", [P, KD, MEM])
        wkv = at("wkv", [P, KD, HALF])
        wvv = over("wvv", "x_hi", [P, KD, HALF])
        x_n = [at("x_n0", [P, NB, D], offset=r_side), at("x_n1", [P, NB, D], offset=r_top)]
        u_ring = at("u_ring", [P, RING * BATCH, D], offset=r_br - 2 * KD * HALF * 4)
        v_ring = at("v_ring", [P, RING * BATCH, D])
        h1 = [at(f"h1_{i}", [P, D]) for i in range(2)]
        pidx = [at(f"pidx{i}", [P, SLOTS], U32) for i in range(2)]
        pgate = [at(f"pgate{i}", [P, SLOTS]) for i in range(2)]
        icol = at("icol", [P, RING, BATCH], U32)
        dots = at("dots", [P, RING, BATCH])
        gel = at("gel", [P, RING, BATCH])
        coef = at("coef", [P, RING, BATCH])
        diag = at("diag", [P, RING, BATCH, P])
        res2 = [at(f"res2_{i}", [P, D]) for i in range(2)]
        g2 = at("g2", [P, D])
        b2 = at("b2", [P, D])
        bst2 = at("bst2", [P, 2, 6])
        bmv2 = at("bmv2", [P, 4])
        assert top[0] <= where["coefe"]

        ps = [ctx.enter_context(nc.psum_tensor(f"ps{i}", [P, HALF], F32)) for i in range(8)]
        PJ = [0, 1, 6]
        banks = Banks(JOBS, [2, 3, 4, 5])

        const_in = sem("const_in")
        setup_in, kv_in = sem("setup_in"), sem("kv_in")
        bias_out = sem("bias_out")
        setup_dma = sem("setup_dma")
        setup_pe, setup_act, setup_dve = sem("setup_pe"), sem("setup_act"), sem("setup_dve")
        w_landed = [sem(f"w_landed{i}") for i in range(2)]
        w_split = [sem(f"w_split{i}") for i in range(2)]
        w_used = [sem(f"w_used{i}") for i in range(2)]
        xn_in = sem("xn_in")
        stage = sem("stage")
        waited = sem("waited")
        PE = Steps(sem("pe_head"), PE_HEAD)
        V = Steps(sem("dve_head"), DVE_HEAD)
        AC = Steps(sem("act_head"), ACT_HEAD)
        BY = {"A": AC, "V": V}
        edge_in = [sem(f"edge_in{g}") for g in range(G)]
        spilled = [sem(f"spilled{g}") for g in range(G)]
        MP = Steps(sem("mid_pe"), "G0 B0 G1 B1 G2 B2".split())
        MA = Steps(sem("mid_act"), "s0 s1 s2".split())
        MV = Steps(sem("mid_dve"), "g0 g1 a1 g2 a2 hi lo".split())
        OP = Steps(sem("out_pe"), "O0 O1 T0 T1".split())
        OA = Steps(sem("out_act"), "c0 c1".split())
        OV = Steps(sem("out_dve"), "r0 r1".split())
        res_in = sem("res_in")
        LV = Steps(sem("ln_dve"), [f"st{tb}" for tb in range(NB)] + [f"ag{tb}" for tb in range(NB)] + ["ep", "rc"]
                   + [f"{n}{tb}" for n in ("nm", "sg", "sb") for tb in range(NB)])
        LA = Steps(sem("ln_act"), ["sq"])
        h1_out = sem("h1_out")
        XP = Steps(sem("xt_pe"), [f"t{k}" for k in range(KD)])
        XA = Steps(sem("xt_act"), [f"hi{k}" for k in range(KD)])
        XV = Steps(sem("xt_dve"), [f"lo{k}" for k in range(KD)])
        QP = Steps(sem("pq_pe"), "Q0 Q1".split())
        QA = Steps(sem("pq_act"), "c0 c1".split())
        TP = Steps(sem("topk_pe"), [f"s{q}" for q in range(4)])
        TA = Steps(sem("topk_act"), ["ex"])
        TK = Steps(sem("topk_dve"), [f"{n}{q}" for q in range(4) for n in
                   "max at rest max2 at2 indf cand cmax cat crest cmax2 cat2 pos1_ pos2_ posf eq in got idx gsub".split()]
                   + "gsum grec gate".split())
        qs_in = [sem(f"qs_in{i}") for i in range(2)]
        qp_out = [sem(f"qp_out{i}") for i in range(2)]
        o_split = sem("o_split")
        tk_in, tk_out = sem("tk_in"), sem("tk_out")
        e_blk = sem("e_blk")
        e_in = [sem(f"e_in{s}") for s in range(E_ROWS)]
        e_idx, e_moved = sem("e_idx"), sem("e_moved")
        e_dots, e_diag, e_acc = sem("e_dots"), sem("e_diag"), sem("e_acc")
        e_gelu, e_coef = sem("e_gelu"), sem("e_coef")
        p_dots, p_gelu, p_coef, p_diag, p_acc = (sem(n) for n in ("p_dots", "p_gelu", "p_coef", "p_diag", "p_acc"))
        p_idx = sem("p_idx")
        p_const = sem("p_const")
        par_in = sem("par_in")
        blk_in = [sem(f"blk_in{i}") for i in range(2)]
        u_in = [sem(f"u_in{i}") for i in range(RING * BATCH)]
        v_in = [sem(f"v_in{i}") for i in range(RING * BATCH)]
        p_close = sem("p_close")
        FA = Steps(sem("fin_act"), "c0 c1 sq".split(), seed=2)
        FV = Steps(sem("fin_dve"), "st ag ep rc nm sg sb".split())
        p_out = [sem(f"p_out{i}") for i in range(2)]

        block = ctx.enter_context(nc.Block())

        def psum_by_residue(t, dil):
            return t.rearrange("p (j r) -> p r j", r=dil)

        def grouped(t, dil):
            return t.rearrange("p (r j) -> p r j", r=dil)

        def apart(eng):
            eng.sem_inc(waited, 1)


        def cross(eng, n):
            eng.drain().then_inc(stage, 1)
            eng.wait_ge(stage, 3 * n)

        def edge_value(g, hf, h):
            per = 32 if g == 0 else 16
            return per * (h + 1) if hf == 0 else per * NH + (per + 32) * (h + 1)

        SETUP_DMAS = 16 * (2 + 2 * NH + 4 * NH + 3)

        def boundary(hf, k):
            return 2 + 6 * hf + k

        @block.sync
        def _(sp):
            sp.dma_start(ident[:, :], A["c_ident"]).then_inc(const_in, 16)
            sp.dma_start(onehot[:, :, :], A["c_onehot"]).then_inc(const_in, 16)
            sp.dma_start(maskr[:, :, :], A["c_mask"]).then_inc(const_in, 16)
            sp.dma_start(relb[:, :], A["rel_bias"]).then_inc(const_in, 16)
            sp.dma_start(rows36[0:24, :], A["b_gate"].rearrange("l (a p) -> (l a) p", p=P)).then_inc(const_in, 16)
            sp.dma_start(rows36[24:32, :], A["hgrn_lb"].rearrange("l (a p) -> (l a) p", p=P)).then_inc(const_in, 16)
            sp.dma_start(rows36[32:36, :], A["hgrn_norm_w"].rearrange("l (a p) -> (l a) p", p=P)).then_inc(const_in, 16)
            sp.dma_start(mean_m[:, :], A["c_mean"]).then_inc(const_in, 16)
            sp.dma_start(causal[:, :], A["c_causal"]).then_inc(const_in, 16)
            sp.dma_start(resets[:, :], A["c_resets"]).then_inc(const_in, 16)
            sp.dma_start(sk_n[:, :, :], A["peer_sub_keys"].rearrange("l h t n k -> n (l h t) k")).then_inc(setup_in, 16)
            sp.dma_start(mem_n[:, :, :], A["mem"].rearrange("b (m p) d -> p (b m) d", p=P)).then_inc(setup_in, 16)
            sp.dma_start(wkv[:, :, :], w_kv[:, :, 0:HALF]).then_inc(kv_in, 16)
            sp.dma_start(wvv[:, :, :], w_kv[:, :, HALF:2 * HALF]).then_inc(kv_in, 16)
            sp.dma_start(x_n[0][:, :, :], x_d[0, 0:HALF, :].rearrange("(b p) d -> p b d", p=P)).then_inc(xn_in, 16)
            sp.wait_ge(setup_dve, 2)
            sp.dma_start(bias_rows.rearrange("g h y -> h g y"), brow[:, :, :]).then_inc(setup_dma, 16)
            sp.wait_ge(setup_dma, 16)
            rep = bass.AP(tensor=bias_rows.tensor, offset=0, ap=[[384, G * NH], [0, P], [1, 384]])
            sp.dma_start(bias_skew, rep).then_inc(setup_dma, 16)
            sp.wait_ge(setup_dma, 32)
            n = 2
            with nc.allow_non_contiguous_dma(reason="rows of a diagonal-constant block"):
                for g in range(2):
                    for h in range(NH):
                        src = bass.AP(tensor=bias_skew.tensor, offset=(g * NH + h) * P * 384 + P - 1, ap=[[383, P], [1, 2 * P]])
                        sp.dma_start(tab[:, g * NH + h, :], src).then_inc(setup_dma, 16)
                        n += 1
                for h in range(NH):
                    for u in range(4):
                        src = bass.AP(tensor=bias_skew.tensor, offset=(2 * NH + h) * P * 384 + 31, ap=[[383, 32], [32, 2], [1, 32]])
                        dst = tab[32 * u:32 * u + 32, 2 * NH + h, :].rearrange("p (t k) -> p t k", t=2)[:, :, 32 * u:32 * u + 32]
                        sp.dma_start(dst, src).then_inc(setup_dma, 16)
                        n += 1
            sp.wait_ge(setup_dma, 16 * n)
            sp.dma_start(bias_tabs[1].rearrange("a p k -> p a k"), tab[:, :, :]).then_inc(setup_dma, 16)
            sp.wait_ge(setup_dma, 16 * n + 16)
            sp.sem_inc(bias_out, 1)
            sp.wait_ge(setup_dve, 9)
            sp.dma_start(bias_tabs[0].rearrange("a p k -> p a k"), tab[:, :, :]).then_inc(setup_dma, 16)
            sp.wait_ge(setup_act, 24)
            sp.dma_start(subkeys_t, sk_t[:, :, :]).then_inc(setup_dma, 16)
            assert SETUP_DMAS == 16 * n + 48
            sp.wait_ge(setup_dma, SETUP_DMAS)

            def weight(n, src, k=KD):
                b, half_n = n
                sp.wait_ge(w_split[b], 2 * half_n + 2)
                apart(sp)
                sp.dma_start(w_raw[b][:, 0:k, :], src).then_inc(w_landed[b], 16)

            def load_e_block():
                sp.dma_start(h1e[:, :], h1_d[0]).then_inc(e_blk, 16)
                sp.dma_start(pidxe[:, :], idx_d[0]).then_inc(e_blk, 16)
                sp.dma_start(pgatee[:, :], gate_d[0]).then_inc(e_blk, 16)

            def load_x(hf):
                sp.dma_start(x_n[hf][:, :, :], x_d[0, hf * HALF:(hf + 1) * HALF, :].rearrange("(b p) d -> p b d", p=P)).then_inc(xn_in, 16)

            def load_queries(hf, tb, q):
                it = NB * hf + tb
                sp.wait_ge(TP.sem, TP.after(f"s{(q - 2) % 4}", it - (q < 2)))
                apart(sp)
                sp.dma_start(tk_tiles[hf].qs[q % 2][:, :, :],
                             qp_d[hf, 4 * q:4 * q + 4, :, bass.ds(P * tb, P)].rearrange("a p t -> p a t")).then_inc(qs_in[q % 2], 16)

            def load_topk(hf):
                sp.dma_start(tk_tiles[hf].skt[:, :, :], subkeys_t).then_inc(tk_in, 16)
                sp.dma_start(tk_tiles[hf].iota[:, :], A["c_iota"]).then_inc(tk_in, 16)
                for t in range(2):
                    sp.wait_ge(qp_out[t], 16 * PH * (hf + 1) + 16)

            for hf in range(NHALF):
                t0 = hf * NT // 2
                sp.wait_ge(stage, 3 * (boundary(hf, 0) - 1))
                if hf == 1:
                    load_topk(0)
                with sp.Fori(0, NH) as h:
                    it = NH * hf + h
                    for t, (name, c0) in enumerate(HEAD_TILES):
                        if hf == 1 and t in (0, 1, 4, 7):
                            load_queries(0, h, (0, 1, 4, 7).index(t))
                        if name[0] == "k":
                            g = int(name[1])
                            sp.wait_ge(PE.sem, PE.after(f"pv{g}", it - 1))
                            apart(sp)
                            sp.wait_ge(V.sem, V.after(("l0b", "l1b", "l2b")[g], it - 1))
                            apart(sp)
                            if g == 0:
                                sp.dma_start(bias[:, 0, :], bias_tabs[1, bass.ds(h, 1)].rearrange("a p k -> (a p) k")).then_inc(edge_in[g], 16)
                            sp.dma_start(bias[:, g + 1, :], bias_tabs[hf, bass.ds(g * NH + h, 1)].rearrange("a p k -> (a p) k")).then_inc(edge_in[g], 16)
                            if hf == 1:
                                c = HALF - P if g == 0 else 0
                                sp.dma_start(kp[g][:, :], kspill[g, bass.ds(h, 1), :, c:HALF].rearrange("a p k -> (a p) k")).then_inc(edge_in[g], 16)
                                sp.dma_start(vp[g][:, :], vspill[g, bass.ds(h, 1), :, c:HALF].rearrange("a p k -> (a p) k")).then_inc(edge_in[g], 16)
                        weight((t % 2, t0 + NT_HEAD // 2 * h + t // 2), w_in[:, :, bass.ds(c0 + P * h, P)])
                if hf == 1:
                    sp.wait_ge(tk_out, 32 * NB + 32)
                    sp.wait_ge(stage, 3 * boundary(1, 1))
                    load_e_block()
                with sp.Fori(0, KD) as j:
                    for t in range(NT_MID):
                        b = t // 2
                        if t % 2 == 0:
                            src, k = w_in[:, :, bass.ds(C_GATE + b * D + P * j, P)], KD
                        else:
                            src, k = w_br[:, b, :, bass.ds(P * j, P)], NH
                        weight((t % 2, t0 + T_MID // 2 + NT_MID // 2 * j + t // 2), src, k)
                for t in range(2):
                    weight((t, t0 + T_OUT // 2), w_out[:, :, P * t:P * t + P])
                sp.wait_ge(stage, 3 * boundary(hf, 2))
                sp.dma_start(res[:, :, :], x_d[0, hf * HALF:(hf + 1) * HALF, :].rearrange("(b p) d -> p b d", p=P)).then_inc(res_in, 16)
                sp.dma_start(ln_g[:, :], A["ln1_g"].to_broadcast([P, D])).then_inc(res_in, 16)
                sp.dma_start(ln_b[:, :], A["ln1_b"].to_broadcast([P, D])).then_inc(res_in, 16)
                with sp.Fori(1, KD // 2) as e:
                    for t in range(2):
                        weight((t, t0 + T_OUT // 2 + e), w_out[:, :, bass.ds(2 * P * e + P * t, P)])
                with sp.Fori(0, PH) as e:
                    for t in range(2):
                        weight((t, t0 + T_PQ // 2 + e), w_pq[:, :, bass.ds(2 * P * e + P * t, P)])
                sp.wait_ge(stage, 3 * boundary(hf, 3))
                sp.dma_start(h1_d[NB * hf:NB * hf + NB].rearrange("b p d -> p b d"), res[:, :, :]).then_inc(h1_out, 16)
                sp.wait_ge(h1_out, 16 * (hf + 1))
                if hf == 0:
                    load_x(1)
                else:
                    sp.wait_ge(stage, 3 * boundary(1, 4))
                    load_topk(1)
                    with sp.Fori(0, NB) as tb:
                        for q in range(4):
                            load_queries(1, tb, q)
                    sp.wait_ge(tk_out, 32 * NB * 2 + 32)

            sp.wait_ge(stage, 3 * boundary(1, 5))
            sp.dma_start(g2[:, :], A["ln2_g"].to_broadcast([P, D])).then_inc(par_in, 16)
            sp.dma_start(b2[:, :], A["ln2_b"].to_broadcast([P, D])).then_inc(par_in, 16)

            def load_block(tb, o):
                sp.dma_start(h1[o][:, :], h1_d[bass.ds(tb, 1)].rearrange("a p d -> (a p) d")).then_inc(blk_in[o], 16)
                sp.dma_start(pidx[o][:, :], idx_d[bass.ds(tb, 1)].rearrange("a p d -> (a p) d")).then_inc(blk_in[o], 16)
                sp.dma_start(pgate[o][:, :], gate_d[bass.ds(tb, 1)].rearrange("a p d -> (a p) d")).then_inc(blk_in[o], 16)

            def store_block(tb, o):
                sp.wait_ge(FV.sem, FV.after("sb", tb))
                apart(sp)
                sp.dma_start(out_d[0, bass.ds(P * tb, P), :], res2[o][:, :]).then_inc(p_out[o], 16)

            NBLK = NHALF * NB
            load_block(1, 1)
            load_block(2, 0)
            store_block(0, 0)
            store_block(1, 1)
            load_block(3, 1)
            with sp.Fori(1, NBLK // 2 - 1) as i:
                for o in range(2):
                    store_block(2 * i + o, o)
                    load_block(2 * i + o + 2, o)
            for o in range(2):
                store_block(NBLK - 2 + o, o)
            for o in range(2):
                sp.wait_ge(p_out[o], 16 * (NBLK // 2) + 16)

        @block.gpsimd
        def _(pool):
            for b in range(2):
                pool.sem_inc(w_split[b], 2)
            pool.memset(zero1[:, :], 0.0).then_inc(p_const, 1)
            pool.wait_ge(p_const, 3)
            def split_lo_only(b, m, k=KD):
                pool.wait_ge(w_split[b], 2 * m + 3)
                pool.tensor_tensor(out=w_lo[b][:, 0:k, :], in0=w_raw[b][:, 0:k, :], in1=w_hi[b][:, 0:k, :].bitcast(F32),
                                   op=ALU.subtract).then_inc(w_split[b], 1)

            def split_hi_lo(b, m):
                pool.wait_ge(w_landed[b], 16 * m + 16)
                pool.wait_ge(w_used[b], m + 1)
                pool.tensor_tensor(out=w_hi[b][:, :, :], in0=w_raw[b][:, :, :],
                                   in1=zero1[:, :].unsqueeze(2).to_broadcast([P, KD, P]), op=ALU.add).then_inc(w_split[b], 1)
                split_lo_only(b, m)

            def gather_rows(first, last, group, slot, table, freed):
                for k in range(first, last):
                    s, r, g = k % E_ROWS, k // E_ROWS % 2, group + k // E_ROWS
                    pool.wait_ge(freed[0], E_ROWS * (g - freed[1]) + s + 1)
                    if s == 0:
                        pool.wait_ge(e_blk, 48)
                        pool.tensor_copy(icole[:, r, :], pidxe[:, bass.ds(slot + k, E_ROWS)]).then_inc(e_idx, 1)
                        pool.wait_ge(e_idx, g + 1)
                    apart(pool)
                    pool.indirect_dma_start(out=e_ring[:, s, :], out_offset=None, in_=table,
                                            in_offset=bass.IndirectOffsetOnAxis(ap=icole[:, r, s:s + 1], axis=0)).then_inc(e_in[s], 16)

            def u_rows(first, last, group, slot):
                gather_rows(first, last, group, slot, u_tab, (e_dots, 0))

            for hf in range(NHALF):
                t0 = hf * NT // 2
                with pool.Fori(0, NH) as h:
                    for t in range(NT_HEAD):
                        split_hi_lo(t % 2, t0 + NT_HEAD // 2 * h + t // 2)
                with pool.Fori(0, KD) as j:
                    for t in range(NT_MID):
                        split_lo_only(t % 2, t0 + T_MID // 2 + NT_MID // 2 * j + t // 2, KD if t % 2 == 0 else NH)
                        if hf == 1:
                            u_rows(E_MID * t // NT_MID, E_MID * (t + 1) // NT_MID, E_MID // E_ROWS * j, E_MID * j)
                with pool.Fori(0, KD // 2) as e:
                    for t in range(2):
                        split_lo_only(t, t0 + T_OUT // 2 + e)
                        if hf == 1:
                            u_rows(E_OUT * t // 2, E_OUT * (t + 1) // 2, G_OUT + E_OUT // E_ROWS * e, E_ROWS * G_OUT + E_OUT * e)
                with pool.Fori(0, PH // 2) as e:
                    for t in range(4):
                        split_lo_only(t % 2, t0 + T_PQ // 2 + 2 * e + t // 2)
                        if hf == 1:
                            u_rows(E_PQ * t // 4, E_PQ * (t + 1) // 4, G_PQ + E_PQ // E_ROWS * e, E_ROWS * G_PQ + E_PQ * e)
            pool.wait_ge(e_dots, E_ROWS + SLOTS)
            apart(pool)
            with pool.Fori(0, NB) as tb:
                gather_rows(0, SLOTS // NB, E_GROUPS + E_GROUPS // NB * tb, SLOTS // NB * tb, v_tab,
                            (e_acc, E_GROUPS))

            def rows(table, ring, landed, r):
                for s in range(BATCH):
                    pool.indirect_dma_start(
                        out=ring[:, BATCH * r + s, :], out_offset=None, in_=table,
                        in_offset=bass.IndirectOffsetOnAxis(ap=icol[:, r, s:s + 1], axis=0)).then_inc(landed[BATCH * r + s], 16)

            def block_rows(i, o):
                pool.wait_ge(blk_in[o], 48 * (i + o))
                apart(pool)
                with pool.Fori(0, NBATCH // RING) as q:
                    for r in range(RING):
                        b = NBATCH * (2 * i + o - 1) + RING * q + r
                        pool.wait_ge(p_acc, b + 1)
                        pool.tensor_copy(icol[:, r, :], pidx[o][:, bass.ds(BATCH * (RING * q + r), BATCH)]).then_inc(p_idx, 1)
                        pool.wait_ge(p_idx, b + 1)
                        pool.wait_ge(p_dots, b + 1)
                        apart(pool)
                        rows(u_tab, u_ring, u_in, r)
                        rows(v_tab, v_ring, v_in, r)

            block_rows(0, 1)
            with pool.Fori(1, NHALF * NB // 2) as i:
                for o in range(2):
                    block_rows(i, o)

        @block.tensor
        def _(pe):
            pe.sem_inc(PE.sem, PE.n)
            for st in (MP, OP, XP, QP, TP):
                pe.sem_inc(st.sem, st.n)
            pe.sem_inc(p_acc, RING)
            pe.sem_inc(w_used[0], 1)
            pe.sem_inc(e_acc, E_ROWS)
            pe.wait_ge(const_in, 160)
            pe.transpose(ps[0][:, 0:36], rows36[:, :], ident[0:36, 0:36]).then_inc(setup_pe, 1)
            for g in range(G):
                pe.matmul(ps[1 + g][0:NH, 0:384], relb[:, NH * g:NH * g + NH], onehot[:, g, :],
                          start=True, stop=True).then_inc(setup_pe, 1)
            pe.wait_ge(setup_in, 32)
            for q in range(4):
                if q >= 2:
                    pe.wait_ge(setup_act, 20 + q - 1)
                for j in range(4):
                    last = pe.transpose(ps[4 + q % 2][:, P * j:P * j + P], sk_n[:, 4 * q + j, :], ident[:, :])
                last.then_inc(setup_pe, 1)
            for q in range(4):
                if q >= 2:
                    pe.wait_ge(setup_act, 24 + q - 1)
                for j in range(4):
                    k, m = 2 * q + j // 2, j % 2
                    last = pe.transpose(ps[6 + q % 2][:, P * j:P * j + P], mem_n[:, m, P * k:P * k + P], ident[:, :])
                last.then_inc(setup_pe, 1)
            pe.wait_ge(setup_act, 28)
            pe.wait_ge(setup_dve, 1)
            pe.wait_ge(kv_in, 32)
            for h in range(NH):
                for k in range(KD):
                    last = pe.matmul(ps[h // 2][:, MEM * (h % 2):MEM * (h % 2) + MEM], wkv[:, k, P * h:P * h + P], mem_t[:, k, :],
                                     start=(k == 0), stop=(k == KD - 1))
            last.then_inc(setup_pe, 1)
            for m in range(2):
                for k in range(KD):
                    last = pe.matmul(ps[2 + m][:, :], mem_t[:, k, P * m:P * m + P], wvv[:, k, :],
                                     start=(k == 0), stop=(k == KD - 1))
            last.then_inc(setup_pe, 1)
            cross(pe, 1)

            def tile(n, hi, lo, k_n, out):
                b, m = n
                pe.wait_ge(w_split[b], 2 * m + 3)
                for k in range(k_n):
                    first = pe.matmul(out, w_hi[b][:, k, :], hi[:, k, :], start=(k == 0), stop=False)
                    if k == 0:
                        first.then_inc(w_used[1 - b], 1)
                    pe.matmul(out, w_hi[b][:, k, :], lo[:, k, :], start=False, stop=False)
                pe.wait_ge(w_split[b], 2 * m + 4)
                for k in range(k_n):
                    last = pe.matmul(out, w_lo[b][:, k, :], hi[:, k, :], start=False, stop=(k == k_n - 1))
                return last

            def transposes(out, blocks):
                for n, src in enumerate(blocks):
                    last = pe.transpose(out[:, P * n:P * n + P], src, ident[:, :])
                return last

            def transposed_half(src, it):
                for k in range(KD):
                    if k >= 4:
                        pe.wait_ge(XV.sem, XV.after(f"lo{k - 4}", it))
                    transposes(ps[2 + k % 4], [src[:, tb, P * k:P * k + P] for tb in range(NB)]).then_inc(*XP.mark(f"t{k}"))

            def scores_of(hf, tb, q, bank, emptied):
                tk, it = tk_tiles[hf], NB * hf + tb
                pe.wait_ge(tk_in, 32 * hf + 32)
                pe.wait_ge(qs_in[q % 2], 32 * it + 16 * (q // 2) + 16)
                pe.wait_ge(TK.sem, TK.after(*emptied))
                for n in range(4):
                    last = pe.matmul(ps[bank][:, P * n:P * n + P], tk.qs[q % 2][:, n, :], tk.skt[:, 4 * q + n, :], start=True, stop=True)
                last.then_inc(*TP.mark(f"s{q}"))

            for hf in range(NHALF):
                t0 = hf * NT // 2
                pe.wait_ge(xn_in, 16 + 16 * hf)
                transposed_half(x_n[hf], 2 * hf)
                cross(pe, boundary(hf, 0))

                with pe.Fori(0, NH) as h:
                    it = NH * hf + h

                    def a(name):
                        pe.wait_ge(AC.sem, AC.after(name, it))

                    def v(name):
                        pe.wait_ge(V.sem, V.after(name, it))

                    def bank(job):
                        before, back = banks.before[job]
                        by, step = JOB_EVAC[before]
                        pe.wait_ge(BY[by].sem, BY[by].after(step, it - back))
                        return ps[banks.bank[job]]

                    def project(t):
                        name, _ = HEAD_TILES[t]
                        n = len(PJ)
                        before = t - n if t >= n else max(u for u in range(NT_HEAD) if u % n == t % n)
                        by, step = TILE_EVAC[HEAD_TILES[before][0]]
                        pe.wait_ge(BY[by].sem, BY[by].after(step, it - (t < n)))
                        last = tile((t % 2, t0 + NT_HEAD // 2 * h + t // 2), x_hi, x_lo, KD, ps[PJ[t % len(PJ)]][:, :])
                        last.then_inc(*PE.mark("P:" + name))

                    def logits(g, part):
                        out = bank(f"qk{g}{'ab'[part]}")
                        if part == 0:
                            a(f"q{g}")
                            if hf == 1:
                                pe.wait_ge(edge_in[g], edge_value(g, hf, h))
                        for b in (2 * part, 2 * part + 1):
                            qb = q_t[:, g, P * b:P * b + P]
                            o = 2 * P * (b % 2)
                            if g == 0 and b > 0:
                                last = pe.matmul(out[:, o:o + 2 * P], qb, k_t[:, g, P * (b - 1):P * (b + 1)], start=True, stop=True)
                            else:
                                pk = kp[g][:, 0:P] if g == 0 else kp[g][:, P * b:P * b + P]
                                pe.matmul(out[:, o:o + P], qb, pk, start=True, stop=True)
                                last = pe.matmul(out[:, o + P:o + 2 * P], qb, k_t[:, g, P * b:P * b + P], start=True, stop=True)
                        last.then_inc(*PE.mark(f"qk{g}{'ab'[part]}"))

                    def prob_t(i, tag, part):
                        out = bank(f"p{tag}{'pc'[part]}")
                        transposes(out, [prob[i][:, b, P * part:P * part + P] for b in range(NB)]).then_inc(*PE.mark(f"p{tag}{'pc'[part]}"))

                    def values(g, i):
                        out = bank(f"pv{g}")
                        a(f"c{g}p")
                        v(f"c{g}c")
                        for b in range(NB):
                            if g == 0:
                                pv = v_n[:, g, P * (b - 1):P * b] if b else vp[g][:, :]
                            else:
                                pv = vp[g][:, P * b:P * b + P]
                            pe.matmul(out[:, P * b:P * b + P], pv, ptp[i][:, P * b:P * b + P], start=True, stop=False)
                            last = pe.matmul(out[:, P * b:P * b + P], v_n[:, g, P * b:P * b + P], ptc[i][:, P * b:P * b + P], start=False, stop=True)
                        last.then_inc(*PE.mark(f"pv{g}"))

                    def lse_rows(g):
                        out = bank(f"lb{g}")
                        v(f"lse{g}")
                        for b in range(NB):
                            last = pe.matmul(out[:, P * b:P * b + P], stat[:, g, 3, b:b + 1].to_broadcast([P, P]), ident[:, :],
                                             start=True, stop=True)
                        last.then_inc(*PE.mark(f"lb{g}"))

                    def v_blocks(g):
                        out = bank(f"Tv{g}")
                        v(f"vt{g}")
                        transposes(out, [v_tmp[:, P * b:P * b + P] for b in range(NB)]).then_inc(*PE.mark(f"Tv{g}"))

                    def scores(q):
                        if hf == 1:
                            scores_of(0, h, q, 7, (f"rest{(q - 1) % 4}", h - (q == 0)))

                    scores(0)
                    for t in range(5):
                        if t == 3:
                            scores(1)
                        project(t)
                    out = bank("Ti")
                    a("i")
                    transposes(out, [hi_[:, P * b:P * b + P] for b in range(NB)]).then_inc(*PE.mark("Ti"))
                    project(5)
                    project(6)
                    out = bank("sc")
                    v("ke")
                    for b in range(NB):
                        last = pe.matmul(out[:, P * b:P * b + P], he1n[:, P * b:P * b + P], he1[:, P * b:P * b + P], start=True, stop=True)
                    last.then_inc(*PE.mark("sc"))
                    scores(2)
                    project(7)
                    out = bank("Tkl")
                    v("kl")
                    transposes(out, [he2[:, P * b:P * b + P] for b in range(NB)]).then_inc(*PE.mark("Tkl"))
                    v_blocks(0)
                    a("kln")
                    v("inat")
                    for j in range(2):
                        out = bank(f"u{j}")
                        for n in range(4):
                            c = 2 * n + j
                            r0 = CH * j
                            last = pe.matmul(out[:, P * n:P * n + P], kln[r0:r0 + CH, c // 2, :], inat[r0:r0 + CH, c // 2, :], start=True, stop=True)
                        last.then_inc(*PE.mark(f"u{j}"))
                    project(8)
                    logits(0, 0)
                    logits(0, 1)
                    for j in range(2):
                        out = bank(f"qm{'ab'[j]}")
                        a("mq")
                        for n in range(2):
                            b = 2 * j + n
                            last = pe.matmul(out[:, MEM * n:MEM * n + MEM], qm_t[:, P * b:P * b + P],
                                             km[:, bass.ds(h, 1), :].rearrange("p a m -> p (a m)"), start=True, stop=True)
                        last.then_inc(*PE.mark(f"qm{'ab'[j]}"))
                    project(9)
                    out = bank("ho")
                    v("s7")
                    for b in range(NB):
                        pe.matmul(out[:, P * b:P * b + P], inat[:, b, :], scm[:, P * b:P * b + P], start=True, stop=False)
                        for c in (2 * b, 2 * b + 1):
                            last = pe.matmul(out[:, CH * c:CH * c + CH], chain[:, c, :], hq[:, CH * c:CH * c + CH], start=False, stop=(c % 2 == 1))
                    last.then_inc(*PE.mark("ho"))
                    scores(3)
                    project(10)
                    v_blocks(1)
                    v("pn0")
                    prob_t(0, "0", 0)
                    prob_t(0, "0", 1)
                    lse_rows(0)
                    project(11)
                    v("pnm")
                    prob_t(1, "m", 0)
                    prob_t(1, "m", 1)
                    out = bank("pvm")
                    a("cmp")
                    v("cmc")
                    pe.matmul(out[:, :], vmh[:, 0, :], ptp[0][:, :], start=True, stop=False)
                    pe.matmul(out[:, :], vmh[:, 1, :], ptc[0][:, :], start=False, stop=True).then_inc(*PE.mark("pvm"))
                    logits(1, 0)
                    logits(1, 1)
                    project(12)
                    values(0, 1)
                    out = bank("ms")
                    a("sq")
                    pe.matmul(out[:, :], mean_m[:, :], hsq[:, :], start=True, stop=True).then_inc(*PE.mark("ms"))
                    project(13)
                    v_blocks(2)
                    logits(2, 0)
                    logits(2, 1)
                    v("pn1")
                    prob_t(0, "1", 0)
                    prob_t(0, "1", 1)
                    lse_rows(1)
                    values(1, 0)
                    v("pn2")
                    prob_t(1, "2", 0)
                    prob_t(1, "2", 1)
                    lse_rows(2)
                    values(2, 1)
                cross(pe, boundary(hf, 1))

                with pe.Fori(0, KD) as j:
                    it = KD * hf + j
                    for t in range(NT_MID):
                        b, name = t // 2, f"{'GB'[t % 2]}{t // 2}"
                        n = (t % 2, t0 + T_MID // 2 + NT_MID // 2 * j + t // 2)
                        if t % 2 == 0:
                            pe.wait_ge(MA.sem, MA.after(f"s{(b - 1) % 3}", it - (b == 0)))
                            last = tile(n, x_hi, x_lo, KD, ps[0][:, :])
                        else:
                            pe.wait_ge(MV.sem, MV.after(f"g{(b - 1) % 3}", it - (b == 0)))
                            pe.wait_ge(o_split, 6 * hf + 2 * b + 2)
                            last = tile(n, o_hi[:, NH * b:NH * b + NH, :], o_lo[:, NH * b:NH * b + NH, :], NH, ps[1][:, :])
                        last.then_inc(*MP.mark(name))
                cross(pe, boundary(hf, 2))

                with pe.Fori(0, KD // 2) as e:
                    it = KD // 2 * hf + e
                    for t in range(2):
                        pe.wait_ge(OA.sem, OA.after(f"c{t}", it - 1))
                        tile((t, t0 + T_OUT // 2 + e), m_hi, m_lo, KD, ps[t][:, :]).then_inc(*OP.mark(f"O{t}"))
                    for t in range(2):
                        pe.wait_ge(OA.sem, OA.after(f"c{t}", it))
                        pe.wait_ge(OV.sem, OV.after(f"r{t}", it - 1))
                        transposes(ps[2 + t], [mixt[:, t, P * b:P * b + P] for b in range(NB)]).then_inc(*OP.mark(f"T{t}"))
                pe.wait_ge(LV.sem, LV.after(f"sb{NB - 1}", hf))
                transposed_half(res, 2 * hf + 1)
                cross(pe, boundary(hf, 3))

                with pe.Fori(0, PH // 2) as e2:
                    for e, t in ((2 * e2 + u, t) for u in range(2) for t in range(2)):
                        it = PH * hf + e
                        pe.wait_ge(QA.sem, QA.after(f"c{t}", it - 1))
                        tile((t, t0 + T_PQ // 2 + e), x_hi, x_lo, KD, ps[t][:, :]).then_inc(*QP.mark(f"Q{t}"))
                cross(pe, boundary(hf, 4))

                if hf == 1:
                    pe.wait_ge(e_blk, 48)
                    for c in range(2):
                        pe.matmul(ps[c][:, :], aident[:, :], h1e[:, HALF * c:HALF * c + HALF], start=True, stop=False)
                    with pe.Fori(0, NB) as tb:
                        for q in range(4):
                            for ahead in ((0, 1), (2,), (3,), ())[q]:
                                scores_of(1, tb, ahead, 2 + ahead, (f"rest{ahead}", NB + tb - 1))
                            n = SLOTS // NB // 4
                            for k in range(n * q, n * q + n):
                                s, g = k % E_ROWS, E_GROUPS // NB * tb + k // E_ROWS
                                pe.wait_ge(e_diag, E_ROWS * g + s + 1)
                                pe.wait_ge(e_in[s], 16 * (E_GROUPS + g) + 16)
                                for c in range(2):
                                    last = pe.matmul(ps[c][:, :], diage[:, s, :], e_ring[:, s, HALF * c:HALF * c + HALF], start=False, stop=False)
                                last.then_inc(e_acc, 1)
                    for c in range(2):
                        last = pe.matmul(ps[c][:, :], zer[:, :], h1e[:, HALF * c:HALF * c + HALF], start=False, stop=True)
                    last.then_inc(p_close, 1)
                cross(pe, boundary(hf, 5))

            def block_sum(i, o):
                tb = 2 * i + o
                acc = [ps[2 * o], ps[2 * o + 1]]
                pe.wait_ge(blk_in[o], 48 * (i + o))
                pe.wait_ge(FA.sem, FA.after("c1", tb - 2))
                for c in range(2):
                    pe.matmul(acc[c][:, :], aident[:, :], h1[o][:, HALF * c:HALF * c + HALF], start=True, stop=False)
                with pe.Fori(0, NBATCH // RING) as q:
                    for r in range(RING):
                        pe.wait_ge(p_diag, NBATCH * (tb - 1) + RING * q + r + 1)
                        for s in range(BATCH):
                            pe.wait_ge(v_in[BATCH * r + s], 16 * (NBATCH // RING * (tb - 1) + q) + 16)
                            for c in range(2):
                                last = pe.matmul(acc[c][:, :], diag[:, r, s, :], v_ring[:, BATCH * r + s, HALF * c:HALF * c + HALF],
                                                 start=False, stop=False)
                        last.then_inc(p_acc, 1)
                for c in range(2):
                    last = pe.matmul(acc[c][:, :], zer[:, :], h1[o][:, HALF * c:HALF * c + HALF], start=False, stop=True)
                last.then_inc(p_close, 1)

            block_sum(0, 1)
            with pe.Fori(1, NHALF * NB // 2) as i:
                for o in range(2):
                    block_sum(i, o)

        @block.scalar
        def _(act):
            act.sem_inc(AC.sem, AC.n)
            for st in (MA, OA, LA, XA, QA, TA):
                act.sem_inc(st.sem, st.n)
            act.sem_inc(FA.sem, FA.seed * FA.n)
            act.sem_inc(p_gelu, RING)
            for g in range(G):
                act.sem_inc(spilled[g], 32)
            for t in range(2):
                act.sem_inc(qp_out[t], 16)
            for o in range(2):
                act.sem_inc(p_out[o], 16)
            act.wait_ge(setup_pe, 1)
            act.activation(cols[:, :], ps[0][:, 0:36], ACT.Copy).then_inc(setup_act, 1)
            act.wait_ge(setup_dve, 4)
            act.activation(lbc[:, 8:16], lbc[:, 0:8], ACT.Exp).then_inc(setup_act, 1)
            act.wait_ge(setup_act, 2)
            act.sem_inc(setup_act, 18)
            for q in range(4):
                act.wait_ge(setup_pe, 5 + q)
                act.activation(sk_t[:, 4 * q:4 * q + 4, :].rearrange("p a n -> p (a n)"), ps[4 + q % 2][:, :], ACT.Copy).then_inc(setup_act, 1)
            for q in range(4):
                act.wait_ge(setup_pe, 9 + q)
                act.activation(mem_t[:, 2 * q:2 * q + 2, :].rearrange("p a m -> p (a m)"), ps[6 + q % 2][:, :], ACT.Copy).then_inc(setup_act, 1)
            act.wait_ge(setup_pe, 13)
            for j in range(2):
                act.activation(km[:, 2 * j:2 * j + 2, :].rearrange("p a m -> p (a m)"), ps[j][:, :], ACT.Copy).then_inc(setup_act, 1)
            act.wait_ge(setup_pe, 14)
            for m in range(2):
                act.activation(vm[:, m, :], ps[2 + m][:, :], ACT.Copy).then_inc(setup_act, 1)
            cross(act, 1)

            def split_hi(it):
                for k in range(KD):
                    act.wait_ge(XP.sem, XP.after(f"t{k}", it))
                    act.activation(x_hi[:, k, :], ps[2 + k % 4][:, :], ACT.Copy).then_inc(*XA.mark(f"hi{k}"))

            def weight_hi(b, m, k=KD):
                act.wait_ge(w_landed[b], 16 * m + 16)
                act.wait_ge(w_used[b], m + 1)
                act.activation(w_hi[b][:, 0:k, :], w_raw[b][:, 0:k, :], ACT.Copy).then_inc(w_split[b], 1)

            def gate_exps(hf, tb):
                act.wait_ge(TK.sem, TK.after("gsub3", NB * hf + tb))
                act.activation(tk_tiles[hf].gex[:, :, :], tk_tiles[hf].gex[:, :, :], ACT.Exp).then_inc(*TA.mark("ex"))

            def store_topk(hf, tb):
                it = NB * hf + tb
                act.wait_ge(TK.sem, TK.after("gate", it))
                apart(act)
                act.dma_start(idx_d[bass.ds(it, 1)].rearrange("a p k -> (a p) k"), tk_tiles[hf].idxu[:, :]).then_inc(tk_out, 16)
                act.dma_start(gate_d[bass.ds(it, 1)].rearrange("a p k -> (a p) k"), tk_tiles[hf].gout[:, :]).then_inc(tk_out, 16)

            def e_diags(first, last, tb):
                for k in range(first, last):
                    s = k % E_ROWS
                    act.wait_ge(e_acc, SLOTS // NB * tb + k + 1)
                    act.activation(diage[:, s, :], ident[:, :], ACT.Copy,
                                   scale=coefe[:, bass.ds(SLOTS // NB * tb + k, 1)]).then_inc(e_diag, 1)

            def e_gelus():
                act.wait_ge(e_moved, 2 + E_GROUPS)
                act.activation(coefe[:, :], coefe[:, :], ACT.Gelu).then_inc(e_gelu, 1)

            for hf in range(NHALF):
                t0 = hf * NT // 2
                split_hi(2 * hf)
                cross(act, boundary(hf, 0))
                with act.Fori(0, NH) as h:
                    it = NH * hf + h

                    def p(name, back=0):
                        act.wait_ge(PE.sem, PE.after(name, it - back))

                    def v(name, back=0):
                        act.wait_ge(V.sem, V.after(name, it - back))

                    def me(name):
                        act.wait_ge(AC.sem, AC.after(name, it))

                    def copy(step, out, in_, func=ACT.Copy, **kw):
                        return act.activation(out, in_, func, **kw).then_inc(*AC.mark(step))

                    def pj(t):
                        return ps[PJ[t % len(PJ)]][:, :]

                    def job(name):
                        return ps[banks.bank[name]]

                    def by_residue(step, buf, g, t, name):
                        p(name)
                        copy(step, grouped(buf[:, g, :], DIL[g]), psum_by_residue(pj(t), DIL[g]))

                    def exps(g, i, source, tag):
                        for b in range(NB):
                            act.activation(prob[i][:, b, :], source(b), ACT.Exp, bias=stat[:, g, 0, b:b + 1],
                                           scale=(SCALE if tag == "m" else 1.0), accum_out=stat[:, g, 1, b:b + 1]).then_inc(*AC.mark(f"x{tag}_{b}"))

                    def values_out(g):
                        p(f"pv{g}")
                        if g == 0:
                            v("eo", 1)
                        copy(f"ov{g}", psum_by_residue(og[:, g, :], DIL[g]), grouped(job(f"pv{g}")[:, :], DIL[g]))

                    def lse_out(g):
                        p(f"lb{g}")
                        copy(f"lbc{g}", psum_by_residue(lseb[:, g, :], DIL[g]), grouped(job(f"lb{g}")[:, :], DIL[g]))

                    def spill(g):
                        if hf == 0:
                            me(f"vn{g}")
                            act.dma_start(kspill[g, bass.ds(h, 1)].rearrange("a p k -> (a p) k"), k_t[:, g, :]).then_inc(spilled[g], 16)
                            act.dma_start(vspill[g, bass.ds(h, 1)].rearrange("a p k -> (a p) k"), v_n[:, g, :]).then_inc(spilled[g], 16)

                    def before_k(g):
                        if hf == 0:
                            act.wait_ge(spilled[g], 32 * h + 32)
                        p(f"qk{g}b", 1)

                    p("P:f")
                    v("ew", 1)
                    copy("f", hf_[:, :], pj(0), ACT.Sigmoid)
                    p("P:i")
                    p("Ti", 1)
                    copy("i", hi_[:, :], pj(1))
                    p("P:hq")
                    p("ho", 1)
                    copy("hq", hq[:, :], pj(2))
                    p("P:g")
                    v("ho1", 1)
                    copy("sg", hg[:, :], pj(3), ACT.Sigmoid)
                    p("P:mq")
                    p("qmb", 1)
                    copy("mq", qm_t[:, :], pj(4))
                    v("fa")
                    copy("ln", hlf[:, :], hf_[:, :], ACT.Ln)
                    v("d1")
                    p("sc", 1)
                    copy("e1", he1[:, :], hlf[:, :], ACT.Exp)
                    copy("e1n", he1n[:, :], hlf[:, :], ACT.Exp, scale=-1.0)
                    before_k(0)
                    by_residue("k0", k_t, 0, 5, "P:k0")
                    v("d2")
                    p("Tkl", 1)
                    copy("e2", he2[:, :], hf_[:, :], ACT.Exp)
                    v("s8", 1)
                    copy("e3", he3[:, :], ha[:, :], ACT.Exp)
                    p("Tkl")
                    p("u1", 1)
                    copy("kln", kln[:, :, :].rearrange("p b d -> p (b d)"), job("Tkl")[:, :])
                    by_residue("q0", q_t, 0, 7, "P:q0")
                    p("Tv0")
                    p("pv0", 1)
                    copy("vn0", v_n[:, 0, :], job("Tv0")[:, :])
                    spill(0)
                    before_k(1)
                    by_residue("k1", k_t, 1, 8, "P:k1")
                    v("mx0")
                    exps(0, 0, lambda b: prob[0][:, b, :], "0")
                    me("x0_3")
                    p("lb0", 1)
                    copy("ln0", stat[:, 0, 3, :], stat[:, 0, 1, :], ACT.Ln)
                    v("nmm")
                    p("qmb")
                    p("p2c", 1)
                    exps(3, 1, lambda b: job("qm" + "ab"[b // 2])[:, MEM * (b % 2):MEM * (b % 2) + MEM], "m")
                    p("ho")
                    p("ms", 1)
                    copy("sq", hsq[:, :], job("ho")[:, :], ACT.Square)
                    by_residue("q1", q_t, 1, 10, "P:q1")
                    p("Tv1")
                    p("pv1", 1)
                    copy("vn1", v_n[:, 1, :], job("Tv1")[:, :])
                    spill(1)
                    p("pvm", 1)
                    copy("vmh", vmh[:, :, :], vm[:, :, bass.ds(P * h, P)])
                    p("p0p")
                    p("pv2", 1)
                    copy("c0p", ptp[1][:, :], job("p0p")[:, :])
                    lse_out(0)
                    before_k(2)
                    by_residue("k2", k_t, 2, 11, "P:k2")
                    p("pmp")
                    p("pv1", 1)
                    copy("cmp", ptp[0][:, :], job("pmp")[:, :])
                    p("pvm")
                    copy("ovm", branch[:, bass.ds(2 * NH + h, 1), :].rearrange("p a t -> p (a t)"), job("pvm")[:, :])
                    v("mx1")
                    exps(1, 0, lambda b: prob[0][:, b, :], "1")
                    me("x1_3")
                    copy("ln1", stat[:, 1, 3, :], stat[:, 1, 1, :], ACT.Ln)
                    values_out(0)
                    p("ms")
                    v("hout", 1)
                    copy("rs", hrs[:, :], job("ms")[:, :], ACT.Sqrt, bias=EPS)
                    by_residue("q2", q_t, 2, 13, "P:q2")
                    p("Tv2")
                    copy("vn2", v_n[:, 2, :], job("Tv2")[:, :])
                    spill(2)
                    p("p1p")
                    p("pvm")
                    copy("c1p", ptp[0][:, :], job("p1p")[:, :])
                    lse_out(1)
                    v("mx2")
                    exps(2, 1, lambda b: prob[1][:, b, :], "2")
                    me("x2_3")
                    if hf == 1:
                        gate_exps(0, h)
                    copy("ln2", stat[:, 2, 3, :], stat[:, 2, 1, :], ACT.Ln)
                    values_out(1)
                    p("p2p")
                    copy("c2p", ptp[1][:, :], job("p2p")[:, :])
                    lse_out(2)
                    values_out(2)
                    v("md")
                    copy("me", lseb[:, :, :], lseb[:, :, :], ACT.Exp)
                    if hf == 1:
                        store_topk(0, h)
                if hf == 0:
                    for g in range(G):
                        act.wait_ge(spilled[g], 32 * NH + 32)
                cross(act, boundary(hf, 1))

                with act.Fori(0, KD) as j:
                    it = KD * hf + j
                    for b in range(3):
                        n = t0 + T_MID // 2 + NT_MID // 2 * j + b
                        weight_hi(0, n)
                        weight_hi(1, n, NH)
                        act.wait_ge(MP.sem, MP.after(f"G{b}", it))
                        act.wait_ge(MV.sem, MV.after(f"g{b}", it - 1))
                        act.activation(sgate[:, b, :], ps[0][:, :], ACT.Sigmoid,
                                       bias=cols[:, bass.ds(KD * b + j, 1)]).then_inc(*MA.mark(f"s{b}"))
                cross(act, boundary(hf, 2))

                with act.Fori(0, KD // 2) as e:
                    it = KD // 2 * hf + e
                    for t in range(2):
                        weight_hi(t, t0 + T_OUT // 2 + e)
                    for t in range(2):
                        act.wait_ge(OP.sem, OP.after(f"O{t}", it))
                        act.wait_ge(OP.sem, OP.after(f"T{t}", it - 1))
                        act.activation(mixt[:, t, :], ps[t][:, :], ACT.Copy).then_inc(*OA.mark(f"c{t}"))
                act.wait_ge(LV.sem, LV.after("ep", hf))
                act.activation(bmv[:, :, 3:4], bmv[:, :, 2:3], ACT.Sqrt).then_inc(*LA.mark("sq"))
                split_hi(2 * hf + 1)
                cross(act, boundary(hf, 3))

                def query(e, t):
                    it = PH * hf + e
                    act.wait_ge(QP.sem, QP.after(f"Q{t}", it))
                    act.wait_ge(qp_out[t], 16 * it + 16)
                    act.activation(qst[t][:, :], ps[t][:, :], ACT.Copy).then_inc(*QA.mark(f"c{t}"))
                    act.wait_ge(QA.sem, QA.after(f"c{t}", it))
                    apart(act)
                    act.dma_start(qp_d[hf, bass.ds(2 * e + t, 1)].rearrange("a p k -> (a p) k"), qst[t][:, :]).then_inc(qp_out[t], 16)

                weight_hi(0, t0 + T_PQ // 2)
                weight_hi(1, t0 + T_PQ // 2)
                query(0, 0)
                with act.Fori(1, PH) as e:
                    weight_hi(0, t0 + T_PQ // 2 + e)
                    query(e - 1, 1)
                    weight_hi(1, t0 + T_PQ // 2 + e)
                    query(e, 0)
                query(PH - 1, 1)
                if hf == 1:
                    e_gelus()
                cross(act, boundary(hf, 4))

                if hf == 1:
                    with act.Fori(0, NB) as tb:
                        e_diags(0, SLOTS // NB, tb)
                        gate_exps(1, tb)
                        store_topk(1, tb)
                cross(act, boundary(hf, 5))

            def diagonals(i, o, q, r):
                b = NBATCH * (2 * i + o - 1) + RING * q + r
                act.wait_ge(p_coef, b + 1)
                act.wait_ge(p_acc, b + 1)
                for s in range(BATCH):
                    last = act.activation(diag[:, r, s, :], ident[:, :], ACT.Copy, scale=coef[:, r, s:s + 1])
                last.then_inc(p_diag, 1)

            def finish(i, o):
                tb = 2 * i + o
                act.wait_ge(p_close, tb + 1)
                act.wait_ge(p_out[o], 16 * i + 16)
                for c in range(2):
                    act.activation(res2[o][:, HALF * c:HALF * c + HALF], ps[2 * o + c][:, :], ACT.Copy).then_inc(*FA.mark(f"c{c}"))
                act.wait_ge(FV.sem, FV.after("ep", tb))
                act.activation(bmv2[:, 3:4], bmv2[:, 2:3], ACT.Sqrt).then_inc(*FA.mark("sq"))

            def block_acts(i, o):
                with act.Fori(0, NBATCH // RING) as q:
                    for r in range(RING):
                        act.wait_ge(p_dots, RING + NBATCH * (2 * i + o - 1) + RING * q + r + 1)
                        act.activation(gel[:, r, :], dots[:, r, :], ACT.Gelu).then_inc(p_gelu, 1)
                        diagonals(i, o, q, r)
                finish(i, o)

            finish(0, 0)
            block_acts(0, 1)
            with act.Fori(1, NHALF * NB // 2) as i:
                for o in range(2):
                    block_acts(i, o)

        @block.vector
        def _(dve):
            dve.sem_inc(V.sem, V.n)
            for st in (MV, OV, LV, XV, TK, FV):
                dve.sem_inc(st.sem, st.n)
            dve.sem_inc(p_dots, RING)
            dve.sem_inc(tk_out, 32)
            dve.sem_inc(e_dots, E_ROWS)
            dve.sem_inc(e_moved, 2)
            dve.wait_ge(const_in, 160)
            dve.wait_ge(setup_pe, 4)
            for g in range(G):
                last = dve.tensor_tensor(out=brow[:, g, :], in0=ps[1 + g][0:NH, 0:384], in1=maskr[:, g, :], op=ALU.add)
            last.then_inc(setup_dve, 1)
            dve.memset(tab[:, 2 * NH:3 * NH, :], NEG).then_inc(setup_dve, 1)
            dve.wait_ge(setup_act, 1)
            dve.tensor_tensor(out=lbc[:, 16:20], in0=cols[:, 24:28], in1=cols[:, 28:32], op=ALU.max).then_inc(setup_dve, 1)
            dve.wait_ge(setup_dve, 3)
            for r in range(2):
                last = dve.tensor_tensor(out=lbc[:, 4 * r:4 * r + 4], in0=cols[:, 24 + 4 * r:28 + 4 * r], in1=lbc[:, 16:20], op=ALU.subtract)
            last.then_inc(setup_dve, 1)
            dve.wait_ge(setup_act, 2)
            dve.tensor_tensor(out=lbc[:, 20:24], in0=lbc[:, 8:12], in1=lbc[:, 12:16], op=ALU.add).then_inc(setup_dve, 1)
            dve.wait_ge(setup_dve, 5)
            dve.reciprocal(lbc[:, 20:24], lbc[:, 20:24]).then_inc(setup_dve, 1)
            dve.wait_ge(setup_dve, 6)
            dve.tensor_tensor(out=lbc[:, 24:28], in0=lbc[:, 8:12], in1=lbc[:, 20:24], op=ALU.mult).then_inc(setup_dve, 1)
            dve.tensor_tensor(out=lbc[:, 28:32], in0=lbc[:, 12:16], in1=lbc[:, 20:24], op=ALU.mult).then_inc(setup_dve, 1)
            dve.memset(state[:, :, :], 0.0)
            dve.tensor_scalar(out=aident[:, :], in0=ident[:, :], scalar1=ALPHA, scalar2=None, op0=ALU.mult).then_inc(p_const, 1)
            dve.memset(zer[:, :], 0.0).then_inc(p_const, 1)
            dve.wait_ge(bias_out, 1)
            dve.memset(tab[:, :, 0:P], NEG).then_inc(setup_dve, 1)
            dve.wait_ge(setup_dve, 9)
            dve.sem_inc(setup_dve, 1)
            cross(dve, 1)

            def split_lo(it):
                for k in range(KD):
                    dve.wait_ge(XA.sem, XA.after(f"hi{k}", it))
                    dve.tensor_tensor(out=x_lo[:, k, :], in0=ps[2 + k % 4][:, :], in1=x_hi[:, k, :].bitcast(F32),
                                      op=ALU.subtract).then_inc(*XV.mark(f"lo{k}"))

            def norm(mark, step, it, rows, stats, mv, gain, shift, sqrt_done):
                for c in range(2):
                    last = dve.bn_stats(out=stats[:, c, :], in_=rows[:, HALF * c:HALF * c + HALF])
                last.then_inc(*mark("st"))
                dve.wait_ge(step.sem, step.after("st", it))
                apart(dve)
                dve.bn_aggr(out=mv[:, 0:2], in_=stats[:, :, :]).then_inc(*mark("ag"))
                dve.wait_ge(step.sem, step.after("ag", it))
                dve.tensor_scalar(out=mv[:, 2:3], in0=mv[:, 1:2], scalar1=EPS, scalar2=None, op0=ALU.add).then_inc(*mark("ep"))
                sqrt_done()
                dve.reciprocal(mv[:, 3:4], mv[:, 3:4]).then_inc(*mark("rc"))
                dve.wait_ge(step.sem, step.after("rc", it))
                dve.tensor_scalar(out=rows, in0=rows, scalar1=mv[:, 0:1], scalar2=mv[:, 3:4], op0=ALU.subtract, op1=ALU.mult).then_inc(*mark("nm"))
                dve.wait_ge(step.sem, step.after("nm", it))
                dve.tensor_tensor(out=rows, in0=rows, in1=gain, op=ALU.mult).then_inc(*mark("sg"))
                dve.wait_ge(step.sem, step.after("sg", it))
                dve.tensor_tensor(out=rows, in0=rows, in1=shift, op=ALU.add).then_inc(*mark("sb"))

            def topk(hf, tb, q, part, bank):
                tk, it = tk_tiles[hf], NB * hf + tb

                def md(name):
                    dve.wait_ge(TK.sem, TK.after(f"{name}{q}", it))

                def m(name):
                    md(name)
                    apart(dve)

                def mark(name):
                    return TK.mark(f"{name}{q}")

                sc = [ps[bank][:, P * n:P * n + P] for n in range(4)]
                heads = slice(2 * q, 2 * q + 2)
                if part == 0:
                    dve.wait_ge(TP.sem, TP.after(f"s{q}", it))
                    apart(dve)
                    for n in range(4):
                        last = dve.max(out=tk.vals[:, n, 0:8], in_=sc[n])
                    last.then_inc(*mark("max"))
                    m("max")
                    for n in range(4):
                        last = dve.max_index(out=tk.inds[:, n, 0:8], in_max=tk.vals[:, n, 0:8], in_values=sc[n])
                    last.then_inc(*mark("at"))
                    for n in range(4):
                        last = dve.match_replace(out=tk.left[:, n, :], in_to_replace=tk.vals[:, n, 0:8], in_values=sc[n], imm_value=LOW)
                    last.then_inc(*mark("rest"))
                elif part == 1:
                    m("rest")
                    for n in range(4):
                        last = dve.max(out=tk.vals[:, n, 8:16], in_=tk.left[:, n, :])
                    last.then_inc(*mark("max2"))
                    m("max2")
                    for n in range(4):
                        last = dve.max_index(out=tk.inds[:, n, 8:16], in_max=tk.vals[:, n, 8:16], in_values=tk.left[:, n, :])
                    last.then_inc(*mark("at2"))
                    md("at2")
                    dve.tensor_copy(tk.indf[:, :, :], tk.inds[:, :, :]).then_inc(*mark("indf"))
                    both = tk.vals[:, :, :].rearrange("p (h t) k -> p h t k", t=2)
                    dve.tensor_tensor(out=tk.cand[:, :, :, :], in0=both[:, :, 0, :].unsqueeze(3).to_broadcast([P, 2, TOPK, TOPK]),
                                      in1=both[:, :, 1, :].unsqueeze(2).to_broadcast([P, 2, TOPK, TOPK]), op=ALU.add).then_inc(*mark("cand"))
                elif part == 2:
                    m("cand")
                    sums = [tk.cand[:, n, :, :].rearrange("p a b -> p (a b)") for n in range(2)]
                    for n in range(2):
                        last = dve.max(out=tk.best[:, 2 * q + n, 0:8], in_=sums[n])
                    last.then_inc(*mark("cmax"))
                    m("cmax")
                    for n in range(2):
                        last = dve.max_index(out=tk.pos[:, 2 * q + n, 0:8], in_max=tk.best[:, 2 * q + n, 0:8], in_values=sums[n])
                    last.then_inc(*mark("cat"))
                    for n in range(2):
                        last = dve.match_replace(out=tk.cleft[:, n, :], in_to_replace=tk.best[:, 2 * q + n, 0:8], in_values=sums[n], imm_value=LOW)
                    last.then_inc(*mark("crest"))
                    m("crest")
                    for n in range(2):
                        last = dve.max(out=tk.best[:, 2 * q + n, 8:16], in_=tk.cleft[:, n, :])
                    last.then_inc(*mark("cmax2"))
                    m("cmax2")
                    for n in range(2):
                        last = dve.max_index(out=tk.pos[:, 2 * q + n, 8:16], in_max=tk.best[:, 2 * q + n, 8:16], in_values=tk.cleft[:, n, :])
                    last.then_inc(*mark("cat2"))
                else:
                    md("cat2")
                    dve.tensor_scalar(out=tk.posu[:, :, 0, :], in0=tk.pos[:, heads, :], scalar1=4, scalar2=None, op0=ALU.logical_shift_right).then_inc(*mark("pos1_"))
                    dve.tensor_scalar(out=tk.posu[:, :, 1, :], in0=tk.pos[:, heads, :], scalar1=TOPK - 1, scalar2=None, op0=ALU.bitwise_and).then_inc(*mark("pos2_"))
                    md("pos2_")
                    dve.tensor_copy(tk.posf[:, :, :, :], tk.posu[:, :, :, :]).then_inc(*mark("posf"))
                    md("posf")
                    dve.tensor_tensor(out=tk.pick[:, :, :], in0=tk.iota[:, :].unsqueeze(1).to_broadcast([P, 4 * TOPK, TOPK]),
                                      in1=tk.posf[:, :, :, :].rearrange("p h t k -> p (h t k)").unsqueeze(2).to_broadcast([P, 4 * TOPK, TOPK]),
                                      op=ALU.is_equal).then_inc(*mark("eq"))
                    md("eq")
                    pk = tk.pick[:, :, :].rearrange("p (m k) c -> p m k c", m=4)
                    dve.tensor_tensor(out=pk, in0=pk, in1=tk.indf[:, :, :].unsqueeze(2).to_broadcast([P, 4, TOPK, TOPK]),
                                      op=ALU.mult).then_inc(*mark("in"))
                    md("in")
                    dve.tensor_reduce(out=tk.got[:, :, :, :].rearrange("p h t k -> p (h t k)"), in_=tk.pick[:, :, :], axis=AX, op=ALU.add).then_inc(*mark("got"))
                    md("got")
                    if q == 0:
                        dve.wait_ge(tk_out, 32 * it + 32)
                    dve.scalar_tensor_tensor(out=tk.idxu[:, 2 * TOPK * q:2 * TOPK * (q + 1)].rearrange("p (h k) -> p h k", h=2),
                                             in0=tk.got[:, :, 0, :], scalar=float(P), in1=tk.got[:, :, 1, :],
                                             op0=ALU.mult, op1=ALU.add).then_inc(*mark("idx"))
                    dve.tensor_tensor(out=tk.gex[:, heads, :], in0=tk.best[:, heads, :],
                                      in1=tk.best[:, heads, 0:1].to_broadcast([P, 2, TOPK]), op=ALU.subtract).then_inc(*mark("gsub"))

            def topk_gates(hf, tb):
                tk, it = tk_tiles[hf], NB * hf + tb
                dve.wait_ge(TA.sem, TA.after("ex", it))
                dve.tensor_reduce(out=tk.gsm[:, 0, :], in_=tk.gex[:, :, :], axis=AX, op=ALU.add).then_inc(*TK.mark("gsum"))
                dve.wait_ge(TK.sem, TK.after("gsum", it))
                dve.reciprocal(tk.gsm[:, 1, :], tk.gsm[:, 0, :]).then_inc(*TK.mark("grec"))
                dve.wait_ge(TK.sem, TK.after("grec", it))
                dve.tensor_tensor(out=tk.gout[:, :].rearrange("p (h k) -> p h k", h=PH), in0=tk.gex[:, :, :],
                                  in1=tk.gsm[:, 1, :].unsqueeze(2).to_broadcast([P, PH, TOPK]), op=ALU.mult).then_inc(*TK.mark("gate"))

            def e_rows(first, last, group, slot):
                for k in range(first, last):
                    s, r, g = k % E_ROWS, k // E_ROWS % 2, group + k // E_ROWS
                    if s == 0:
                        dve.wait_ge(e_blk, 48)
                        dve.wait_ge(e_moved, g + 1)
                    dve.wait_ge(e_in[s], 16 * g + 16)
                    dve.tensor_tensor_reduce(out=e_ring[:, s, :], in0=e_ring[:, s, :], in1=h1e[:, :], scale=1.0, scalar=0.0,
                                             op0=ALU.mult, op1=ALU.add, accum_out=dotse[:, r, s:s + 1]).then_inc(e_dots, 1)
                    if s == E_ROWS - 1:
                        dve.wait_ge(e_dots, E_ROWS * g + 2 * E_ROWS)
                        dve.tensor_copy(coefe[:, bass.ds(slot + k - s, E_ROWS)], dotse[:, r, :]).then_inc(e_moved, 1)

            def e_gates():
                dve.wait_ge(e_gelu, 1)
                dve.tensor_tensor(out=coefe[:, :], in0=coefe[:, :], in1=pgatee[:, :], op=ALU.mult).then_inc(e_coef, 1)

            for hf in range(NHALF):
                split_lo(2 * hf)
                if hf == 0:
                    dve.wait_ge(setup_dma, SETUP_DMAS)
                cross(dve, boundary(hf, 0))
                if hf == 0:
                    dve.memset(scm[:, :], 0.0)
                    for g in range(G):
                        dve.memset(kp[g][:, :], 0.0)
                        dve.memset(vp[g][:, :], 0.0)
                else:
                    dve.memset(scm[:, :], 0.0)
                with dve.Fori(0, NH) as h:
                    it = NH * hf + h

                    def a(name, back=0):
                        dve.wait_ge(AC.sem, AC.after(name, it - back))

                    def p(name, back=0):
                        dve.wait_ge(PE.sem, PE.after(name, it - back))

                    def me(name):
                        dve.wait_ge(V.sem, V.after(name, it))

                    def job(name):
                        return ps[banks.bank[name]]

                    def tt(step, out, in0, in1, op):
                        dve.tensor_tensor(out=out, in0=in0, in1=in1, op=op).then_inc(*V.mark(step))

                    def chunks(t):
                        return t[:, :].rearrange("p (c n) -> p c n", n=CH)

                    def at_chunk(t, n):
                        return chunks(t)[:, :, n:n + 1].to_broadcast([P, NCH, CH])

                    def pairs(name):
                        return job(name)[:, :].rearrange("p (b k) -> p b k", b=2)

                    def logit(step, g, blocks, src, table):
                        dve.scalar_tensor_tensor(out=prob[1 if g == 2 else 0][:, blocks, :],
                                                 in0=src, scalar=SCALE, in1=table, op0=ALU.mult, op1=ALU.add).then_inc(*V.mark(step))

                    def softmax_scale(g, tag, i):
                        a(f"x{tag}_3")
                        dve.reciprocal(stat[:, g, 2, :], stat[:, g, 1, :]).then_inc(*V.mark("rl" + tag))
                        me("rl" + tag)
                        tt("pn" + tag, prob[i][:, :, :], prob[i][:, :, :],
                           stat[:, g, 2, :].unsqueeze(2).to_broadcast([P, NB, 2 * P]), ALU.mult)

                    def lse(g):
                        a(f"ln{g}")
                        tt(f"lse{g}", stat[:, g, 3, :], stat[:, g, 3, :], stat[:, g, 0, :], ALU.subtract)

                    def maxes(g, i, last):
                        me(last)
                        dve.tensor_reduce(out=stat[:, g, 0, :], in_=prob[i][:, :, :], axis=AX, op=ALU.max, negate=True).then_inc(*V.mark(f"mx{g}"))

                    def v_tokens(g, t):
                        p(f"P:v{g}")
                        p(f"Tv{g - 1}") if g else p(f"Tv{G - 1}", 1)
                        dve.tensor_copy(grouped(v_tmp[:, :], DIL[g]), psum_by_residue(ps[PJ[t % len(PJ)]][:, :], DIL[g])).then_inc(*V.mark(f"vt{g}"))

                    def beside(n):
                        if hf == 1:
                            topk(0, h, n // 4, n % 4, 7)

                    def head_col(c0):
                        return bass.ds(c0 + h, 1)

                    a("f")
                    dve.tensor_scalar(out=hf_[:, :], in0=hf_[:, :], scalar1=lbc[:, head_col(28)], scalar2=lbc[:, head_col(24)],
                                      op0=ALU.mult, op1=ALU.add).then_inc(*V.mark("fa"))
                    beside(0)
                    beside(1)
                    me("fa")
                    dve.tensor_scalar(out=hkey[:, :], in0=hf_[:, :], scalar1=-1.0, scalar2=1.0, op0=ALU.mult, op1=ALU.add).then_inc(*V.mark("key"))
                    a("sg")
                    tt("gm", hg[:, :], ps[PJ[3 % len(PJ)]][:, :], hg[:, :], ALU.mult)
                    beside(2)
                    beside(3)
                    a("ln")
                    a("e3", 1)
                    dve.tensor_tensor_scan(out=ha[:, :], data0=resets[:, :], data1=hlf[:, :], initial=0.0, op0=ALU.mult, op1=ALU.add).then_inc(*V.mark("scan"))
                    me("scan")
                    tt("d1", chunks(hlf), chunks(ha), at_chunk(ha, CH // 2 - 1), ALU.subtract)
                    p("Ti")
                    p("ho", 1)
                    dve.tensor_copy(inat[:, :, :].rearrange("p b d -> p (b d)"), job("Ti")[:, :]).then_inc(*V.mark("inat"))
                    a("e1n")
                    tt("qe", he1[:, :], hq[:, :], he1[:, :], ALU.mult)
                    tt("ke", he1n[:, :], hkey[:, :], he1n[:, :], ALU.mult)
                    tt("d2", chunks(hf_), at_chunk(ha, CH - 1), chunks(ha), ALU.subtract)
                    beside(4)
                    a("e2")
                    tt("kl", he2[:, :], hkey[:, :], he2[:, :], ALU.mult)
                    p("sc")
                    apart(dve)
                    dve.copy_predicated(scm[:, :], causal[:, :], job("sc")[:, :]).then_inc(*V.mark("scm"))
                    beside(5)
                    a("e3")
                    me("qe")
                    tt("qa", hq[:, :], hq[:, :], he3[:, :], ALU.mult)
                    v_tokens(0, 6)
                    beside(6)
                    dve.tensor_copy(chain[:, 0, :], state[:, head_col(0), :].rearrange("p a d -> p (a d)")).then_inc(*V.mark("s0"))
                    for c in range(NCH):
                        me(f"s{c}")
                        if c < 2:
                            p(f"u{c}")
                        out = chain[:, c + 1, :] if c < NCH - 1 else state[:, head_col(0), :].rearrange("p a d -> p (a d)")
                        dve.scalar_tensor_tensor(out=out, in0=chain[:, c, :], scalar=he3[:, CH * c + CH - 1:CH * c + CH],
                                                 in1=job(f"u{c % 2}")[:, P * (c // 2):P * (c // 2) + P], op0=ALU.mult, op1=ALU.add).then_inc(*V.mark(f"s{c + 1}"))
                    beside(7)
                    dve.wait_ge(edge_in[0], edge_value(0, hf, h))
                    p("qk0a")
                    p("p1c", 1)
                    logit("l0x", 0, 0, job("qk0a")[:, 0:2 * P], bias[:, 1, :])
                    logit("l0y", 0, 1, job("qk0a")[:, 2 * P:4 * P], bias[:, 0, :])
                    p("qk0b")
                    logit("l0b", 0, slice(2, 4), pairs("qk0b"), bias[:, 0:1, :].to_broadcast([P, 2, 2 * P]))
                    beside(8)
                    maxes(0, 0, "l0b")
                    for j in range(2):
                        p(f"qm{'ab'[j]}")
                        dve.tensor_reduce(out=stat[:, 3, 3, 2 * j:2 * j + 2], in_=pairs(f"qm{'ab'[j]}"), axis=AX, op=ALU.max).then_inc(*V.mark(f"mxm{'ab'[j]}"))
                    me("mxmb")
                    dve.tensor_scalar(out=stat[:, 3, 0, :], in0=stat[:, 3, 3, :], scalar1=-SCALE, scalar2=None, op0=ALU.mult).then_inc(*V.mark("nmm"))
                    beside(9)
                    v_tokens(1, 9)
                    softmax_scale(0, "0", 0)
                    lse(0)
                    beside(10)
                    a("sq")
                    dve.scalar_tensor_tensor(out=ht[:, :], in0=job("ho")[:, :], scalar=cols[:, head_col(32)], in1=hg[:, :],
                                             op0=ALU.mult, op1=ALU.mult).then_inc(*V.mark("ho1"))
                    softmax_scale(3, "m", 1)

                    def group_logits(g):
                        dve.wait_ge(edge_in[g], edge_value(g, hf, h))
                        p("p0c" if g == 1 else "pmc")
                        for j in range(2):
                            p(f"qk{g}{'ab'[j]}")
                            logit(f"l{g}{'ab'[j]}", g, slice(2 * j, 2 * j + 2), pairs(f"qk{g}{'ab'[j]}"), bias[:, g + 1:g + 2, :].to_broadcast([P, 2, 2 * P]))
                        maxes(g, g - 1, f"l{g}b")

                    p("p0c")
                    p("pv2", 1)
                    dve.tensor_copy(ptc[1][:, :], job("p0c")[:, :]).then_inc(*V.mark("c0c"))
                    beside(11)
                    p("pmc")
                    p("pv1", 1)
                    dve.tensor_copy(ptc[0][:, :], job("pmc")[:, :]).then_inc(*V.mark("cmc"))
                    group_logits(1)
                    beside(12)
                    v_tokens(2, 12)
                    softmax_scale(1, "1", 0)
                    lse(1)
                    beside(13)
                    a("rs")
                    dve.reciprocal(hrs[:, :], hrs[:, :]).then_inc(*V.mark("rrs"))
                    me("rrs")
                    tt("hout", branch[:, head_col(NH), :].rearrange("p a t -> p (a t)"), ht[:, :], hrs[:, :], ALU.mult)
                    beside(14)
                    group_logits(2)
                    p("p1c")
                    dve.tensor_copy(ptc[0][:, :], job("p1c")[:, :]).then_inc(*V.mark("c1c"))
                    beside(15)
                    softmax_scale(2, "2", 1)
                    lse(2)
                    p("p2c")
                    dve.tensor_copy(ptc[1][:, :], job("p2c")[:, :]).then_inc(*V.mark("c2c"))
                    if hf == 1:
                        topk_gates(0, h)
                    a("lbc2")
                    tt("m1", mmax[:, :], lseb[:, 0, :], lseb[:, 1, :], ALU.max)
                    me("m1")
                    tt("m2", mmax[:, :], mmax[:, :], lseb[:, 2, :], ALU.max)
                    me("m2")
                    tt("md", lseb[:, :, :], lseb[:, :, :], mmax[:, :].unsqueeze(1).to_broadcast([P, G, HALF]), ALU.subtract)
                    a("me")
                    tt("e1", msum[:, :], lseb[:, 0, :], lseb[:, 1, :], ALU.add)
                    me("e1")
                    tt("e2", msum[:, :], msum[:, :], lseb[:, 2, :], ALU.add)
                    me("e2")
                    dve.reciprocal(msum[:, :], msum[:, :]).then_inc(*V.mark("er"))
                    tt("ew", og[:, :, :], og[:, :, :], lseb[:, :, :], ALU.mult)
                    me("ew")
                    tt("ea1", og[:, 0, :], og[:, 0, :], og[:, 1, :], ALU.add)
                    me("ea1")
                    tt("ea2", og[:, 0, :], og[:, 0, :], og[:, 2, :], ALU.add)
                    me("ea2")
                    tt("eo", branch[:, head_col(0), :].rearrange("p a t -> p (a t)"), og[:, 0, :], msum[:, :], ALU.mult)
                cross(dve, boundary(hf, 1))

                for b in range(3):
                    part = slice(NH * b, NH * b + NH)
                    dve.tensor_copy(o_hi[:, part, :], branch[:, part, :]).then_inc(o_split, 1)
                    dve.wait_ge(o_split, 6 * hf + 2 * b + 1)
                    dve.tensor_tensor(out=o_lo[:, part, :], in0=branch[:, part, :], in1=o_hi[:, part, :].bitcast(F32), op=ALU.subtract).then_inc(o_split, 1)
                dve.wait_ge(o_split, 6 * hf + 6)
                apart(dve)
                with dve.Fori(0, KD) as j:
                    it = KD * hf + j

                    def m(name):
                        dve.wait_ge(MV.sem, MV.after(name, it))

                    for b in range(3):
                        if hf == 1:
                            e_rows(2 * b, 2 * b + 2, E_MID // E_ROWS * j, E_MID * j)
                        dve.wait_ge(MA.sem, MA.after(f"s{b}", it))
                        dve.wait_ge(MP.sem, MP.after(f"B{b}", it))
                        if b == 0:
                            dve.wait_ge(MV.sem, MV.after("lo", it - 1))
                        dve.tensor_tensor(out=macc[:, min(b, 1), :], in0=ps[1][:, :], in1=sgate[:, b, :], op=ALU.mult).then_inc(*MV.mark(f"g{b}"))
                        if b:
                            m(f"g{b}")
                            dve.tensor_tensor(out=macc[:, 0, :], in0=macc[:, 0, :], in1=macc[:, 1, :], op=ALU.add).then_inc(*MV.mark(f"a{b}"))
                            m(f"a{b}")
                    if hf == 1:
                        e_rows(6, 8, E_MID // E_ROWS * j, E_MID * j)
                    mh = m_hi[:, bass.ds(j, 1), :].rearrange("p a t -> p (a t)")
                    ml = m_lo[:, bass.ds(j, 1), :].rearrange("p a t -> p (a t)")
                    dve.tensor_copy(mh, macc[:, 0, :]).then_inc(*MV.mark("hi"))
                    m("hi")
                    dve.tensor_tensor(out=ml, in0=macc[:, 0, :], in1=mh.bitcast(F32), op=ALU.subtract).then_inc(*MV.mark("lo"))
                cross(dve, boundary(hf, 2))

                dve.wait_ge(res_in, 48 * (hf + 1))
                with dve.Fori(0, KD // 2) as e:
                    it = KD // 2 * hf + e
                    for t in range(2):
                        if hf == 1:
                            e_rows(4 * t, 4 * t + 4, G_OUT + E_OUT // E_ROWS * e, E_ROWS * G_OUT + E_OUT * e)
                        dve.wait_ge(OP.sem, OP.after(f"T{t}", it))
                        r = res[:, :, bass.ds(2 * P * e + P * t, P)]
                        dve.scalar_tensor_tensor(out=r, in0=r, scalar=ALPHA, in1=ps[2 + t][:, :].rearrange("p (b c) -> p b c", b=NB),
                                                 op0=ALU.mult, op1=ALU.add).then_inc(*OV.mark(f"r{t}"))
                dve.wait_ge(OV.sem, OV.after("r1", KD // 2 * (hf + 1) - 1))
                for tb in range(NB):
                    for c in range(2):
                        last = dve.bn_stats(out=bst[:, tb, c, :], in_=res[:, tb, HALF * c:HALF * c + HALF])
                    last.then_inc(*LV.mark(f"st{tb}"))
                for tb in range(NB):
                    dve.wait_ge(LV.sem, LV.after(f"st{tb}", hf))
                    apart(dve)
                    dve.bn_aggr(out=bmv[:, tb, 0:2], in_=bst[:, tb, :, :]).then_inc(*LV.mark(f"ag{tb}"))
                dve.wait_ge(LV.sem, LV.after(f"ag{NB - 1}", hf))
                dve.tensor_scalar(out=bmv[:, :, 2:3], in0=bmv[:, :, 1:2], scalar1=EPS, scalar2=None, op0=ALU.add).then_inc(*LV.mark("ep"))
                dve.wait_ge(LA.sem, LA.after("sq", hf))
                dve.reciprocal(bmv[:, :, 3:4], bmv[:, :, 3:4]).then_inc(*LV.mark("rc"))
                for tb in range(NB):
                    dve.wait_ge(LV.sem, LV.after("rc", hf))
                    dve.tensor_scalar(out=res[:, tb, :], in0=res[:, tb, :], scalar1=bmv[:, tb, 0:1], scalar2=bmv[:, tb, 3:4],
                                      op0=ALU.subtract, op1=ALU.mult).then_inc(*LV.mark(f"nm{tb}"))
                for tb in range(NB):
                    dve.wait_ge(LV.sem, LV.after(f"nm{tb}", hf))
                    dve.tensor_tensor(out=res[:, tb, :], in0=res[:, tb, :], in1=ln_g[:, :], op=ALU.mult).then_inc(*LV.mark(f"sg{tb}"))
                for tb in range(NB):
                    dve.wait_ge(LV.sem, LV.after(f"sg{tb}", hf))
                    dve.tensor_tensor(out=res[:, tb, :], in0=res[:, tb, :], in1=ln_b[:, :], op=ALU.add).then_inc(*LV.mark(f"sb{tb}"))
                split_lo(2 * hf + 1)
                cross(dve, boundary(hf, 3))
                if hf == 1:
                    with dve.Fori(0, PH // 2) as e:
                        e_rows(0, E_PQ, G_PQ + E_PQ // E_ROWS * e, E_ROWS * G_PQ + E_PQ * e)
                    e_gates()
                cross(dve, boundary(hf, 4))

                if hf == 1:
                    with dve.Fori(0, NB) as tb:
                        for q in range(4):
                            for part in range(4):
                                topk(1, tb, q, part, 2 + q)
                        topk_gates(1, tb)
                    dve.wait_ge(tk_out, 32 * NB * 2 + 32)
                cross(dve, boundary(hf, 5))

            def dot(i, o, q, r):
                tb = 2 * i + o
                dve.wait_ge(p_gelu, NBATCH * (tb - 1) + RING * q + r + 1)
                for s in range(BATCH):
                    dve.wait_ge(u_in[BATCH * r + s], 16 * (NBATCH // RING * (tb - 1) + q) + 16)
                    last = dve.tensor_tensor_reduce(out=u_ring[:, BATCH * r + s, :], in0=u_ring[:, BATCH * r + s, :], in1=h1[o][:, :], scale=1.0,
                                                    scalar=0.0, op0=ALU.mult, op1=ALU.add, accum_out=dots[:, r, s:s + 1])
                last.then_inc(p_dots, 1)

            def coefficient(i, o, q, r):
                dve.wait_ge(p_gelu, RING + NBATCH * (2 * i + o - 1) + RING * q + r + 1)
                dve.tensor_tensor(out=coef[:, r, :], in0=gel[:, r, :], in1=pgate[o][:, bass.ds(BATCH * (RING * q + r), BATCH)],
                                  op=ALU.mult).then_inc(p_coef, 1)

            def finish(i, o):
                tb = 2 * i + o
                dve.wait_ge(FA.sem, FA.after("c1", tb))
                norm(FV.mark, FV, tb, res2[o][:, :], bst2, bmv2, g2[:, :], b2[:, :],
                     lambda: dve.wait_ge(FA.sem, FA.after("sq", tb)))

            def block_dots(i, o):
                dve.wait_ge(blk_in[o], 48 * (i + o))
                apart(dve)
                with dve.Fori(0, NBATCH // RING) as q:
                    dot(i, o, q, 0)
                    for r in range(1, RING):
                        dot(i, o, q, r)
                        coefficient(i, o, q, r - 1)
                    coefficient(i, o, q, RING - 1)
                finish(i, o)

            dve.wait_ge(par_in, 32)
            finish(0, 0)
            block_dots(0, 1)
            with dve.Fori(1, NHALF * NB // 2) as i:
                for o in range(2):
                    block_dots(i, o)


_INS = ["x", "mem", "w_in", "b_gate", "w_mem_kv", "rel_bias", "hgrn_lb", "hgrn_norm_w", "w_branch", "w_out",
        "ln1_g", "ln1_b", "w_peer_q", "peer_sub_keys", "peer_u", "peer_v", "ln2_g", "ln2_b"]


def kernel(**inputs):
    import concourse.bacc as bacc
    from concourse.bass_utils import run_bass_kernel_spmd

    nc = bacc.Bacc("TRN2", target_bir_lowering=False, num_devices=1)
    arrays = {f"in_{n}": np.ascontiguousarray(inputs[n]) for n in _INS}
    arrays |= {f"in_{n}": a for n, a in shape_constants().items()}
    aps = {n[3:]: nc.dram_tensor(n, a.shape, mybir.dt.from_np(a.dtype), kind="ExternalInput").ap() for n, a in arrays.items()}
    aps["out"] = nc.dram_tensor("out_0", (1, S, D), F32, kind="ExternalOutput").ap()
    layer(nc, aps)
    r = run_bass_kernel_spmd(nc, [arrays], core_ids=[0])
    return r.results[0]["out_0"]
```
